# Optimizing a Trainium2 kernel written in Bass

```python
import math
import jax, jax.numpy as jnp
from jax import lax
import numpy as np
import jax
import jax.numpy as jnp

D_MODEL = 1024
BATCH = 1
SEQ = 256
DEPTH = 2

HEAD_DIM = 64
NSA_HEADS = 8
NSA_GROUPS = 2
CMP_BLOCK = 32
CMP_STRIDE = 16
CMP_HIDDEN = 256
SEL_BLOCK = 64
SEL_TOPK = 8
NSA_WINDOW = 512
SWA_HEADS = 8
SWA_GROUPS = 2
SWA_WINDOW = 128
FOX_HEADS = 8
FOX_GATE_BIAS = 3.0
Q_BLOCK = 128
REL_BUCKETS = 32
REL_MAX_DIST = 128
D_FF = 2816
N_BRANCH = 3
LN_EPS = 1e-5
DN_ALPHA = (2 * DEPTH) ** 0.25
DN_BETA = (8 * DEPTH) ** -0.25

W_A = NSA_HEADS * HEAD_DIM
KV_A = NSA_GROUPS * HEAD_DIM
W_B = SWA_HEADS * HEAD_DIM
KV_B = SWA_GROUPS * HEAD_DIM
W_C = FOX_HEADS * HEAD_DIM
D_IN = W_A + 6 * KV_A + 3 * NSA_HEADS + W_B + 2 * KV_B + 3 * W_C + FOX_HEADS


def _layer_norm(x, g, b):
    xf = x.astype(jnp.float32)
    mu = jnp.mean(xf, axis=-1, keepdims=True)
    var = jnp.mean(jnp.square(xf - mu), axis=-1, keepdims=True)
    return ((xf - mu) * lax.rsqrt(var + LN_EPS) * g + b).astype(x.dtype)

def _swiglu(x, w1, w2):
    gt, up = jnp.split(x @ w1, 2, axis=-1)
    return (jax.nn.silu(gt) * up) @ w2

def _t5_bucket(dist):
    n = jnp.maximum(dist, 0)
    exact = REL_BUCKETS // 2
    log_ratio = jnp.log(jnp.maximum(n, 1).astype(jnp.float32) / exact) / math.log(REL_MAX_DIST / exact)
    large = exact + (log_ratio * (REL_BUCKETS - exact)).astype(jnp.int32)
    return jnp.where(n < exact, n, jnp.minimum(large, REL_BUCKETS - 1))

def _masked_softmax(logits, mask):
    logits = jnp.where(mask, logits.astype(jnp.float32), -jnp.inf)
    m = jnp.max(logits, axis=-1, keepdims=True)
    m = jnp.where(jnp.isfinite(m), m, 0.0)
    p = jnp.exp(logits - m)
    return p / jnp.maximum(jnp.sum(p, axis=-1, keepdims=True), 1e-30)

def _split_cols(z):
    sizes = [W_A, 6 * KV_A, 3 * NSA_HEADS, W_B, KV_B, KV_B, W_C, W_C, W_C, FOX_HEADS]
    return jnp.split(z, np.cumsum(sizes)[:-1].tolist(), axis=-1)

def _compress(z, pe, w1, w2):
    B, S, G, dh = z.shape
    r = CMP_BLOCK // CMP_STRIDE
    n_chunk = S // CMP_STRIDE
    nc = n_chunk - r + 1
    zr = z.reshape(B, n_chunk, CMP_STRIDE, G, dh)
    blocks = jnp.concatenate([zr[:, j:j + nc] for j in range(r)], axis=2)
    blocks = blocks + pe[:, None, :]
    flat = blocks.transpose(0, 3, 1, 2, 4).reshape(B, G, nc, CMP_BLOCK * dh)
    return jax.nn.gelu(flat @ w1) @ w2

def _nsa(q_a, kv_a, g_a, pe_k, pe_v, ck_w1, ck_w2, cv_w1, cv_w2, rel_a):
    B, S, _ = q_a.shape
    G, HPG, dh = NSA_GROUPS, NSA_HEADS // NSA_GROUPS, HEAD_DIM
    nb = S // Q_BLOCK
    scale = HEAD_DIM ** -0.5
    q = q_a.reshape(B, S, G, HPG, dh).transpose(0, 2, 3, 1, 4)
    k_cmp, v_cmp, k_slc, v_slc, k_win, v_win = [z.reshape(B, S, G, dh) for z in jnp.split(kv_a, 6, axis=-1)]
    kc = _compress(k_cmp, pe_k, ck_w1, ck_w2)
    vc = _compress(v_cmp, pe_v, cv_w1, cv_w2)
    nc = kc.shape[2]
    ns = S // SEL_BLOCK
    n_sel = min(SEL_TOPK, ns)
    ks = k_slc.reshape(B, ns, SEL_BLOCK, G, dh).transpose(0, 3, 1, 2, 4)
    vs = v_slc.reshape(B, ns, SEL_BLOCK, G, dh).transpose(0, 3, 1, 2, 4)
    pad = ((0, 0), (0, 0), (NSA_WINDOW, 0), (0, 0))
    kw = jnp.pad(k_win.transpose(0, 2, 1, 3), pad)
    vw = jnp.pad(v_win.transpose(0, 2, 1, 3), pad)
    gates = jax.nn.sigmoid(g_a.astype(jnp.float32)).reshape(B, S, G, HPG, 3).transpose(0, 2, 3, 1, 4)
    rel_g = rel_a.reshape(G, HPG, REL_BUCKETS)
    c_start = jnp.arange(nc) * CMP_STRIDE
    c_end = c_start + (CMP_BLOCK - 1)
    s_start = jnp.arange(ns) * SEL_BLOCK
    overlap = ((c_start[:, None] < s_start[None] + SEL_BLOCK) & (c_end[:, None] >= s_start[None])).astype(jnp.float32)
    i_w = jnp.arange(Q_BLOCK)
    j_w = jnp.arange(Q_BLOCK + NSA_WINDOW)
    dist_w = NSA_WINDOW + i_w[:, None] - j_w[None]
    band_w = (dist_w >= 0) & (dist_w < NSA_WINDOW)
    bias_w = rel_g[:, :, _t5_bucket(dist_w)]
    blk = jnp.arange(ns)
    sel_off = jnp.arange(SEL_BLOCK)
    gather = jax.vmap(jax.vmap(lambda kb, ix: kb[ix]))
    lookup = jax.vmap(lambda tab, bk: jnp.moveaxis(tab[:, bk], 0, 1), in_axes=(0, 1), out_axes=1)

    def block(qb):
        q0 = qb * Q_BLOCK
        t = q0 + jnp.arange(Q_BLOCK)
        qq = lax.dynamic_slice_in_dim(q, q0, Q_BLOCK, axis=3)
        gg = lax.dynamic_slice_in_dim(gates, q0, Q_BLOCK, axis=3)
        s_c = jnp.einsum('bghqd,bgkd->bghqk', qq, kc, preferred_element_type=jnp.float32) * scale
        s_c = s_c + rel_g[:, :, _t5_bucket(t[:, None] - c_end[None])]
        p_c = _masked_softmax(s_c, c_end[None] <= t[:, None])
        o_c = jnp.einsum('bghqk,bgkd->bghqd', p_c.astype(vc.dtype), vc)
        imp = jnp.einsum('bghqk,kj->bgqj', p_c, overlap)
        cur = (t // SEL_BLOCK)[:, None]
        forced = (blk[None] == 0) | (blk[None] == cur) | (blk[None] == cur - 1)
        valid = blk[None] * SEL_BLOCK <= t[:, None]
        score = jnp.where(forced, jnp.inf, jnp.where(valid, imp, -jnp.inf))
        _, idx = lax.top_k(score, n_sel)
        k_sel = gather(ks, idx).reshape(B, G, Q_BLOCK, n_sel * SEL_BLOCK, dh)
        v_sel = gather(vs, idx).reshape(B, G, Q_BLOCK, n_sel * SEL_BLOCK, dh)
        pos = (idx[..., None] * SEL_BLOCK + sel_off).reshape(B, G, Q_BLOCK, n_sel * SEL_BLOCK)
        dist = t[:, None] - pos
        s_s = jnp.einsum('bghqd,bgqkd->bghqk', qq, k_sel, preferred_element_type=jnp.float32) * scale
        s_s = s_s + lookup(rel_g, _t5_bucket(dist))
        p_s = _masked_softmax(s_s, (dist >= 0)[:, :, None])
        o_s = jnp.einsum('bghqk,bgqkd->bghqd', p_s.astype(v_sel.dtype), v_sel)
        kwb = lax.dynamic_slice_in_dim(kw, q0, Q_BLOCK + NSA_WINDOW, axis=2)
        vwb = lax.dynamic_slice_in_dim(vw, q0, Q_BLOCK + NSA_WINDOW, axis=2)
        s_w = jnp.einsum('bghqd,bgkd->bghqk', qq, kwb, preferred_element_type=jnp.float32) * scale + bias_w
        mask_w = band_w & ((q0 - NSA_WINDOW + j_w) >= 0)[None]
        p_w = _masked_softmax(s_w, mask_w)
        o_w = jnp.einsum('bghqk,bgkd->bghqd', p_w.astype(vwb.dtype), vwb)
        return gg[..., 0:1] * o_c + gg[..., 1:2] * o_s + gg[..., 2:3] * o_w

    out = lax.map(block, jnp.arange(nb))
    return out.transpose(1, 0, 4, 2, 3, 5).reshape(B, S, W_A).astype(q_a.dtype)

def _swa_sink(q_b, k_b, v_b, sinks, rel_b):
    B, S, _ = q_b.shape
    G, HPG, dh, W = SWA_GROUPS, SWA_HEADS // SWA_GROUPS, HEAD_DIM, SWA_WINDOW
    nb = S // W
    scale = HEAD_DIM ** -0.5
    q = q_b.reshape(B, nb, W, G, HPG, dh)
    k = k_b.reshape(B, nb, W, G, dh)
    v = v_b.reshape(B, nb, W, G, dh)

    def with_prev(z):
        prev = jnp.pad(z[:, :-1], ((0, 0), (1, 0), (0, 0), (0, 0), (0, 0)))
        return jnp.concatenate([prev, z], axis=2)

    kk, vv = with_prev(k), with_prev(v)
    i = jnp.arange(W)
    j = jnp.arange(2 * W)
    dist = W + i[:, None] - j[None]
    band = (dist >= 0) & (dist < W)
    first = (jnp.arange(nb)[:, None] * W - W + j[None]) >= 0
    mask = band[None] & first[:, None, :]
    bias = rel_b.reshape(G, HPG, REL_BUCKETS)[:, :, _t5_bucket(dist)]
    logits = jnp.einsum('bnqghd,bnkgd->bghnqk', q, kk, preferred_element_type=jnp.float32) * scale
    logits = jnp.where(mask, logits + bias[:, :, None], -jnp.inf)
    sink = jnp.broadcast_to(sinks.astype(jnp.float32).reshape(1, G, HPG, 1, 1, 1), logits.shape[:-1] + (1,))
    p = jax.nn.softmax(jnp.concatenate([logits, sink], axis=-1), axis=-1)[..., :-1]
    o = jnp.einsum('bghnqk,bnkgd->bnqghd', p.astype(vv.dtype), vv)
    return o.reshape(B, S, W_B)

def _fox(q_c, k_c, v_c, f_c, b_f):
    B, S, _ = q_c.shape
    H, dh = FOX_HEADS, HEAD_DIM
    nb = S // Q_BLOCK
    scale = HEAD_DIM ** -0.5
    q = q_c.reshape(B, S, H, dh).transpose(0, 2, 1, 3)
    k = k_c.reshape(B, S, H, dh).transpose(0, 2, 1, 3)
    v = v_c.reshape(B, S, H, dh).transpose(0, 2, 1, 3)
    log_f = jax.nn.log_sigmoid((f_c + b_f).astype(jnp.float32))
    c = jnp.cumsum(log_f, axis=1).transpose(0, 2, 1)
    s_idx = jnp.arange(S)

    def block(qb):
        q0 = qb * Q_BLOCK
        t = q0 + jnp.arange(Q_BLOCK)
        qq = lax.dynamic_slice_in_dim(q, q0, Q_BLOCK, axis=2)
        cq = lax.dynamic_slice_in_dim(c, q0, Q_BLOCK, axis=2)
        logits = jnp.einsum('bhqd,bhkd->bhqk', qq, k, preferred_element_type=jnp.float32) * scale
        logits = logits + cq[..., None] - c[:, :, None, :]
        logits = jnp.where(s_idx[None] <= t[:, None], logits, -jnp.inf)
        p = jax.nn.softmax(logits, axis=-1)
        return jnp.einsum('bhqk,bhkd->bhqd', p.astype(v.dtype), v)

    out = lax.map(block, jnp.arange(nb))
    return out.transpose(1, 0, 3, 2, 4).reshape(B, S, W_C)

def _token_mix(h, w_in, pe_k, pe_v, ck_w1, ck_w2, cv_w1, cv_w2, sinks, b_f, rel_bias,
               w_br_a, w_br_b, w_br_c, w_gate, b_gate, w_out):
    B, S, D = h.shape
    q_a, kv_a, g_a, q_b, k_b, v_b, q_c, k_c, v_c, f_c = _split_cols(h @ w_in)
    rel_t = rel_bias.T
    o_a = _nsa(q_a, kv_a, g_a, pe_k, pe_v, ck_w1, ck_w2, cv_w1, cv_w2, rel_t[:NSA_HEADS])
    o_b = _swa_sink(q_b, k_b, v_b, sinks, rel_t[NSA_HEADS:])
    o_c = _fox(q_c, k_c, v_c, f_c, b_f)
    g = jax.nn.sigmoid(h @ w_gate + b_gate).reshape(B, S, N_BRANCH, D)
    merged = g[:, :, 0] * (o_a @ w_br_a) + g[:, :, 1] * (o_b @ w_br_b) + g[:, :, 2] * (o_c @ w_br_c)
    return merged @ w_out

def first_inputs(seed: int = 0) -> dict:
    key = jax.random.key(seed)
    keys = iter(jax.random.split(key, 32))
    L, D, F = DEPTH, D_MODEL, D_FF

    def nrm(shape, scale):
        return jax.random.normal(next(keys), shape, jnp.float32) * scale

    return {
        'x': nrm((BATCH, SEQ, D), 1.0),
        'rel_bias': nrm((REL_BUCKETS, NSA_HEADS + SWA_HEADS), 0.5),
        'ln1_g': 1.0 + nrm((L, D), 0.02),
        'ln1_b': nrm((L, D), 0.02),
        'ffn1_w1': nrm((L, D, 2 * F), D ** -0.5),
        'ffn1_w2': nrm((L, F, D), DN_BETA * F ** -0.5),
        'w_in': nrm((L, D, D_IN), D ** -0.5),
        'cmp_pe_k': nrm((L, CMP_BLOCK, HEAD_DIM), 0.1),
        'cmp_pe_v': nrm((L, CMP_BLOCK, HEAD_DIM), 0.1),
        'cmp_k_w1': nrm((L, CMP_BLOCK * HEAD_DIM, CMP_HIDDEN), (CMP_BLOCK * HEAD_DIM) ** -0.5),
        'cmp_k_w2': nrm((L, CMP_HIDDEN, HEAD_DIM), CMP_HIDDEN ** -0.5),
        'cmp_v_w1': nrm((L, CMP_BLOCK * HEAD_DIM, CMP_HIDDEN), (CMP_BLOCK * HEAD_DIM) ** -0.5),
        'cmp_v_w2': nrm((L, CMP_HIDDEN, HEAD_DIM), CMP_HIDDEN ** -0.5),
        'swa_sinks': nrm((L, SWA_HEADS), 1.0),
        'fox_b_f': FOX_GATE_BIAS + nrm((L, FOX_HEADS), 0.1),
        'w_br_a': nrm((L, W_A, D), W_A ** -0.5),
        'w_br_b': nrm((L, W_B, D), W_B ** -0.5),
        'w_br_c': nrm((L, W_C, D), W_C ** -0.5),
        'w_gate': nrm((L, D, N_BRANCH * D), D ** -0.5),
        'b_gate': nrm((L, N_BRANCH * D), 0.01),
        'w_out': nrm((L, D, D), DN_BETA * D ** -0.5),
        'ln2_g': 1.0 + nrm((L, D), 0.02),
        'ln2_b': nrm((L, D), 0.02),
        'ffn2_w1': nrm((L, D, 2 * F), D ** -0.5),
        'ffn2_w2': nrm((L, F, D), DN_BETA * F ** -0.5),
        'ln3_g': 1.0 + nrm((L, D), 0.02),
        'ln3_b': nrm((L, D), 0.02),
    }

def first_block(x, rel_bias, ln1_g, ln1_b, ffn1_w1, ffn1_w2, w_in, cmp_pe_k, cmp_pe_v,
              cmp_k_w1, cmp_k_w2, cmp_v_w1, cmp_v_w2, swa_sinks, fox_b_f,
              w_br_a, w_br_b, w_br_c, w_gate, b_gate, w_out, ln2_g, ln2_b,
              ffn2_w1, ffn2_w2, ln3_g, ln3_b):
    for l in range(DEPTH):
        x = _layer_norm(DN_ALPHA * x + 0.5 * _swiglu(x, ffn1_w1[l], ffn1_w2[l]), ln1_g[l], ln1_b[l])
        mix = _token_mix(x, w_in[l], cmp_pe_k[l], cmp_pe_v[l], cmp_k_w1[l], cmp_k_w2[l],
                         cmp_v_w1[l], cmp_v_w2[l], swa_sinks[l], fox_b_f[l], rel_bias,
                         w_br_a[l], w_br_b[l], w_br_c[l], w_gate[l], b_gate[l], w_out[l])
        x = _layer_norm(DN_ALPHA * x + mix, ln2_g[l], ln2_b[l])
        x = _layer_norm(DN_ALPHA * x + 0.5 * _swiglu(x, ffn2_w1[l], ffn2_w2[l]), ln3_g[l], ln3_b[l])
    return x


N_MIXERS = 2

SSD_D_INNER = 2 * D_MODEL
SSD_HEAD_DIM = 64
SSD_N_HEADS = SSD_D_INNER // SSD_HEAD_DIM
SSD_N_GROUPS = 4
SSD_HEADS_PER_GROUP = SSD_N_HEADS // SSD_N_GROUPS
SSD_D_STATE = 128
SSD_D_CONV = 4
SSD_CHUNK = 128
SSD_CONV_DIM = SSD_D_INNER + 2 * SSD_N_GROUPS * SSD_D_STATE
SSD_D_IN_PROJ = SSD_D_INNER + SSD_CONV_DIM + SSD_N_HEADS

ATT_HEAD_DIM = 64
ATT_HEADS_PER_GROUP = 8
ATT_PATTERNS = ((128, 1), (512, 4), (2048, 16))
ATT_N_GROUPS = len(ATT_PATTERNS)
ATT_QKV_DIM = ATT_N_GROUPS * 3 * ATT_HEADS_PER_GROUP * ATT_HEAD_DIM
ATT_OUT_DIM = ATT_HEADS_PER_GROUP * ATT_HEAD_DIM
ROPE_THETA = 500000.0
ROPE_DIM = ATT_HEAD_DIM // 4

MOE_N_GROUPS = 4
MOE_EXPERTS_PER_GROUP = 8
MOE_N_EXPERTS = MOE_N_GROUPS * MOE_EXPERTS_PER_GROUP
MOE_TOP_K = 2
MOE_HIDDEN = 512
MOE_BLOCK = 128

DEEPNORM_ALPHA = (2 * DEPTH) ** 0.25
DEEPNORM_BETA = (8 * DEPTH) ** -0.25
RMS_EPS = 1e-5
NEG_INF = -1e30


def _layer_norm_2(x, g, b):
    xf = x.astype(jnp.float32)
    mu = jnp.mean(xf, -1, keepdims=True)
    var = jnp.mean(jnp.square(xf - mu), -1, keepdims=True)
    return ((xf - mu) * lax.rsqrt(var + LN_EPS) * g + b).astype(x.dtype)

def _rope_tables(positions):
    inv_freq = ROPE_THETA ** (-jnp.arange(0, ROPE_DIM, 2, dtype=jnp.float32) / ROPE_DIM)
    ang = positions.astype(jnp.float32)[..., None] * inv_freq
    return jnp.cos(ang)[:, :, None, :], jnp.sin(ang)[:, :, None, :]

def _apply_partial_rope(t, cos, sin):
    half = ROPE_DIM // 2
    t1, t2, rest = t[..., :half], t[..., half:ROPE_DIM], t[..., ROPE_DIM:]
    cos = cos.astype(t.dtype)
    sin = sin.astype(t.dtype)
    return jnp.concatenate([t1 * cos - t2 * sin, t2 * cos + t1 * sin, rest], -1)

def _causal_depthwise_conv(u, w, b):
    c = u.shape[-1]
    y = lax.conv_general_dilated(u, w.reshape(SSD_D_CONV, 1, c), window_strides=(1,),
                                 padding=((SSD_D_CONV - 1, 0),),
                                 dimension_numbers=('NWC', 'WIO', 'NWC'),
                                 feature_group_count=c)
    return y + b

def _ssd_chunked_scan(x, dt, a, b_in, c_in):
    bsz, s = x.shape[:2]
    nc = s // SSD_CHUNK
    Q, G, E, P, N = SSD_CHUNK, SSD_N_GROUPS, SSD_HEADS_PER_GROUP, SSD_HEAD_DIM, SSD_D_STATE
    xr = (x.astype(jnp.float32) * dt[..., None]).reshape(bsz, nc, Q, G, E, P)
    da = (dt * a).reshape(bsz, nc, Q, G, E).transpose(0, 1, 3, 4, 2)
    br = b_in.astype(jnp.float32).reshape(bsz, nc, Q, G, N)
    cr = c_in.astype(jnp.float32).reshape(bsz, nc, Q, G, N)
    da_cs = jnp.cumsum(da, -1)
    causal = jnp.tril(jnp.ones((Q, Q), bool))
    decay_in = jnp.exp(jnp.where(causal, da_cs[..., :, None] - da_cs[..., None, :], -jnp.inf))
    cb = jnp.einsum('bclgn,bcsgn->bcgls', cr, br)
    y_diag = jnp.einsum('bcgls,bcgels,bcsgep->bclgep', cb, decay_in, xr)
    decay_to_end = jnp.exp(da_cs[..., -1:] - da_cs)
    states = jnp.einsum('bclgn,bcgel,bclgep->bcgepn', br, decay_to_end, xr)
    chunk_decay = jnp.exp(da_cs[..., -1])

    def step(h, inp):
        s_c, dec_c = inp
        return h * dec_c[..., None, None] + s_c, h

    h0 = jnp.zeros((bsz, G, E, P, N), jnp.float32)
    _, prev = lax.scan(step, h0, (jnp.moveaxis(states, 1, 0), jnp.moveaxis(chunk_decay, 1, 0)))
    prev = jnp.moveaxis(prev, 0, 1)
    y_off = jnp.einsum('bclgn,bcgepn,bcgel->bclgep', cr, prev, jnp.exp(da_cs))
    return (y_diag + y_off).reshape(bsz, s, G * E, P)

def _ssd_mixer(x, w_in, conv_w, conv_b, dt_bias, a_log, d_skip, norm_w, w_out):
    bsz, s, _ = x.shape
    zxbcdt = x @ w_in
    z = zxbcdt[..., :SSD_D_INNER]
    xbc = zxbcdt[..., SSD_D_INNER:SSD_D_INNER + SSD_CONV_DIM]
    dt_raw = zxbcdt[..., SSD_D_INNER + SSD_CONV_DIM:]
    xbc = jax.nn.silu(_causal_depthwise_conv(xbc, conv_w, conv_b))
    gn = SSD_N_GROUPS * SSD_D_STATE
    xs = xbc[..., :SSD_D_INNER].reshape(bsz, s, SSD_N_HEADS, SSD_HEAD_DIM)
    b_in = xbc[..., SSD_D_INNER:SSD_D_INNER + gn].reshape(bsz, s, SSD_N_GROUPS, SSD_D_STATE)
    c_in = xbc[..., SSD_D_INNER + gn:].reshape(bsz, s, SSD_N_GROUPS, SSD_D_STATE)
    dt = jax.nn.softplus((dt_raw + dt_bias).astype(jnp.float32))
    a = -jnp.exp(a_log.astype(jnp.float32))
    y = _ssd_chunked_scan(xs, dt, a, b_in, c_in) + xs.astype(jnp.float32) * d_skip.astype(jnp.float32)[:, None]
    y = y.reshape(bsz, s, SSD_D_INNER) * jax.nn.silu(z.astype(jnp.float32))
    yg = y.reshape(bsz, s, SSD_N_GROUPS, -1)
    yg = yg * lax.rsqrt(jnp.mean(jnp.square(yg), -1, keepdims=True) + RMS_EPS)
    y = (yg.reshape(bsz, s, SSD_D_INNER) * norm_w).astype(x.dtype)
    return y @ w_out

def _dilated_window_attention(q, k, v, window, dilation):
    bsz, s, h, d = q.shape
    w = window // dilation
    n = s // dilation
    nb = -(-n // w)
    n_pad = nb * w - n

    def to_residues(t):
        return t.reshape(bsz, n, dilation, h, d).transpose(0, 2, 1, 3, 4)

    def key_blocks(t):
        t = jnp.pad(to_residues(t), ((0, 0), (0, 0), (w, n_pad), (0, 0), (0, 0)))
        t = t.reshape(bsz, dilation, nb + 1, w, h, d)
        return jnp.concatenate([t[:, :, :-1], t[:, :, 1:]], axis=3)

    q_r = jnp.pad(to_residues(q), ((0, 0), (0, 0), (0, n_pad), (0, 0), (0, 0)))
    q_r = q_r.reshape(bsz, dilation, nb, w, h, d).astype(jnp.float32)
    k_b = key_blocks(k).astype(jnp.float32)
    v_b = key_blocks(v).astype(jnp.float32)
    scores = jnp.einsum('brnqhd,brnkhd->brnhqk', q_r, k_b) * (ATT_HEAD_DIM ** -0.5)
    qi = jnp.arange(w)[:, None]
    ki = jnp.arange(2 * w)[None, :]
    blk = jnp.arange(nb)[:, None, None]
    valid = (ki >= qi) & (ki <= qi + w) & (blk * w + ki - w >= 0)
    scores = jnp.where(valid[None, None, :, None], scores, NEG_INF)
    m = jnp.max(scores, -1)
    p = jnp.exp(scores - m[..., None])
    l = jnp.sum(p, -1)
    m_t = m.transpose(0, 1, 2, 4, 3)
    l_t = l.transpose(0, 1, 2, 4, 3)
    o = jnp.einsum('brnhqk,brnkhd->brnqhd', p, v_b) / l_t[..., None]

    def from_residues(t):
        t = t.reshape(bsz, dilation, nb * w, *t.shape[4:])[:, :, :n]
        t = jnp.moveaxis(t, 1, 2)
        return t.reshape(bsz, s, *t.shape[3:])

    return from_residues(o), from_residues(m_t), from_residues(l_t)

def _dilated_attention_mixer(x, cos, sin, w_qkv, w_o):
    bsz, s, _ = x.shape
    qkv = (x @ w_qkv).reshape(bsz, s, ATT_N_GROUPS, 3, ATT_HEADS_PER_GROUP, ATT_HEAD_DIM)
    outs, maxes, dens = [], [], []
    for g, (window, dilation) in enumerate(ATT_PATTERNS):
        q = _apply_partial_rope(qkv[:, :, g, 0], cos, sin)
        k = _apply_partial_rope(qkv[:, :, g, 1], cos, sin)
        o, m, l = _dilated_window_attention(q, k, qkv[:, :, g, 2], window, dilation)
        outs.append(o)
        maxes.append(m)
        dens.append(l)
    o = jnp.stack(outs)
    m = jnp.stack(maxes)
    l = jnp.stack(dens)
    wgt = l * jnp.exp(m - jnp.max(m, 0, keepdims=True))
    merged = jnp.sum(wgt[..., None] * o, 0) / jnp.sum(wgt, 0)[..., None]
    return merged.reshape(bsz, s, ATT_OUT_DIM).astype(x.dtype) @ w_o

def _hierarchical_moe(x, w_rg, b_rg, w_re, b_re, w_gate, w_up, w_down):
    bsz, s, d = x.shape
    t = bsz * s
    xf = x.reshape(t, d)
    g_logits = (xf @ w_rg + b_rg).astype(jnp.float32)
    g_w, g_idx = lax.top_k(jax.nn.softmax(g_logits, axis=-1), 1)
    e_logits = (xf @ w_re + b_re).astype(jnp.float32).reshape(t, MOE_N_GROUPS, MOE_EXPERTS_PER_GROUP)
    e_logits = e_logits[jnp.arange(t), g_idx[:, 0]]
    e_w, e_idx = lax.top_k(jax.nn.softmax(e_logits, axis=-1), MOE_TOP_K)
    e_w = e_w / jnp.sum(e_w, -1, keepdims=True)
    gates = (g_w * e_w).reshape(-1)
    expert_id = (g_idx * MOE_EXPERTS_PER_GROUP + e_idx).reshape(-1).astype(jnp.int32)
    token_id = jnp.repeat(jnp.arange(t, dtype=jnp.int32), MOE_TOP_K)
    n_assign = t * MOE_TOP_K
    n_blocks = -(-n_assign // MOE_BLOCK) + MOE_N_EXPERTS
    n_rows = n_blocks * MOE_BLOCK
    order = jnp.argsort(expert_id)
    sorted_e = expert_id[order]
    counts = jnp.bincount(expert_id, length=MOE_N_EXPERTS)
    padded = (counts + MOE_BLOCK - 1) // MOE_BLOCK * MOE_BLOCK
    pad_end = jnp.cumsum(padded)
    pad_start = pad_end - padded
    cnt_start = jnp.cumsum(counts) - counts
    dest = pad_start[sorted_e] + jnp.arange(n_assign, dtype=jnp.int32) - cnt_start[sorted_e]
    row_tok = jnp.full((n_rows,), t, jnp.int32).at[dest].set(token_id[order])
    row_gate = jnp.zeros((n_rows,), x.dtype).at[dest].set(gates[order].astype(x.dtype))
    block_e = jnp.minimum(jnp.searchsorted(pad_end, jnp.arange(n_blocks) * MOE_BLOCK, side='right'),
                          MOE_N_EXPERTS - 1)
    x_rows = jnp.concatenate([xf, jnp.zeros((1, d), x.dtype)], 0)[row_tok]
    x_rows = x_rows.reshape(n_blocks, MOE_BLOCK, d)

    def expert_block(args):
        xb, e = args
        h = jax.nn.silu(xb @ w_gate[e]) * (xb @ w_up[e])
        return h @ w_down[e]

    y_rows = lax.map(expert_block, (x_rows, block_e)).reshape(n_rows, d)
    y = jax.ops.segment_sum(y_rows * row_gate[:, None], row_tok, num_segments=t + 1)[:t]
    return y.reshape(bsz, s, d)

def second_inputs(seed: int = 0) -> dict:
    key = jax.random.key(seed)
    ks = jax.random.split(key, 24)
    f32 = jnp.float32
    n_ssd = len(range(0, DEPTH, N_MIXERS))
    n_att = len(range(1, DEPTH, N_MIXERS))

    def nrm(k, shape, scale):
        return jax.random.normal(k, shape, f32) * scale

    x = jax.random.normal(ks[0], (BATCH, SEQ, D_MODEL), f32)
    positions = jnp.broadcast_to(jnp.arange(SEQ, dtype=jnp.int32), (BATCH, SEQ))
    dt0 = jnp.exp(jax.random.uniform(ks[4], (n_ssd, SSD_N_HEADS), f32) * (np.log(0.1) - np.log(0.001)) + np.log(0.001))
    return {
        'x': x,
        'positions': positions,
        'ssd_w_in': nrm(ks[1], (n_ssd, D_MODEL, SSD_D_IN_PROJ), D_MODEL ** -0.5),
        'ssd_conv_w': nrm(ks[2], (n_ssd, SSD_D_CONV, SSD_CONV_DIM), SSD_D_CONV ** -0.5),
        'ssd_conv_b': nrm(ks[3], (n_ssd, SSD_CONV_DIM), 0.02),
        'ssd_dt_bias': dt0 + jnp.log(-jnp.expm1(-dt0)),
        'ssd_a_log': jnp.log(jax.random.uniform(ks[5], (n_ssd, SSD_N_HEADS), f32, 1.0, 16.0)),
        'ssd_d': 1.0 + nrm(ks[6], (n_ssd, SSD_N_HEADS), 0.01),
        'ssd_norm_w': 1.0 + nrm(ks[7], (n_ssd, SSD_D_INNER), 0.02),
        'ssd_w_out': nrm(ks[8], (n_ssd, SSD_D_INNER, D_MODEL), SSD_D_INNER ** -0.5 * DEEPNORM_BETA),
        'attn_w_qkv': nrm(ks[9], (n_att, D_MODEL, ATT_QKV_DIM), D_MODEL ** -0.5),
        'attn_w_o': nrm(ks[10], (n_att, ATT_OUT_DIM, D_MODEL), ATT_OUT_DIM ** -0.5 * DEEPNORM_BETA),
        'ln_g': 1.0 + nrm(ks[11], (DEPTH, 2, D_MODEL), 0.02),
        'ln_b': nrm(ks[12], (DEPTH, 2, D_MODEL), 0.02),
        'moe_w_router_group': nrm(ks[13], (DEPTH, D_MODEL, MOE_N_GROUPS), D_MODEL ** -0.5),
        'moe_b_router_group': nrm(ks[14], (DEPTH, MOE_N_GROUPS), 0.01),
        'moe_w_router_expert': nrm(ks[15], (DEPTH, D_MODEL, MOE_N_EXPERTS), D_MODEL ** -0.5),
        'moe_b_router_expert': nrm(ks[16], (DEPTH, MOE_N_EXPERTS), 0.01),
        'moe_w_gate': nrm(ks[17], (DEPTH, MOE_N_EXPERTS, D_MODEL, MOE_HIDDEN), D_MODEL ** -0.5),
        'moe_w_up': nrm(ks[18], (DEPTH, MOE_N_EXPERTS, D_MODEL, MOE_HIDDEN), D_MODEL ** -0.5),
        'moe_w_down': nrm(ks[19], (DEPTH, MOE_N_EXPERTS, MOE_HIDDEN, D_MODEL), MOE_HIDDEN ** -0.5 * DEEPNORM_BETA),
    }

def second_block(x, positions, ssd_w_in, ssd_conv_w, ssd_conv_b, ssd_dt_bias, ssd_a_log, ssd_d,
              ssd_norm_w, ssd_w_out, attn_w_qkv, attn_w_o, ln_g, ln_b,
              moe_w_router_group, moe_b_router_group, moe_w_router_expert, moe_b_router_expert,
              moe_w_gate, moe_w_up, moe_w_down):
    cos, sin = _rope_tables(positions)
    for i in range(DEPTH):
        j = i // N_MIXERS
        if i % N_MIXERS == 0:
            mix = _ssd_mixer(x, ssd_w_in[j], ssd_conv_w[j], ssd_conv_b[j], ssd_dt_bias[j],
                             ssd_a_log[j], ssd_d[j], ssd_norm_w[j], ssd_w_out[j])
        else:
            mix = _dilated_attention_mixer(x, cos, sin, attn_w_qkv[j], attn_w_o[j])
        x = _layer_norm_2(DEEPNORM_ALPHA * x + mix, ln_g[i, 0], ln_b[i, 0])
        ffn = _hierarchical_moe(x, moe_w_router_group[i], moe_b_router_group[i],
                                moe_w_router_expert[i], moe_b_router_expert[i],
                                moe_w_gate[i], moe_w_up[i], moe_w_down[i])
        x = _layer_norm_2(DEEPNORM_ALPHA * x + ffn, ln_g[i, 1], ln_b[i, 1])
    return x


def setup_inputs(seed=0):
    out = dict(first_inputs(seed))
    for name, value in second_inputs(seed + 1).items():
        if name != "x":
            out[name + "_2"] = value
    return out


def reference(
    x, rel_bias, ln1_g, ln1_b, ffn1_w1, ffn1_w2, w_in, cmp_pe_k, cmp_pe_v, cmp_k_w1, cmp_k_w2,
    cmp_v_w1, cmp_v_w2, swa_sinks, fox_b_f, w_br_a, w_br_b, w_br_c, w_gate, b_gate, w_out,
    ln2_g, ln2_b, ffn2_w1, ffn2_w2, ln3_g, ln3_b, positions_2, ssd_w_in_2, ssd_conv_w_2,
    ssd_conv_b_2, ssd_dt_bias_2, ssd_a_log_2, ssd_d_2, ssd_norm_w_2, ssd_w_out_2, attn_w_qkv_2,
    attn_w_o_2, ln_g_2, ln_b_2, moe_w_router_group_2, moe_b_router_group_2,
    moe_w_router_expert_2, moe_b_router_expert_2, moe_w_gate_2, moe_w_up_2, moe_w_down_2,
):
    x = first_block(
        x, rel_bias, ln1_g, ln1_b, ffn1_w1, ffn1_w2, w_in, cmp_pe_k, cmp_pe_v, cmp_k_w1,
        cmp_k_w2, cmp_v_w1, cmp_v_w2, swa_sinks, fox_b_f, w_br_a, w_br_b, w_br_c, w_gate,
        b_gate, w_out, ln2_g, ln2_b, ffn2_w1, ffn2_w2, ln3_g, ln3_b,
    )
    return second_block(
        x, positions_2, ssd_w_in_2, ssd_conv_w_2, ssd_conv_b_2, ssd_dt_bias_2, ssd_a_log_2,
        ssd_d_2, ssd_norm_w_2, ssd_w_out_2, attn_w_qkv_2, attn_w_o_2, ln_g_2, ln_b_2,
        moe_w_router_group_2, moe_b_router_group_2, moe_w_router_expert_2,
        moe_b_router_expert_2, moe_w_gate_2, moe_w_up_2, moe_w_down_2,
    )


_drawn_inputs = setup_inputs


def setup_inputs(seed=0):
    import zlib

    import numpy as np

    out = dict(_drawn_inputs(seed))
    spreads = {}
    factors = {'cmp_pe_k': 28.302,
     'cmp_pe_v': 5.167,
     'swa_sinks': 7.675,
     'fox_b_f': 39.64,
     'b_gate': 51.826,
     'ssd_conv_b_2': 3.151,
     'ssd_d_2': 30.103,
     'ssd_norm_w_2': 5.033,
     'moe_b_router_group_2': 18.366,
     'moe_b_router_expert_2': 6.492}
    for name, (base, spread) in spreads.items():
        noise = np.random.default_rng([zlib.crc32(name.encode()), seed]).standard_normal(out[name].shape)
        drawn = base * np.exp(spread * noise) if base else spread * noise
        out[name] = jnp.asarray(drawn.astype(out[name].dtype))
    for name, factor in factors.items():
        out[name] = (out[name] * factor).astype(out[name].dtype)
    return out
```

```python
from contextlib import ExitStack

import numpy as np

import concourse.bass as bass
from concourse import mybir

F32 = mybir.dt.float32
I32 = mybir.dt.int32
ALU = mybir.AluOpType
ACT = mybir.ActivationFunctionType
AX = mybir.AxisListType.X

P = 128
D = 1024
S = 256
KT = D // P
TT = S // P
DEPTH = 2
HD = 64
SCALE = HD ** -0.5
NEG = -1e30
D_FF = 2816
CHUNK = 256
EXPERTS = 32
HIDDEN = 512
ALPHA = (2 * DEPTH) ** 0.25
LN_EPS = 1e-5
NC_CMP = 15
RING = 12
SLOT = 2048
AHEAD = RING - 2
BODY = 4
SSD_T = 16
XBC_T = 24
N_UNITS = 40


class Signal:

    def __init__(self, sem, credit=0):
        self.sem = sem
        self.base = credit
        self.issued = credit

    def one(self):
        self.issued += 1
        return 1

    def at(self, n):
        return self.base + n


class Chain:

    def __init__(self, sem):
        self.sem = sem
        self.n = 0

    def link(self, eng, ins):
        self.n += 1
        ins.then_inc(self.sem, 1)
        eng.wait_ge(self.sem, self.n)


class WeightStream:

    def __init__(self, ring, landed, used):
        self.ring = ring
        self.landed = landed
        self.used = used
        self.loads = [None] * RING
        self.value = [0] * RING
        self.total = [0] * RING
        self.issued = RING

    def slot(self, pos):
        return self.ring[:, pos % RING, :]

    def add(self, *loads):
        pos = len(self.loads)
        self.total[pos % RING] += 16 * len(loads)
        self.loads.append(loads)
        self.value.append(self.total[pos % RING])
        return pos

    def align(self):
        n = -len(self.loads) % RING
        self.loads += [None] * n
        self.value += [0] * n
        return n

    def issue(self, sp, upto):
        for pos in range(self.issued, min(upto, len(self.loads))):
            if self.loads[pos] is None:
                continue
            sp.wait_ge(self.used, pos - RING + 1)
            for into, src in self.loads[pos]:
                sp.dma_start(into(self.slot(pos)), src).then_inc(self.landed[pos % RING], 16)
        self.issued = max(self.issued, upto)

    def ready(self, pe, pos):
        pe.wait_ge(self.landed[pos % RING], self.value[pos])


def cols8(ap):
    return ap.rearrange("p (k n) -> p k n", k=8)


def rows2(ap):
    return ap.rearrange("p (k n) -> p k n", k=2)


def col_piece(w, c0, n=CHUNK):
    return (lambda s: cols8(s)[:, :, 0:n]), w[:, c0:c0 + n].rearrange("(k p) n -> p k n", p=P)


def row_piece(w, r0):
    return rows2, w[r0:r0 + 2 * P, :].rearrange("(k p) n -> p k n", p=P)


class Core:

    def __init__(self, nc, ctx, a, out):
        self.nc = nc
        self.a = a
        self.out = out
        self.counts = []
        self.ctx = ctx

        def sb(name, shape):
            return ctx.enter_context(nc.sbuf_tensor(name, shape, F32))

        self.ring = sb("ring", [P, RING, SLOT])
        self.x = sb("x_rows", [P, TT, D])
        self.xT = sb("xT", [P, KT, S])
        self.norm = sb("norm_params", [P, 2, D])
        self.E = sb("bias_tiles", [P, 17 * 384])
        self.ident = sb("ident", [P, P])
        self.ones = sb("ones", [P, P])
        self.zeros = sb("zeros", [P, 512])
        self.tri = sb("tri", [P, TT, S])
        self.tiny = sb("tiny", [P, 64])
        self.arena = sb("arena", [P, 14600])
        self.taken = 0
        self.etaken = 0
        self.ps = ctx.enter_context(nc.psum_tensor("ps", [P, 8, 512], F32))
        self.scratch = nc.dram_tensor("bias_scratch", [16, 512], F32, kind="Internal").ap()
        self.gates_dram = nc.dram_tensor("gates_scratch", [DEPTH, EXPERTS, S], F32, kind="Internal").ap()

        self.small = self.counted("small_loads_landed")
        self.setup_dve = self.counted("setup_vector_done")
        self.setup_pe = self.counted("setup_tensor_done")
        self.setup_act = self.counted("setup_scalar_done")
        self.norm_loaded = self.counted("norm_params_landed")
        self.hid_full = self.counted("hidden_products_full")
        self.sg_full = self.counted("silu_full")
        self.h_full = self.counted("hidden_full", credit=4)
        self.up_gated = self.counted("up_gated")
        self.stat = self.counted("variance_ready")
        self.std = self.counted("std_ready")
        self.x_new = self.counted("x_rows_ready")
        self.xT_ps = self.counted("xT_in_psum")
        self.xT_done = self.counted("xT_ready")
        self.proj_full = self.counted("projection_full")
        self.by_act = self.counted("evacuated_by_scalar")
        self.by_dve = self.counted("evacuated_by_vector")
        self.sc_full = self.counted("scores_full")
        self.s_ready = self.counted("logits_ready")
        self.nm_ready = self.counted("negative_max_ready")
        self.p_ready = self.counted("probs_ready")
        self.pt_ps = self.counted("probsT_in_psum")
        self.pt_ready = self.counted("probsT_ready")
        self.o_ps = self.counted("head_output_in_psum")
        self.o_raw = self.counted("head_output_kept")
        self.mix = self.counted("mixer_rows_ready")
        self.mixT_ps = self.counted("mixer_transposed_in_psum")
        self.mixT = self.counted("mixerT_ready")
        self.gate_act = self.counted("branch_gate_ready")
        self.merged = self.counted("merged_ready")
        self.aux_pe = self.counted("aux_tensor_steps")
        self.aux_act = self.counted("aux_scalar_steps")
        self.aux_dve = self.counted("aux_vector_steps")
        self.stored = self.counted("stores_landed")
        self.dve_chain = Chain(ctx.enter_context(nc.semaphore("vector_chain")))
        self.act_chain = Chain(ctx.enter_context(nc.semaphore("scalar_chain")))
        landed = [ctx.enter_context(nc.semaphore(f"weights_landed_{n}")) for n in range(RING)]
        used = ctx.enter_context(nc.semaphore("weights_used"))
        self.stream = WeightStream(self.ring, landed, used)

    def counted(self, name, credit=0):
        s = Signal(self.ctx.enter_context(self.nc.semaphore(name)), credit)
        self.counts.append(s)
        return s

    def next_stage(self):
        for s in self.counts:
            s.base = s.issued

    def take(self, n):
        v = self.arena[:, self.taken:self.taken + n]
        self.taken += n
        assert self.taken <= 14600, self.taken
        return v

    def etake(self, n):
        v = self.E[:, self.etaken:self.etaken + n]
        self.etaken += n
        assert self.etaken <= 17 * 384
        return v


def window(view, offset, dims):
    return bass.AP(view.tensor, view.offset + offset, [view.ap[0]] + dims)


def setup_stage(c):
    nc, a, ps = c.nc, c.a, c.ps
    c.taken = 0
    rb = c.take(16)
    onehot = c.take(512)
    bmask = c.take(512)
    brow = c.take(512)
    flip = c.take(P)
    hank = c.take(16 * 384)
    hank_v = hank.rearrange("p (h n) -> p h n", h=16)
    E_v = c.E[:, :].rearrange("p (h n) -> p h n", h=17)
    s = c.stream
    with nc.Block() as block:
        @block.sync
        def _(sp):
            sp.dma_start(c.x[:, :, :], a["x"][0].rearrange("(t p) n -> p t n", p=P)).then_inc(c.small.sem, 16)
            sp.dma_start(c.ident[:, :], a["c_ident"]).then_inc(c.small.sem, 16)
            sp.dma_start(rb[0:32, :], a["rel_bias"]).then_inc(c.small.sem, 16)
            sp.dma_start(onehot[0:32, :], a["c_onehot"]).then_inc(c.small.sem, 16)
            sp.dma_start(bmask[0:16, :], a["c_bmask"]).then_inc(c.small.sem, 16)
            sp.dma_start(flip, a["c_flip"]).then_inc(c.small.sem, 16)
            sp.dma_start(E_v[:, 16, :], a["c_causal"]).then_inc(c.small.sem, 16)
            sp.dma_start(c.tri[:, :, :], a["c_tri"]).then_inc(c.small.sem, 16)
            sp.dma_start(c.tiny[:, 0:2], a["c_cols"]).then_inc(c.small.sem, 16)
            s.issue(sp, RING + AHEAD)

        @block.scalar
        def _(act):
            act.wait_ge(c.setup_dve.sem, 2)
            act.dma_start(c.scratch, brow[0:16, :]).then_inc(c.stored.sem, 16)
            act.wait_ge(c.stored.sem, 16)
            act.dma_start(hank_v, bass.AP(c.scratch.tensor, 0, [[1, P], [512, 16], [1, 384]])).then_inc(c.setup_act.sem, 16)

        @block.tensor
        def _(pe):
            pe.wait_ge(c.small.sem, 16 * 9)
            pe.matmul(ps[0:16, 7, :], rb[0:32, :], onehot[0:32, :], start=True, stop=True).then_inc(c.setup_pe.sem, 1)
            for t in range(TT):
                for k in range(KT):
                    m = pe.transpose(ps[:, 2 * t + k // 4, (k % 4) * P:(k % 4 + 1) * P],
                                     c.x[:, t, k * P:(k + 1) * P], c.ident[:, :])
            m.then_inc(c.setup_pe.sem, 1)
            pe.wait_ge(c.setup_act.sem, 16)
            for h in range(16):
                if h >= 4:
                    pe.wait_ge(c.setup_dve.sem, 3 + h - 4 + 1)
                pe.matmul(ps[:, 4 + h % 4, 0:384], flip, hank_v[:, h, :], start=True, stop=True).then_inc(c.setup_pe.sem, 1)

        @block.vector
        def _(dve):
            dve.memset(c.ones[:, :], 1.0)
            dve.memset(c.zeros[:, :], 0.0)
            dve.memset(c.tiny[:, 2:3], 0.0).then_inc(s.used, RING)
            dve.memset(c.tiny[:, 3:4], 0.0).then_inc(c.h_full.sem, 4)
            dve.memset(c.tiny[:, 4:8], 0.0).then_inc(c.setup_dve.sem, 1)
            dve.wait_ge(c.setup_pe.sem, 1)
            dve.tensor_tensor(brow[0:16, :], ps[0:16, 7, :], bmask[0:16, :], ALU.add).then_inc(c.setup_dve.sem, 1)
            dve.wait_ge(c.setup_pe.sem, 2)
            for t in range(TT):
                m = dve.tensor_copy(c.xT[:, :, t * P:(t + 1) * P],
                                    ps[:, 2 * t:2 * t + 2, :].rearrange("p b (k n) -> p (b k) n", k=4))
            m.then_inc(c.setup_dve.sem, 1)
            for h in range(16):
                dve.wait_ge(c.setup_pe.sem, 2 + h + 1)
                dve.tensor_copy(E_v[:, h, :], ps[:, 4 + h % 4, 0:384]).then_inc(c.setup_dve.sem, 1)

    c.small.issued += 144
    c.stored.issued += 16
    c.next_stage()


class Mlp:

    def __init__(self, c, chunks, source):
        self.chunks = chunks
        self.source = source
        self.loops = chunks // BODY
        self.tail = chunks % BODY
        self.pad = c.stream.align()
        self.pos = len(c.stream.loads)
        for n in range(chunks):
            for piece in source(n):
                c.stream.add(piece)


def mlp_stage(c, mlp, load_norm, gates=None):
    nc, ps, s = c.nc, c.ps, c.stream
    hid = [c.take(2 * S).rearrange("p (k n) -> p k n", k=2) for _ in range(2)]
    sg = [c.take(S) for _ in range(2)]
    upg = [c.take(S) for _ in range(2)]
    p0 = mlp.pos
    end = p0 + 3 * mlp.chunks
    slots0 = [s.value[p0 + q] for q in range(RING)]

    def bodies(eng, emit):
        if mlp.loops:
            with eng.Fori(0, mlp.loops) as i:
                for n in range(BODY):
                    emit(i, n)
        for n in range(mlp.tail):
            emit(mlp.loops, n)

    with nc.Block() as block:
        @block.sync
        def _(sp):
            s.issue(sp, p0 + RING)
            if mlp.loops > 1:
                with sp.Fori(1, mlp.loops) as i:
                    for q in range(RING):
                        sp.wait_ge(s.used, i * RING + (p0 + q - RING + 1))
                        into, src = mlp.source(q // 3, i)[q % 3]
                        sp.dma_start(into(s.slot(q)), src).then_inc(s.landed[q], 16)
            s.issued = max(s.issued, p0 + RING * mlp.loops)
            s.issue(sp, end + AHEAD)

        @block.tensor
        def _(pe):
            for b in range(4):
                z = pe.matmul(ps[:, b, :], c.zeros[0:1, 0:P], c.zeros[0:1, :], start=True, stop=False)
                if b == 0:
                    owed = mlp.pad
                    if owed:
                        z.then_inc(s.used, owed)

            def chunk(i, n):
                for j in range(2):
                    m = 2 * n + j
                    bank = 4 + m % 4
                    pe.wait_ge(c.h_full.sem, i * 2 * BODY + c.h_full.at(m - 3))
                    for q in range(2):
                        slot = 3 * n + q
                        if j == 0:
                            pe.wait_ge(s.landed[slot], i * 16 + slots0[slot])
                        w = cols8(s.slot(slot))
                        for k in range(KT):
                            mm = pe.matmul(ps[:, bank, q * S:(q + 1) * S], w[:, k, j * P:(j + 1) * P],
                                           c.xT[:, k, :], start=(k == 0), stop=(k == KT - 1))
                        if q == 0 and j == 1:
                            mm.then_inc(s.used, 1)
                    mm.then_inc(c.hid_full.sem, 1)
                slot = 3 * n + 2
                pe.wait_ge(s.landed[slot], i * 16 + slots0[slot])
                w = rows2(s.slot(slot))
                for kk in range(2):
                    pe.wait_ge(c.h_full.sem, i * 2 * BODY + c.h_full.at(2 * n + kk + 1))
                    for t in range(TT):
                        for half in range(2):
                            mm = pe.matmul(ps[:, 2 * t + half, :], hid[n % 2][:, kk, t * P:(t + 1) * P],
                                           w[:, kk, half * 512:(half + 1) * 512], start=False, stop=False)
                            if kk == 0 and t == 0 and half == 0:
                                mm.then_inc(s.used, 1)
                mm.then_inc(s.used, 1)

            bodies(pe, chunk)
            for b in range(4):
                pe.matmul(ps[:, b, 0:1], c.zeros[0:1, 0:P], c.zeros[0:1, 0:1], start=False, stop=True)

        @block.scalar
        def _(act):
            load_norm(act)

            def chunk(i, n):
                for j in range(2):
                    m = 2 * n + j
                    act.wait_ge(c.hid_full.sem, i * 2 * BODY + c.hid_full.at(m + 1))
                    act.wait_ge(c.h_full.sem, i * 2 * BODY + c.h_full.at(m - 1))
                    act.activation(sg[m % 2], ps[:, 4 + m % 4, 0:S], ACT.Silu).then_inc(c.sg_full.sem, 1)

            bodies(act, chunk)

        @block.vector
        def _(dve):
            if gates is not None:
                dve.wait_ge(c.small.sem, c.small.at(0))

            def chunk(i, n):
                for j in range(2):
                    m = 2 * n + j
                    up = ps[:, 4 + m % 4, S:2 * S]
                    if j == 0:
                        dve.wait_ge(s.used, i * RING + (p0 + 3 * n - 3))
                    dve.wait_ge(c.sg_full.sem, i * 2 * BODY + c.sg_full.at(m + 1))
                    if gates is not None:
                        e = i * 2 + n // 2
                        dve.tensor_tensor(upg[m % 2], up, gates[:, bass.ds(e * S, S)], ALU.mult).then_inc(c.up_gated.sem, 1)
                        dve.wait_ge(c.up_gated.sem, i * 2 * BODY + c.up_gated.at(m + 1))
                        up = upg[m % 2]
                    dve.tensor_tensor(hid[n % 2][:, j, :], up, sg[m % 2], ALU.mult).then_inc(c.h_full.sem, 1)

            bodies(dve, chunk)

    for sig in [c.hid_full, c.sg_full, c.h_full] + ([c.up_gated] if gates is not None else []):
        sig.issued += 2 * mlp.chunks
    c.next_stage()


def norm_loader(c, gamma, beta):
    def load(act):
        act.dma_start(c.norm[:, 0, :], gamma.partition_broadcast(P)).then_inc(c.norm_loaded.sem, 16)
        act.dma_start(c.norm[:, 1, :], beta.partition_broadcast(P)).then_inc(c.norm_loaded.sem, 16)
        c.norm_loaded.issued += 32
    return load


def norm_stage(c, weight, last=False):
    nc, ps, s = c.nc, c.ps, c.stream
    c.taken = 0
    stats = c.take(2 * 2 * 6).rearrange("p (t h n) -> p t h n", t=2, h=2)
    mv = c.take(4).rearrange("p (t n) -> p t n", t=2)
    rstd = c.take(4).rearrange("p (t n) -> p t n", t=2)
    with nc.Block() as block:
        @block.sync
        def _(sp):
            if last:
                for t in range(TT):
                    sp.wait_ge(c.x_new.sem, c.x_new.at(t + 1))
                    sp.dma_start(c.out[0, t * P:(t + 1) * P, :], c.x[:, t, :]).then_inc(c.stored.sem, 16)
                sp.wait_ge(c.stored.sem, c.stored.at(32))

        @block.vector
        def _(dve):
            ch = c.dve_chain
            for t in range(TT):
                ch.link(dve, dve.scalar_tensor_tensor(c.x[:, t, :], c.x[:, t, :], ALPHA / weight,
                                                      ps[:, 2 * t:2 * t + 2, :].rearrange("p b n -> p (b n)"),
                                                      ALU.mult, ALU.add))
                for half in range(2):
                    ins = dve.bn_stats(stats[:, t, half, :], c.x[:, t, half * 512:(half + 1) * 512])
                ch.link(dve, ins)
                ch.link(dve, dve.bn_aggr(mv[:, t, :], stats[:, t, :, :].rearrange("p h n -> p (h n)")))
                dve.tensor_scalar(rstd[:, t, 0:1], mv[:, t, 1:2], LN_EPS / weight ** 2, None, ALU.add).then_inc(c.stat.sem, c.stat.one())
            for t in range(TT):
                dve.wait_ge(c.std.sem, c.std.at(t + 1))
                ch.link(dve, dve.reciprocal(rstd[:, t, 0:1], rstd[:, t, 1:2]))
                ch.link(dve, dve.tensor_scalar(c.x[:, t, :], c.x[:, t, :], mv[:, t, 0:1], rstd[:, t, 0:1], ALU.subtract, ALU.mult))
                if t == 0:
                    dve.wait_ge(c.norm_loaded.sem, c.norm_loaded.at(0))
                ch.link(dve, dve.tensor_tensor(c.x[:, t, :], c.x[:, t, :], c.norm[:, 0, :], ALU.mult))
                dve.tensor_tensor(c.x[:, t, :], c.x[:, t, :], c.norm[:, 1, :], ALU.add).then_inc(c.x_new.sem, c.x_new.one())

        @block.scalar
        def _(act):
            for t in range(TT):
                act.wait_ge(c.stat.sem, c.stat.at(t + 1))
                act.activation(rstd[:, t, 1:2], rstd[:, t, 0:1], ACT.Sqrt).then_inc(c.std.sem, c.std.one())
            if not last:
                for t in range(TT):
                    act.wait_ge(c.xT_ps.sem, c.xT_ps.at(t + 1))
                    act.activation(c.xT[:, :, t * P:(t + 1) * P],
                                   ps[:, 4 + 2 * t:6 + 2 * t, :].rearrange("p b (k n) -> p (b k) n", k=4), ACT.Copy)

        @block.tensor
        def _(pe):
            if not last:
                for t in range(TT):
                    pe.wait_ge(c.x_new.sem, c.x_new.at(t + 1))
                    for k in range(KT):
                        m = pe.transpose(ps[:, 4 + 2 * t + k // 4, (k % 4) * P:(k % 4 + 1) * P],
                                         c.x[:, t, k * P:(k + 1) * P], c.ident[:, :])
                    m.then_inc(c.xT_ps.sem, c.xT_ps.one())
    if last:
        c.stored.issued += 32
    c.next_stage()


class Group:

    def __init__(self, products, copy, engine, needs=(), frees=0):
        self.products = products
        self.copy = copy
        self.engine = engine
        self.needs = needs
        self.frees = frees


def run_projections(c, groups, pe=None, act=None, dve=None, banks=(4, 5, 6, 7), owed=0):
    s = c.stream
    nb = len(banks)
    done = {"act": 0, "dve": 0}
    sigs = {"act": c.by_act, "dve": c.by_dve}
    freed = []
    for g, grp in enumerate(groups):
        bank = c.ps[:, banks[g % nb], :]
        if pe is not None:
            if g >= nb:
                eng, n = freed[g - nb]
                pe.wait_ge(sigs[eng].sem, sigs[eng].at(n))
            for pos in grp.needs:
                s.ready(pe, pos)
            for acc in grp.products(bank):
                for k, (o, lhsT, rhs) in enumerate(acc):
                    m = pe.matmul(o, lhsT, rhs, start=(k == 0), stop=(k == len(acc) - 1))
                    if owed and k == 0:
                        m.then_inc(s.used, owed)
                        owed = 0
            m.then_inc(c.proj_full.sem, c.proj_full.one())
            owed = grp.frees
        done[grp.engine] += 1
        freed.append((grp.engine, done[grp.engine]))
        if grp.engine == "act" and act is not None:
            act.wait_ge(c.proj_full.sem, c.proj_full.at(g + 1))
            grp.copy(act, bank).then_inc(c.by_act.sem, c.by_act.one())
        if grp.engine == "dve" and dve is not None:
            dve.wait_ge(c.proj_full.sem, c.proj_full.at(g + 1))
            grp.copy(dve, bank).then_inc(c.by_dve.sem, c.by_dve.one())
    return done, owed


def settle(c, pe, owed):
    if owed:
        pe.drain().then_inc(c.stream.used, owed)


def copier(dst, src):
    def copy(eng, bank):
        if eng.engine == mybir.EngineType.Activation:
            return eng.activation(dst, src(bank), ACT.Copy)
        return eng.tensor_copy(dst, src(bank))
    return copy


def feature_tiles(c, pos, cols, dst, engine, frees=0):
    def products(bank):
        return [[(bank[:, j * S:(j + 1) * S], cols(k, j), c.xT[:, k, :]) for k in range(KT)] for j in range(2)]
    return Group(products, copier(dst, lambda b: b.rearrange("p (j n) -> p j n", j=2)), engine, (pos,), frees)


class Unit:

    def __init__(self, q, k, nk, bias, values, extra=None, sink=None):
        self.q = q
        self.k = k
        self.nk = nk
        self.bias = bias
        self.values = values
        self.extra = extra
        self.sink = sink


def attention_stage(c, units, raw, nm, lsum, before=None):
    nc, ps, s = c.nc, c.ps, c.stream
    n = len(units)
    norm = c.norm[:, :, :].rearrange("p k n -> p (k n)")
    sb_s = [norm[:, i * 512:(i + 1) * 512] for i in range(3)]
    sb_pT = [norm[:, 1536:1920], c.take(384)]
    mx = [c.take(2) for _ in range(2)]

    def lay(u, v):
        return v[:, 0:2 * units[u].nk].rearrange("p (s k) -> p s k", s=2)

    def blocks(u):
        if units[u].nk == NC_CMP:
            return [(0, 0, 0), (1, 0, P)]
        return [(0, 0, 0), (0, P, P), (1, 0, 2 * P)]

    with nc.Block() as block:
        @block.tensor
        def _(pe):
            for step in range(n + 3):
                u = step
                if u < n:
                    un = units[u]
                    if u >= 2:
                        pe.wait_ge(c.s_ready.sem, c.s_ready.at(u - 1))
                    for slot in range(2):
                        t = 1 - slot
                        o = ps[:, u % 2, slot * un.nk:(slot + 1) * un.nk]
                        pairs = [(un.q(t), un.k)] + (un.extra(t) if un.extra else [])
                        for i, (lhsT, rhs) in enumerate(pairs):
                            m = pe.matmul(o, lhsT, rhs, start=(i == 0), stop=(i == len(pairs) - 1))
                    m.then_inc(c.sc_full.sem, c.sc_full.one())
                u = step - 2
                if 0 <= u < n:
                    pe.wait_ge(c.p_ready.sem, c.p_ready.at(u + 1))
                    if u >= 2:
                        pe.wait_ge(c.pt_ready.sem, c.pt_ready.at(u - 1))
                    nk = min(units[u].nk, P)
                    p = lay(u, sb_s[u % 3])
                    for slot, k0, col in blocks(u):
                        m = pe.transpose(ps[0:nk, 2 + u % 2, col:col + P], p[:, slot, k0:k0 + nk], c.ident[:, :])
                    m.then_inc(c.pt_ps.sem, c.pt_ps.one())
                u = step - 3
                if 0 <= u < n:
                    pe.wait_ge(c.pt_ready.sem, c.pt_ready.at(u + 1))
                    if u >= 2:
                        pe.wait_ge(c.o_raw.sem, c.o_raw.at(u - 1))
                    nk = min(units[u].nk, P)
                    seen = [0, 0]
                    for slot, k0, col in blocks(u):
                        last = seen[slot] + 1 == sum(1 for b in blocks(u) if b[0] == slot)
                        m = pe.matmul(ps[:, 4 + u % 2, slot * HD:(slot + 1) * HD], sb_pT[u % 2][0:nk, col:col + P],
                                      units[u].values[k0 // P], start=(seen[slot] == 0), stop=last)
                        seen[slot] += 1
                    m.then_inc(c.o_ps.sem, c.o_ps.one())

        @block.vector
        def _(dve):
            ch = c.dve_chain
            for step in range(n + 4):
                u = step
                if u < n:
                    un = units[u]
                    dve.wait_ge(c.sc_full.sem, c.sc_full.at(u + 1))
                    if u >= 3:
                        dve.wait_ge(c.pt_ps.sem, c.pt_ps.at(u - 2))
                    sv = lay(u, sb_s[u % 3])
                    ins = dve.scalar_tensor_tensor(sv, lay(u, ps[:, u % 2, :]), SCALE, un.bias, ALU.mult, ALU.add)
                    ins.then_inc(c.s_ready.sem, c.s_ready.one())
                    dve.wait_ge(c.s_ready.sem, c.s_ready.at(u + 1))
                    ch.link(dve, dve.tensor_reduce(mx[u % 2], sv, AX, ALU.max))
                    if un.sink is not None:
                        ins = dve.tensor_scalar(nm[:, u, :], mx[u % 2], -1.0, un.sink, ALU.mult, ALU.min)
                    else:
                        ins = dve.tensor_scalar(nm[:, u, :], mx[u % 2], -1.0, None, ALU.mult)
                    ins.then_inc(c.nm_ready.sem, c.nm_ready.one())
                u = step - 4
                if 0 <= u < n:
                    dve.wait_ge(c.o_ps.sem, c.o_ps.at(u + 1))
                    dve.tensor_copy(raw[:, u, :, :], ps[:, 4 + u % 2, 0:2 * HD].rearrange("p (s d) -> p s d", s=2)
                                    ).then_inc(c.o_raw.sem, c.o_raw.one())

        @block.scalar
        def _(act):
            for step in range(n + 2):
                u = step
                if u < n:
                    act.wait_ge(c.nm_ready.sem, c.nm_ready.at(u + 1))
                    sv = lay(u, sb_s[u % 3])
                    for slot in range(2):
                        ins = act.activation(sv[:, slot, :], sv[:, slot, :], ACT.Exp, bias=nm[:, u, slot:slot + 1],
                                             accum_out=lsum[:, u, slot:slot + 1])
                    ins.then_inc(c.p_ready.sem, c.p_ready.one())
                u = step - 2
                if 0 <= u < n:
                    act.wait_ge(c.pt_ps.sem, c.pt_ps.at(u + 1))
                    if u >= 2:
                        act.wait_ge(c.o_ps.sem, c.o_ps.at(u - 1))
                    nk = min(units[u].nk, P)
                    w = P * len(blocks(u))
                    act.activation(sb_pT[u % 2][0:nk, 0:w], ps[0:nk, 2 + u % 2, 0:w], ACT.Copy
                                   ).then_inc(c.pt_ready.sem, c.pt_ready.one())
    c.next_stage()


def transpose_mix(c, rows, outT, n):
    def tensor(pe):
        for g in range(n // 2):
            if g >= 4:
                pe.wait_ge(c.mixT.sem, c.mixT.at(g - 3))
            for f in range(2 * g, 2 * g + 2):
                for t in range(TT):
                    m = pe.transpose(c.ps[:, 4 + g % 4, (f % 2) * S + t * P:(f % 2) * S + (t + 1) * P],
                                     rows[:, 1 - t, f * P:(f + 1) * P], c.ident[:, :])
            m.then_inc(c.mixT_ps.sem, c.mixT_ps.one())

    def scalar(act):
        for g in range(n // 2):
            act.wait_ge(c.mixT_ps.sem, c.mixT_ps.at(g + 1))
            act.activation(outT[:, 2 * g:2 * g + 2, :], c.ps[:, 4 + g % 4, :].rearrange("p (f n) -> p f n", f=2),
                           ACT.Copy).then_inc(c.mixT.sem, c.mixT.one())
    return tensor, scalar


class MixPlan:

    def __init__(self, c, l):
        s, a = c.stream, c.a
        w = a["w_in"][l]

        def pair(c0, i):
            def part(g, h):
                lo, src = (2 * h + g) * HD, c0 + 256 * g + (2 * i + h) * HD
                return (lambda v: cols8(v)[:, :, lo:lo + HD]), w[:, src:src + HD].rearrange("(k p) n -> p k n", p=P)
            return s.add(*[part(g, h) for h in range(2) for g in range(2)])

        def straight(c0):
            return s.add(col_piece(w, c0))

        self.qa = [pair(0, i) for i in range(2)]
        self.cmp = straight(512)
        self.slc = straight(768)
        self.win = straight(1024)
        self.qb = [pair(1304, i) for i in range(2)]
        self.kvb = straight(1816)
        self.qc = [straight(2072 + CHUNK * i) for i in range(2)]
        self.kc = [straight(2584 + CHUNK * i) for i in range(2)]
        self.vc = [straight(3096 + CHUNK * i) for i in range(2)]
        self.gf = s.add(((lambda v: cols8(v)[:, :, 0:24]), w[:, 1280:1304].rearrange("(k p) n -> p k n", p=P)),
                        ((lambda v: cols8(v)[:, :, 24:32]), w[:, 3608:3616].rearrange("(k p) n -> p k n", p=P)))
        self.cw1 = [[s.add(col_piece(a[name][l][r * D:(r + 1) * D, :], 0)) for r in range(2)]
                    for name in ("cmp_k_w1", "cmp_v_w1")]
        self.cw2 = s.add(((lambda v: v[:, 0:P].rearrange("p (j n) -> p j n", j=2)), a["cmp_k_w2"][l].rearrange("(j p) n -> p j n", p=P)),
                         ((lambda v: v[:, P:2 * P].rearrange("p (j n) -> p j n", j=2)), a["cmp_v_w2"][l].rearrange("(j p) n -> p j n", p=P)))
        self.proj_end = len(s.loads)
        self.br = []
        self.gate = []
        for b, name in enumerate(("w_br_a", "w_br_b", "w_br_c")):
            self.br.append([s.add(row_piece(a[name][l], r * 2 * P)) for r in range(2)])
            self.gate.append([s.add(col_piece(a["w_gate"][l], b * D + CHUNK * i)) for i in range(4)])
        self.out = [s.add(row_piece(a["w_out"][l], r * 2 * P)) for r in range(4)]
        self.end = len(s.loads)


def mix_buffers(c):
    c.taken = 0
    b = {}
    b["qT"] = c.take(12 * S).rearrange("p (i n) -> p i n", i=12)
    b["kT"] = c.take(7 * S).rearrange("p (i n) -> p i n", i=7)
    b["v"] = c.take(3 * 2 * P).rearrange("p (v t n) -> p v t n", v=3, t=2)
    b["vc"] = c.take(2 * 512).rearrange("p (t n) -> p t n", t=2)
    b["z2"] = c.take(4 * P)
    b["gf"] = c.take(2 * 32).rearrange("p (t n) -> p t n", t=2)
    b["hidT"] = c.take(2 * 2 * 30).rearrange("p (v j n) -> p v j n", v=2, j=2)
    b["hb"] = c.take(4)
    b["kcT"] = c.take(15)
    b["vcmp"] = c.take(2 * HD).rearrange("p (g n) -> p g n", g=2)
    b["pe"] = c.take(32)
    b["bf"] = c.take(8)
    b["sinks"] = c.take(8)
    b["bgate"] = c.take(24)
    b["lf"] = c.take(16).rearrange("p (t n) -> p t n", t=2)
    b["lt"] = c.take(32).rearrange("p (k t n) -> p k t n", k=2, t=2)
    b["cT"] = c.take(2 * S).rearrange("p (k n) -> p k n", k=2)
    b["G"] = c.take(48).rearrange("p (s n) -> p s n", s=2)
    b["nm"] = c.take(2 * N_UNITS).rearrange("p (u s) -> p u s", s=2)
    b["lsum"] = c.take(2 * N_UNITS).rearrange("p (u s) -> p u s", s=2)
    b["es"] = c.take(16).rearrange("p (u s) -> p u s", s=2)
    b["raw"] = c.take(N_UNITS * 2 * HD).rearrange("p (u s d) -> p u s d", u=N_UNITS, s=2)
    return b


def mix_projection_stage(c, plan, b, l):
    nc, s, a = c.nc, c.stream, c.a

    def pair_tiles(pos, i0, last):
        def cols(k, j):
            return cols8(s.slot(pos))[:, k, j * P:(j + 1) * P]
        return feature_tiles(c, pos, cols, b["qT"][:, i0:i0 + 2, :], "act", 1)

    def straight_tiles(pos, dst):
        return feature_tiles(c, pos, lambda k, j: cols8(s.slot(pos))[:, k, j * P:(j + 1) * P], dst, "act", 1)

    def kv_tile(pos, ik, iv):
        w = cols8(s.slot(pos))
        keys = Group(lambda bank: [[(bank[:, 0:S], w[:, k, 0:P], c.xT[:, k, :]) for k in range(KT)]],
                     copier(b["kT"][:, ik, :], lambda bank: bank[:, 0:S]), "dve", (pos,), 0)
        vals = Group(lambda bank: [[(bank[:, t * P:(t + 1) * P], c.xT[:, k, t * P:(t + 1) * P], w[:, k, P:2 * P])
                                    for k in range(KT)] for t in range(TT)],
                     copier(b["v"][:, iv, :, :], lambda bank: bank[:, 0:S].rearrange("p (t n) -> p t n", t=2)), "dve", (), 1)
        return [keys, vals]

    def compress_input():
        w = cols8(s.slot(plan.cmp))
        return Group(lambda bank: [[(bank[64 * par:64 * par + 64, q * P:(q + 1) * P], w[:, k, q * HD:(q + 1) * HD],
                                     c.xT[:, k, par:S:2]) for k in range(KT)] for q in range(4) for par in range(2)],
                     copier(b["z2"], lambda bank: bank), "dve", (plan.cmp,), 1)

    def value_rows(pos, i):
        w = cols8(s.slot(pos))
        return Group(lambda bank: [[(bank[:, t * S:(t + 1) * S], c.xT[:, k, t * P:(t + 1) * P], w[:, k, :])
                                    for k in range(KT)] for t in range(TT)],
                     copier(b["vc"][:, :, i * CHUNK:(i + 1) * CHUNK], lambda bank: bank.rearrange("p (t n) -> p t n", t=2)),
                     "dve", (pos,), 1)

    wgf = cols8(s.slot(plan.gf))
    gf = Group(lambda bank: [[(bank[:, t * 32:(t + 1) * 32], c.xT[:, k, t * P:(t + 1) * P], wgf[:, k, 0:32])
                              for k in range(KT)] for t in range(TT)],
               copier(b["gf"], lambda bank: bank[:, 0:64].rearrange("p (t n) -> p t n", t=2)), "dve", (plan.gf,), 1)
    groups = ([pair_tiles(plan.qa[i], 2 * i, False) for i in range(2)] + [compress_input()]
              + kv_tile(plan.slc, 0, 0) + kv_tile(plan.win, 1, 1)
              + [pair_tiles(plan.qb[i], 4 + 2 * i, False) for i in range(2)] + kv_tile(plan.kvb, 2, 2)
              + [straight_tiles(plan.qc[i], b["qT"][:, 8 + 2 * i:10 + 2 * i, :]) for i in range(2)]
              + [straight_tiles(plan.kc[i], b["kT"][:, 3 + 2 * i:5 + 2 * i, :]) for i in range(2)]
              + [value_rows(plan.vc[i], i) for i in range(2)] + [gf])

    with nc.Block() as block:
        @block.sync
        def _(sp):
            s.issue(sp, plan.cw1[0][0] + AHEAD)

        @block.tensor
        def _(pe):
            _, owed = run_projections(c, groups, pe=pe)
            settle(c, pe, owed)

        @block.scalar
        def _(act):
            for dst, src in ((b["pe"], a["c_pe"][l]), (b["bf"], a["fox_b_f"][l].partition_broadcast(P)),
                             (b["sinks"], a["swa_sinks"][l].partition_broadcast(P)), (b["bgate"], a["c_bgate"][l])):
                act.dma_start(dst, src).then_inc(c.small.sem, 16)
            run_projections(c, groups, act=act)

        @block.vector
        def _(dve):
            run_projections(c, groups, dve=dve)
    c.small.issued += 64
    c.next_stage()


def mix_small_stage(c, plan, b):
    nc, s, ps = c.nc, c.stream, c.ps
    z2, hidT = b["z2"], b["hidT"]
    with nc.Block() as block:
        @block.sync
        def _(sp):
            s.issue(sp, plan.proj_end + AHEAD)

        @block.tensor
        def _(pe):
            pe.wait_ge(c.small.sem, c.small.at(0))
            for v in range(2):
                for r in range(2):
                    s.ready(pe, plan.cw1[v][r])
                for j in range(2):
                    def w1(m):
                        return cols8(s.slot(plan.cw1[v][m // 8]))[:, m % 8, j * P:(j + 1) * P]
                    for m in range(16):
                        pe.matmul(ps[:, 4 + v, j * 32:j * 32 + 30], w1(m), window(z2, v * 2 * P + m, [[P, 2], [8, NC_CMP]]),
                                  start=(m == 0), stop=(m == 15))
                    for m in range(16):
                        mm = pe.matmul(ps[:, 4 + v, j * 32 + 30:j * 32 + 31], w1(m), b["pe"][:, v * 16 + m:v * 16 + m + 1],
                                       start=(m == 0), stop=(m == 15))
                mm.then_inc(c.aux_pe.sem, c.aux_pe.one())
            pe.wait_ge(c.aux_dve.sem, c.aux_dve.at(3))
            for t in range(TT):
                mm = pe.matmul(ps[0:8, 6, 0:S], b["lf"][:, t, :], c.tri[:, t, :], start=(t == 0), stop=(t == 1))
                if t == 0:
                    mm.then_inc(s.used, 4)
            mm.then_inc(c.aux_pe.sem, c.aux_pe.one())
            s.ready(pe, plan.cw2)
            w2 = s.slot(plan.cw2).rearrange("p (v j n) -> p v j n", v=16, j=2)
            pe.wait_ge(c.aux_act.sem, c.aux_act.at(3))
            for g in range(2):
                for j in range(2):
                    pe.matmul(ps[64 * g:64 * g + 64, 7, 0:NC_CMP], w2[:, 0, j, :], hidT[:, 0, j, g * NC_CMP:(g + 1) * NC_CMP],
                              start=(j == 0), stop=(j == 1))
            for g in range(2):
                for j in range(2):
                    pe.matmul(ps[0:NC_CMP, 7, 64 + g * HD:64 + (g + 1) * HD], hidT[:, 1, j, g * NC_CMP:(g + 1) * NC_CMP],
                              w2[:, 1, j, :], start=(j == 0), stop=(j == 1))
            pe.drain().then_inc(c.aux_pe.sem, c.aux_pe.one())
            pe.drain().then_inc(s.used, 1)

        @block.scalar
        def _(act):
            ch = c.act_chain
            act.wait_ge(c.aux_dve.sem, c.aux_dve.at(1))
            ch.link(act, act.activation(b["lt"][:, 1, :, :], b["lt"][:, 1, :, :], ACT.Exp, scale=-1.0))
            act.activation(b["lt"][:, 1, :, :], b["lt"][:, 1, :, :], ACT.Ln, bias=c.ones[:, 0:1]).then_inc(c.aux_act.sem, c.aux_act.one())
            for v in range(2):
                act.wait_ge(c.aux_pe.sem, c.aux_pe.at(v + 1))
                for j in range(2):
                    ins = act.activation(b["hb"][:, 2 * v + j:2 * v + j + 1], ps[:, 4 + v, j * 32 + 30:j * 32 + 31], ACT.Copy)
                ch.link(act, ins)
                for j in range(2):
                    ins = act.activation(hidT[:, v, j, :], ps[:, 4 + v, j * 32:j * 32 + 30], ACT.Gelu_apprx_tanh,
                                         bias=b["hb"][:, 2 * v + j:2 * v + j + 1])
                ins.then_inc(c.aux_act.sem, c.aux_act.one())
            for t in range(TT):
                act.activation(b["G"][:, 1 - t, :], b["gf"][:, t, 0:24], ACT.Sigmoid)

        @block.vector
        def _(dve):
            ch = c.dve_chain
            dve.wait_ge(c.small.sem, c.small.at(0))
            for t in range(TT):
                ins = dve.tensor_tensor(b["lt"][:, 0, t, :], b["gf"][:, t, 24:32], b["bf"], ALU.add)
            ch.link(dve, ins)
            dve.scalar_tensor_tensor(b["lt"][:, 1, :, :], b["lt"][:, 0, :, :], -1.0, b["lt"][:, 0, :, :], ALU.mult, ALU.max).then_inc(c.aux_dve.sem, c.aux_dve.one())
            ch.link(dve, dve.tensor_scalar(b["sinks"], b["sinks"], -1.0, None, ALU.mult))
            dve.memset(c.tiny[:, 8:9], 0.0).then_inc(c.aux_dve.sem, c.aux_dve.one())
            dve.wait_ge(c.aux_act.sem, c.aux_act.at(1))
            dve.scalar_tensor_tensor(b["lf"], b["lt"][:, 0, :, :], 0.0, b["lt"][:, 1, :, :], ALU.min, ALU.subtract
                                     ).then_inc(c.aux_dve.sem, c.aux_dve.one())
            dve.wait_ge(c.aux_pe.sem, c.aux_pe.at(3))
            for k, sign in enumerate((1.0, -1.0)):
                dve.tensor_scalar(b["cT"][0:8, k, :], ps[0:8, 6, 0:S], sign / SCALE, None, ALU.mult)
            dve.wait_ge(c.aux_pe.sem, c.aux_pe.at(4))
            dve.tensor_copy(b["kcT"], ps[:, 7, 0:NC_CMP])
            dve.tensor_copy(b["vcmp"][0:NC_CMP, :, :], ps[0:NC_CMP, 7, 64:64 + 2 * HD].rearrange("p (g n) -> p g n", g=2))
    c.next_stage()


def mix_units(c, b):
    def bias(h):
        return window(c.E[:, :], h * 384, [[P, 2], [1, S]])

    units = []
    for branch in range(3):
        for h in range(8):
            g, i = h // 4, h % 4
            lo = 64 * g
            q = (lambda t, i=i, lo=lo: b["qT"][lo:lo + 64, i, t * P:(t + 1) * P])
            if branch < 2:
                units.append(Unit(q, b["kT"][lo:lo + 64, branch, :], S, bias(h),
                                  [b["v"][:, branch, t, g * HD:(g + 1) * HD] for t in range(TT)]))
            else:
                units.append(Unit(q, b["kcT"][lo:lo + 64, :], NC_CMP, window(c.E[:, :], h * 384 + 31, [[P, 2], [16, NC_CMP]]),
                                  [b["vcmp"][0:NC_CMP, g, :]]))
    for h in range(8):
        g, i = h // 4, h % 4
        lo = 64 * g
        q = (lambda t, i=i, lo=lo: b["qT"][lo:lo + 64, 4 + i, t * P:(t + 1) * P])
        units.append(Unit(q, b["kT"][lo:lo + 64, 2, :], S, bias(8 + h),
                          [b["v"][:, 2, t, g * HD:(g + 1) * HD] for t in range(TT)], sink=b["sinks"][:, h:h + 1]))
    for h in range(8):
        i, lo = h // 2, 64 * (h % 2)
        q = (lambda t, i=i, lo=lo: b["qT"][lo:lo + 64, 8 + i, t * P:(t + 1) * P])
        extra = (lambda t, h=h: [(b["cT"][0:8, 0, t * P:(t + 1) * P], c.ident[0:8, h:h + 1].to_broadcast([8, S])),
                                 (c.ident[0:8, h:h + 1].to_broadcast([8, P]), b["cT"][0:8, 1, :])])
        units.append(Unit(q, b["kT"][lo:lo + 64, 3 + i, :], S, bias(16),
                          [b["vc"][:, t, h * HD:(h + 1) * HD] for t in range(TT)], extra=extra))
    return units


def spread(v, n):
    return bass.AP(v.tensor, v.offset, list(v.ap) + [[0, n]])


def mix_combine_stage(c, b):
    nc = c.nc
    raw, nm, lsum, es, G = b["raw"], b["nm"], b["lsum"], b["es"], b["G"]
    rows = c.arena[:, 0:2 * 1536].rearrange("p (s n) -> p s n", s=2)
    outT_v = raw[:, 0:24, :, :].rearrange("p u s d -> p (u s d)").rearrange("p (f n) -> p f n", f=12)
    tensor, scalar = transpose_mix(c, rows, outT_v, 12)
    with nc.Block() as block:
        @block.vector
        def _(dve):
            ch = c.dve_chain
            dve.tensor_tensor(es, nm[:, 24:32, :], spread(b["sinks"], 2), ALU.subtract).then_inc(c.aux_dve.sem, c.aux_dve.one())
            dve.wait_ge(c.aux_act.sem, c.aux_act.at(1))
            ch.link(dve, dve.tensor_tensor(lsum[:, 24:32, :], lsum[:, 24:32, :], es, ALU.add))
            ch.link(dve, dve.tensor_scalar(lsum, lsum, 1e-30, None, ALU.max))
            ch.link(dve, dve.reciprocal(lsum, lsum))
            ch.link(dve, dve.tensor_scalar(lsum[:, 16:24, 1], lsum[:, 16:24, 1], c.tiny[:, 0:1], None, ALU.mult))
            for br, col in ((0, 1), (1, 2), (2, 0)):
                gv = bass.AP(G.tensor, G.offset + col, [G.ap[0], [3, 8], [24, 2]])
                ins = dve.tensor_tensor(lsum[:, 8 * br:8 * br + 8, :], lsum[:, 8 * br:8 * br + 8, :], gv, ALU.mult)
            ch.link(dve, ins)

            def head_rows(m):
                return rows[:, :, m * 512:(m + 1) * 512].rearrange("p s (h d) -> p h s d", h=8)

            def scaled(dst, u0):
                return dve.tensor_tensor(dst, raw[:, u0:u0 + 8, :, :], spread(lsum[:, u0:u0 + 8, :], HD), ALU.mult)
            scaled(head_rows(1), 24)
            scaled(head_rows(2), 32)
            scaled(head_rows(0), 0)
            scaled(raw[:, 8:16, :, :], 8)
            ch.link(dve, scaled(raw[:, 16:24, :, :], 16))
            ch.link(dve, dve.tensor_tensor(raw[:, 8:16, :, :], raw[:, 8:16, :, :], raw[:, 16:24, :, :], ALU.add))
            dve.tensor_tensor(head_rows(0), head_rows(0), raw[:, 8:16, :, :], ALU.add).then_inc(c.mix.sem, c.mix.one())

        @block.scalar
        def _(act):
            act.wait_ge(c.aux_dve.sem, c.aux_dve.at(1))
            act.activation(es, es, ACT.Exp).then_inc(c.aux_act.sem, c.aux_act.one())
            scalar(act)

        @block.tensor
        def _(pe):
            pe.wait_ge(c.mix.sem, c.mix.at(1))
            tensor(pe)
    c.next_stage()
    return outT_v


def mix_merge_stage(c, plan, b, outT, load_norm):
    nc, s, ps = c.nc, c.stream, c.ps
    mT = c.arena[:, 0:8 * S].rearrange("p (f n) -> p f n", f=8)
    sgm = [c.arena[:, (8 + i) * S:(9 + i) * S] for i in range(2)]
    tmps = [c.arena[:, (10 + i) * S:(11 + i) * S] for i in range(2)]
    with nc.Block() as block:
        @block.sync
        def _(sp):
            s.issue(sp, plan.end + AHEAD)

        @block.tensor
        def _(pe):
            for g in range(24):
                br, f = g // 8, g % 8
                bank = 4 + g % 4
                if g >= 4:
                    pe.wait_ge(c.merged.sem, c.merged.at(g - 3))
                if f == 0:
                    for pos in plan.br[br]:
                        s.ready(pe, pos)
                if f % 2 == 0:
                    s.ready(pe, plan.gate[br][f // 2])
                w = cols8(s.slot(plan.gate[br][f // 2]))
                for k in range(KT):
                    m = pe.matmul(ps[:, bank, 0:S], w[:, k, (f % 2) * P:(f % 2 + 1) * P], c.xT[:, k, :],
                                  start=(k == 0), stop=(k == KT - 1))
                    if k == 0 and f == 0 and br > 0:
                        m.then_inc(s.used, 6)
                for k in range(4):
                    w = rows2(s.slot(plan.br[br][k // 2]))
                    m = pe.matmul(ps[:, bank, S:2 * S], w[:, k % 2, f * P:(f + 1) * P], outT[:, 4 * br + k, :],
                                  start=(k == 0), stop=(k == 3))
                m.then_inc(c.proj_full.sem, c.proj_full.one())
            pe.wait_ge(c.merged.sem, c.merged.at(24))
            for r in range(4):
                s.ready(pe, plan.out[r])
                w = rows2(s.slot(plan.out[r]))
                for kk in range(2):
                    for t in range(TT):
                        for half in range(2):
                            k = 2 * r + kk
                            m = pe.matmul(ps[:, 2 * t + half, :], mT[:, k, t * P:(t + 1) * P],
                                          w[:, kk, half * 512:(half + 1) * 512], start=(k == 0), stop=(k == 7))
                            if k == 0 and t == 0 and half == 0:
                                m.then_inc(s.used, 6)
                m.then_inc(s.used, 1)

        @block.scalar
        def _(act):
            load_norm(act)
            for g in range(24):
                act.wait_ge(c.proj_full.sem, c.proj_full.at(g + 1))
                if g >= 2:
                    act.wait_ge(c.merged.sem, c.merged.at(g - 1))
                act.activation(sgm[g % 2], ps[:, 4 + g % 4, 0:S], ACT.Sigmoid, bias=b["bgate"][:, g:g + 1]
                               ).then_inc(c.gate_act.sem, c.gate_act.one())

        @block.vector
        def _(dve):
            ch = c.dve_chain
            for g in range(24):
                br, f = g // 8, g % 8
                dve.wait_ge(c.gate_act.sem, c.gate_act.at(g + 1))
                out = ps[:, 4 + g % 4, S:2 * S]
                if br == 0:
                    dve.tensor_tensor(mT[:, f, :], out, sgm[g % 2], ALU.mult).then_inc(c.merged.sem, c.merged.one())
                else:
                    tmp = tmps[g % 2]
                    dve.wait_ge(c.merged.sem, c.merged.at(g - 1))
                    ch.link(dve, dve.tensor_tensor(tmp, out, sgm[g % 2], ALU.mult))
                    dve.tensor_tensor(mT[:, f, :], mT[:, f, :], tmp, ALU.add).then_inc(c.merged.sem, c.merged.one())
    c.next_stage()


def token_mix(c, plan, l, load_norm):
    b = mix_buffers(c)
    mix_projection_stage(c, plan, b, l)
    mix_small_stage(c, plan, b)
    attention_stage(c, mix_units(c, b), b["raw"], b["nm"], b["lsum"])
    outT = mix_combine_stage(c, b)
    mix_merge_stage(c, plan, b, outT, load_norm)


class SsdPlan:
    def __init__(self, c):
        s, a = c.stream, c.a
        w = a["ssd_w_in_2"][0]
        self.z = [s.add(col_piece(w, CHUNK * i)) for i in range(8)]
        self.xbc = [s.add(col_piece(w, 2048 + CHUNK * i)) for i in range(12)]
        self.dt = s.add(col_piece(w, 5120, 32))
        self.proj_end = len(s.loads)
        self.out = [s.add(row_piece(a["ssd_w_out_2"][0], r * 2 * P)) for r in range(8)]
        self.end = len(s.loads)


def ssd_mixer(c, plan, load_norm):
    nc, s, ps, a = c.nc, c.stream, c.ps, c.a
    c.taken = 0
    c.etaken = 0
    NH, PG = 32, 4
    zT = c.take(16 * S).rearrange("p (i n) -> p i n", i=16)
    xbc = c.take(24 * S).rearrange("p (i n) -> p i n", i=24)
    conv = [c.take(S) for _ in range(2)]
    dt = c.take(64).rearrange("p (t n) -> p t n", t=2)
    da = c.take(64).rearrange("p (t n) -> p t n", t=2)
    dt1 = c.take(64).rearrange("p (t n) -> p t n", t=2)
    ncs = c.take(64).rearrange("p (t n) -> p t n", t=2)
    csT = c.take(S)
    dtb = c.take(32)
    alog = c.take(32)
    cols = c.take(6 * 24 + 32)
    diff = [c.take(384) for _ in range(2)]
    dec = [c.take(384) for _ in range(2)]
    rstd = c.take(S)
    xr = c.etake(2 * 2048).rearrange("p (t n) -> p t n", t=2)
    cb = c.etake(4 * 384).rearrange("p (g n) -> p g n", g=4)
    conv_w = cols[:, 0:96].rearrange("p (i k) -> p i k", i=24)
    conv_b = cols[:, 96:120]
    norm_w = cols[:, 120:136]
    dskip = cols[:, 136:152]

    def z_group(i):
        w = cols8(s.slot(plan.z[i]))

        def copy(eng, bank):
            return eng.activation(zT[:, 2 * i:2 * i + 2, :], bank.rearrange("p (j n) -> p j n", j=2), ACT.Silu)
        return Group(lambda bank: [[(bank[:, j * S:(j + 1) * S], w[:, k, j * P:(j + 1) * P], c.xT[:, k, :])
                                    for k in range(KT)] for j in range(2)], copy, "act", (plan.z[i],), 1)

    with nc.Block() as block:
        @block.sync
        def _(sp):
            for dst, src in ((cols[:, 0:152], a["c_ssd"]), (dtb, a["ssd_dt_bias_2"][0].partition_broadcast(P)),
                             (alog, a["ssd_a_log_2"][0].partition_broadcast(P))):
                sp.dma_start(dst, src).then_inc(c.small.sem, 16)
            s.issue(sp, plan.proj_end + AHEAD)

        @block.tensor
        def _(pe):
            owed = 0
            for g in range(8 + 24):
                is_z = g < 8
                bank = 4 + g % 4
                if g >= 4:
                    if g - 4 < 8:
                        pe.wait_ge(c.by_act.sem, c.by_act.at(g - 3))
                    else:
                        pe.wait_ge(c.by_dve.sem, c.by_dve.at(g - 4 - 8 + 1))
                if is_z:
                    s.ready(pe, plan.z[g])
                    w = cols8(s.slot(plan.z[g]))
                    tiles = [(ps[:, bank, j * S:(j + 1) * S], j) for j in range(2)]
                    free = 1
                else:
                    i = g - 8
                    if i % 2 == 0:
                        s.ready(pe, plan.xbc[i // 2])
                    w = cols8(s.slot(plan.xbc[i // 2]))
                    tiles = [(ps[:, bank, 0:S], i % 2)]
                    free = i % 2
                for o, j in tiles:
                    for k in range(KT):
                        m = pe.matmul(o, w[:, k, j * P:(j + 1) * P], c.xT[:, k, :], start=(k == 0), stop=(k == KT - 1))
                        if owed and k == 0:
                            m.then_inc(s.used, owed)
                            owed = 0
                m.then_inc(c.proj_full.sem, c.proj_full.one())
                owed = free
            pe.wait_ge(c.by_dve.sem, c.by_dve.at(21))
            s.ready(pe, plan.dt)
            w = cols8(s.slot(plan.dt))
            for t in range(TT):
                for k in range(KT):
                    m = pe.matmul(ps[:, 4, t * 32:(t + 1) * 32], c.xT[:, k, t * P:(t + 1) * P], w[:, k, 0:32],
                                  start=(k == 0), stop=(k == KT - 1))
                    if owed and k == 0:
                        m.then_inc(s.used, owed)
                        owed = 0
            m.then_inc(c.proj_full.sem, c.proj_full.one())
            settle(c, pe, 1)

        @block.scalar
        def _(act):
            for g in range(8):
                act.wait_ge(c.proj_full.sem, c.proj_full.at(g + 1))
                act.activation(zT[:, 2 * g:2 * g + 2, :], ps[:, 4 + g % 4, :].rearrange("p (j n) -> p j n", j=2),
                               ACT.Silu).then_inc(c.by_act.sem, c.by_act.one())
            for i in range(24):
                act.wait_ge(c.by_dve.sem, c.by_dve.at(i + 1))
                act.activation(xbc[:, i, :], conv[i % 2], ACT.Silu).then_inc(c.aux_act.sem, c.aux_act.one())

        @block.vector
        def _(dve):
            ch = c.dve_chain
            dve.wait_ge(c.small.sem, c.small.at(48))
            for i in range(24):
                dve.wait_ge(c.proj_full.sem, c.proj_full.at(8 + i + 1))
                if i >= 2:
                    dve.wait_ge(c.aux_act.sem, c.aux_act.at(i - 1))
                u, y = ps[:, 4 + i % 4, 0:S], conv[i % 2]
                ch.link(dve, dve.tensor_scalar(y, u, conv_w[:, i, 3:4], conv_b[:, i:i + 1], ALU.mult, ALU.add))
                for k in (2, 1, 0):
                    d = 3 - k
                    ins = dve.scalar_tensor_tensor(y[:, d:S], u[:, 0:S - d], conv_w[:, i, k:k + 1], y[:, d:S], ALU.mult, ALU.add)
                    if k:
                        ch.link(dve, ins)
                ins.then_inc(c.by_dve.sem, c.by_dve.one())
            dve.wait_ge(c.proj_full.sem, c.proj_full.at(33))
            v = ps[:, 4, 0:64].rearrange("p (t n) -> p t n", t=2)
            dve.tensor_tensor(dt, v, bass.AP(dtb.tensor, dtb.offset, [dtb.ap[0], [0, 2], [1, 32]]), ALU.add)
    c.small.issued += 48
    c.next_stage()

    with nc.Block() as block:
        @block.scalar
        def _(act):
            ch = c.act_chain
            act.wait_ge(c.aux_dve.sem, c.aux_dve.at(1))
            ch.link(act, act.activation(dt1, dt1, ACT.Exp, scale=-1.0))
            act.activation(alog, alog, ACT.Exp).then_inc(c.aux_act.sem, c.aux_act.one())
            act.activation(dt1, dt1, ACT.Ln, bias=c.ones[:, 0:1]).then_inc(c.aux_act.sem, c.aux_act.one())

        @block.vector
        def _(dve):
            ch = c.dve_chain
            dve.scalar_tensor_tensor(dt1, dt, -1.0, dt, ALU.mult, ALU.max).then_inc(c.aux_dve.sem, c.aux_dve.one())
            dve.wait_ge(c.aux_act.sem, c.aux_act.at(2))
            ch.link(dve, dve.scalar_tensor_tensor(dt, dt, 0.0, dt1, ALU.max, ALU.add))
            dve.scalar_tensor_tensor(da, dt, -1.0, bass.AP(alog.tensor, alog.offset, [alog.ap[0], [0, 2], [1, 32]]),
                                     ALU.mult, ALU.mult).then_inc(c.aux_dve.sem, c.aux_dve.one())
            for q in range(8):
                t, f = q % 2, q // 2
                dve.wait_ge(c.mixT_ps.sem, c.mixT_ps.at(q + 1))
                dve.tensor_tensor(xr[:, t, f * 512:(f + 1) * 512].rearrange("p (h d) -> p h d", h=8),
                                  ps[:, q % 4, :].rearrange("p (h d) -> p h d", h=8),
                                  spread(dt[:, t, 8 * f:8 * f + 8], HD), ALU.mult).then_inc(c.mixT.sem, c.mixT.one())
            for g in range(PG):
                dve.wait_ge(c.aux_pe.sem, c.aux_pe.at(g + 1))
                dve.tensor_tensor(cb[:, g, 0:S], ps[:, 4 + g % 4, 0:S], c.tri[:, 0, :], ALU.mult)
                dve.tensor_tensor(cb[:, g, S:384], ps[:, 4 + g % 4, S:384], c.tri[:, 1, P:S], ALU.mult).then_inc(c.by_dve.sem, c.by_dve.one())
            dve.wait_ge(c.aux_pe.sem, c.aux_pe.at(5))
            for t in range(TT):
                dve.tensor_scalar(ncs[:, t, :], ps[:, 4, 64 * t:64 * t + 32], -1.0, None, ALU.mult)
            dve.tensor_copy(csT[0:32, :], ps[0:32, 5, 0:S])

        @block.tensor
        def _(pe):
            for q in range(8):
                t, f = q % 2, q // 2
                if q >= 4:
                    pe.wait_ge(c.mixT.sem, c.mixT.at(q - 3))
                for i in range(4):
                    m = pe.transpose(ps[:, q % 4, i * P:(i + 1) * P], xbc[:, 4 * f + i, t * P:(t + 1) * P], c.ident[:, :])
                m.then_inc(c.mixT_ps.sem, c.mixT_ps.one())
            for g in range(PG):
                pe.matmul(ps[:, 4 + g, 0:S], xbc[:, 16 + g, 0:P], xbc[:, 20 + g, :], start=True, stop=True)
                pe.matmul(ps[:, 4 + g, S:384], xbc[:, 16 + g, P:S], xbc[:, 20 + g, P:S], start=True, stop=True
                          ).then_inc(c.aux_pe.sem, c.aux_pe.one())
            pe.wait_ge(c.aux_dve.sem, c.aux_dve.at(2))
            pe.wait_ge(c.by_dve.sem, c.by_dve.at(2))
            for t in range(TT):
                for u in range(TT):
                    pe.matmul(ps[:, 4, 64 * t:64 * t + 32], c.tri[:, u, t * P:(t + 1) * P], da[:, u, :], start=(u == 0), stop=(u == 1))
            for u in range(TT):
                m = pe.matmul(ps[0:32, 5, 0:S], da[:, u, :], c.tri[:, u, :], start=(u == 0), stop=(u == 1))
            m.then_inc(c.aux_pe.sem, c.aux_pe.one())
    c.next_stage()

    with nc.Block() as block:
        @block.tensor
        def _(pe):
            for step in range(NH + 2):
                h = step
                if h < NH:
                    if h >= 2:
                        pe.wait_ge(c.s_ready.sem, c.s_ready.at(h - 1))
                    pe.matmul(ps[:, h % 2, 0:S], c.ident[0:32, h:h + 1].to_broadcast([32, P]), csT[0:32, :],
                              start=True, stop=True).then_inc(c.sc_full.sem, c.sc_full.one())
                h = step - 2
                if h >= 0:
                    i, lo = h // 2, 64 * (h % 2)
                    if h % 2 == 0 and i >= 2:
                        pe.wait_ge(c.o_raw.sem, c.o_raw.at(i - 1))
                    pe.wait_ge(c.p_ready.sem, c.p_ready.at(h + 1))
                    pe.matmul(ps[lo:lo + 64, 2 + i % 2, 0:S], xr[:, 0, h * HD:(h + 1) * HD], diff[h % 2][:, 0:S], start=True, stop=False)
                    pe.matmul(ps[lo:lo + 64, 2 + i % 2, P:S], xr[:, 1, h * HD:(h + 1) * HD], diff[h % 2][:, S:384],
                              start=False, stop=True).then_inc(c.o_ps.sem, c.o_ps.one())

        @block.vector
        def _(dve):
            ch = c.dve_chain
            for step in range(NH + 3):
                h = step
                if h < NH:
                    dve.wait_ge(c.sc_full.sem, c.sc_full.at(h + 1))
                    if h >= 2:
                        dve.wait_ge(c.o_ps.sem, c.o_ps.at(h - 1))
                    dve.tensor_scalar(diff[h % 2][:, 0:S], ps[:, h % 2, 0:S], ncs[:, 0, h:h + 1], 0.0, ALU.add, ALU.min)
                    dve.tensor_scalar(diff[h % 2][:, S:384], ps[:, h % 2, P:S], ncs[:, 1, h:h + 1], 0.0, ALU.add, ALU.min
                                      ).then_inc(c.s_ready.sem, c.s_ready.one())
                h = step - 1
                if 0 <= h < NH:
                    dve.wait_ge(c.pt_ready.sem, c.pt_ready.at(h + 1))
                    dve.tensor_tensor(diff[h % 2], dec[h % 2], cb[:, h // 8, :], ALU.mult).then_inc(c.p_ready.sem, c.p_ready.one())
                h = step - 3
                if h >= 0 and h % 2 == 1:
                    i = h // 2
                    dve.wait_ge(c.o_ps.sem, c.o_ps.at(h + 1))
                    ins = dve.scalar_tensor_tensor(xbc[:, i, :], xbc[:, i, :], dskip[:, i:i + 1], ps[:, 2 + i % 2, 0:S], ALU.mult, ALU.add)
                    ins.then_inc(c.o_raw.sem, c.o_raw.one())
                    dve.wait_ge(c.o_raw.sem, c.o_raw.at(i + 1))
                    dve.tensor_tensor(zT[:, i, :], zT[:, i, :], xbc[:, i, :], ALU.mult)

        @block.scalar
        def _(act):
            for h in range(NH):
                act.wait_ge(c.s_ready.sem, c.s_ready.at(h + 1))
                if h >= 2:
                    act.wait_ge(c.p_ready.sem, c.p_ready.at(h - 1))
                act.activation(dec[h % 2], diff[h % 2], ACT.Exp).then_inc(c.pt_ready.sem, c.pt_ready.one())
    c.next_stage()

    with nc.Block() as block:
        @block.sync
        def _(sp):
            s.issue(sp, plan.end + AHEAD)

        @block.scalar
        def _(act):
            load_norm(act)
            for i in range(16):
                act.activation(xbc[:, i, :], zT[:, i, :], ACT.Square).then_inc(c.aux_act.sem, c.aux_act.one())
            for g in range(PG):
                act.wait_ge(c.stat.sem, c.stat.at(g + 1))
                act.activation(diff[0][:, 0:S], diff[1][:, 0:S], ACT.Sqrt).then_inc(c.std.sem, c.std.one())

        @block.tensor
        def _(pe):
            for g in range(PG):
                for i in range(4):
                    pe.wait_ge(c.aux_act.sem, c.aux_act.at(4 * g + i + 1))
                    m = pe.matmul(ps[:, 4 + g, 0:S], c.ones[:, :], xbc[:, 4 * g + i, :], start=(i == 0), stop=(i == 3))
                m.then_inc(c.aux_pe.sem, c.aux_pe.one())
            for r in range(8):
                pe.wait_ge(c.mix.sem, c.mix.at(r // 2 + 1))
                s.ready(pe, plan.out[r])
                w = rows2(s.slot(plan.out[r]))
                for kk in range(2):
                    k = 2 * r + kk
                    for t in range(TT):
                        for half in range(2):
                            m = pe.matmul(ps[:, 2 * t + half, :], zT[:, k, t * P:(t + 1) * P],
                                          w[:, kk, half * 512:(half + 1) * 512], start=(k == 0), stop=(k == 15))
                m.then_inc(s.used, 1)

        @block.vector
        def _(dve):
            ch = c.dve_chain
            for g in range(PG):
                dve.wait_ge(c.aux_pe.sem, c.aux_pe.at(g + 1))
                if g:
                    dve.wait_ge(c.std.sem, c.std.at(g))
                dve.tensor_scalar(diff[1][:, 0:S], ps[:, 4 + g, 0:S], 1.0 / 512, 1e-5, ALU.mult, ALU.add).then_inc(c.stat.sem, c.stat.one())
                dve.wait_ge(c.std.sem, c.std.at(g + 1))
                ch.link(dve, dve.reciprocal(rstd, diff[0][:, 0:S]))
                for i in range(4):
                    k = 4 * g + i
                    ins = dve.scalar_tensor_tensor(zT[:, k, :], zT[:, k, :], norm_w[:, k:k + 1], rstd, ALU.mult, ALU.mult)
                ins.then_inc(c.mix.sem, c.mix.one())
    c.next_stage()


class MoePlan:
    def __init__(self, c, l):
        s, a = c.stream, c.a
        self.router = s.add(((lambda v: cols8(v)[:, :, 0:4]), a["moe_w_router_group_2"][l].rearrange("(k p) n -> p k n", p=P)),
                            ((lambda v: cols8(v)[:, :, 4:36]), a["moe_w_router_expert_2"][l].rearrange("(k p) n -> p k n", p=P)))
        self.router_end = len(s.loads)
        wg, wu, wd = a["moe_w_gate_2"][l], a["moe_w_up_2"][l], a["moe_w_down_2"][l]

        def source(n, i=0):
            e, half = i * (BODY // 2) + n // 2, n % 2
            c0 = half * CHUNK
            up = [((lambda v: cols8(v)), w[bass.ds(e, 1), :, c0:c0 + CHUNK].rearrange("o (k p) n -> p (o k) n", p=P)) for w in (wg, wu)]
            return up + [(rows2, wd[bass.ds(e, 1), c0:c0 + CHUNK, :].rearrange("o (k p) n -> p (o k) n", p=P))]
        self.mlp = Mlp(c, 2 * EXPERTS, source)
        self.end = len(s.loads)


def router_stage(c, plan, l):
    nc, s, ps, a = c.nc, c.stream, c.ps, c.a
    c.taken = 0
    spread_gates = c.take(EXPERTS * S)
    lg = c.take(2 * 36).rearrange("p (t n) -> p t n", t=2)
    bias = c.take(36)
    first = c.take(36)
    eg = c.take(8).rearrange("p (t n) -> p t n", t=2)
    e32 = c.take(64).rearrange("p (t n) -> p t n", t=2)
    o1 = c.take(64).rearrange("p (t n) -> p t n", t=2)
    o2 = c.take(64).rearrange("p (t n) -> p t n", t=2)
    w32 = c.take(64).rearrange("p (t n) -> p t n", t=2)
    sc = c.take(32).rearrange("p (k t) -> p k t", t=2)
    gT = c.take(S)

    def over(v, t_step, n):
        return bass.AP(v.tensor, v.offset, [v.ap[0], [t_step, 2], [0, n]])

    with nc.Block() as block:
        @block.sync
        def _(sp):
            sp.dma_start(bias[:, 0:4], a["moe_b_router_group_2"][l].partition_broadcast(P)).then_inc(c.small.sem, 16)
            sp.dma_start(bias[:, 4:36], a["moe_b_router_expert_2"][l].partition_broadcast(P)).then_inc(c.small.sem, 16)
            sp.dma_start(first, a["c_first"]).then_inc(c.small.sem, 16)
            s.issue(sp, plan.router_end + AHEAD)
            sp.wait_ge(c.aux_dve.sem, c.aux_dve.at(4))
            sp.dma_start(c.gates_dram[l], gT[0:32, :]).then_inc(c.stored.sem, 16)
            sp.wait_ge(c.stored.sem, c.stored.at(16))
            sp.dma_start(spread_gates, c.gates_dram[l].rearrange("e n -> (e n)").partition_broadcast(P)).then_inc(c.small.sem, 16)
            sp.wait_ge(c.small.sem, c.small.at(64))

        @block.tensor
        def _(pe):
            s.ready(pe, plan.router)
            w = cols8(s.slot(plan.router))
            for t in range(TT):
                for k in range(KT):
                    m = pe.matmul(ps[:, 4, t * 64:t * 64 + 36], c.xT[:, k, t * P:(t + 1) * P], w[:, k, 0:36],
                                  start=(k == 0), stop=(k == KT - 1))
            m.then_inc(c.aux_pe.sem, c.aux_pe.one())
            settle(c, pe, 1)
            pe.wait_ge(c.aux_dve.sem, c.aux_dve.at(3))
            for t in range(TT):
                m = pe.transpose(ps[0:32, 5, t * P:(t + 1) * P], w32[:, t, :], c.ident[:, :])
            m.then_inc(c.aux_pe.sem, c.aux_pe.one())

        @block.scalar
        def _(act):
            act.wait_ge(c.aux_dve.sem, c.aux_dve.at(1))
            act.activation(eg, eg, ACT.Exp).then_inc(c.aux_act.sem, c.aux_act.one())
            act.wait_ge(c.aux_dve.sem, c.aux_dve.at(2))
            act.activation(sc[:, 5, :], sc[:, 5, :], ACT.Exp).then_inc(c.aux_act.sem, c.aux_act.one())

        @block.vector
        def _(dve):
            ch = c.dve_chain

            def do(ins):
                ch.link(dve, ins)

            def first_of_largest(onehot, v, idx, n):
                do(dve.tensor_reduce(sc[:, 0, :], v, AX, ALU.max))
                do(dve.tensor_tensor(onehot, v, over(sc[:, 0, :], 1, n), ALU.is_equal))
                do(dve.tensor_tensor(onehot, onehot, bass.AP(idx.tensor, idx.offset, [idx.ap[0], [0, 2], [1, n]]), ALU.mult))
                do(dve.tensor_reduce(sc[:, 1, :], onehot, AX, ALU.max))
                do(dve.tensor_tensor(onehot, onehot, over(sc[:, 1, :], 1, n), ALU.is_equal))

            dve.wait_ge(c.small.sem, c.small.at(48))
            dve.wait_ge(c.aux_pe.sem, c.aux_pe.at(1))
            do(dve.tensor_tensor(lg, ps[:, 4, 0:128].rearrange("p (t n) -> p t n", t=2)[:, :, 0:36],
                                 bass.AP(bias.tensor, bias.offset, [bias.ap[0], [0, 2], [1, 36]]), ALU.add))
            og = o1[:, :, 0:4]
            first_of_largest(og, lg[:, :, 0:4], first[:, 0:4], 4)
            dve.tensor_tensor(eg, lg[:, :, 0:4], over(sc[:, 0, :], 1, 4), ALU.subtract).then_inc(c.aux_dve.sem, c.aux_dve.one())
            do(dve.tensor_scalar(og, og, 1.0, -NEG, ALU.subtract, ALU.mult))
            for t in range(TT):
                ins = dve.tensor_tensor(e32[:, t, :].rearrange("p (g n) -> p g n", g=4), lg[:, t, 4:36].rearrange("p (g n) -> p g n", g=4),
                                        spread(o1[:, t, 0:4], 8), ALU.add)
            do(ins)
            dve.wait_ge(c.aux_act.sem, c.aux_act.at(1))
            do(dve.tensor_reduce(sc[:, 2, :], eg, AX, ALU.add))
            first_of_largest(o1, e32, first[:, 4:36], 32)
            do(dve.tensor_copy(sc[:, 3, :], sc[:, 0, :]))
            do(dve.scalar_tensor_tensor(e32, o1, 3 * NEG, e32, ALU.mult, ALU.add))
            first_of_largest(o2, e32, first[:, 4:36], 32)
            dve.tensor_tensor(sc[:, 5, :], sc[:, 0, :], sc[:, 3, :], ALU.subtract).then_inc(c.aux_dve.sem, c.aux_dve.one())
            dve.wait_ge(c.aux_act.sem, c.aux_act.at(2))
            do(dve.scalar_tensor_tensor(sc[:, 6, :], sc[:, 5, :], 1.0, sc[:, 2, :], ALU.add, ALU.mult))
            do(dve.reciprocal(sc[:, 6, :], sc[:, 6, :]))
            do(dve.tensor_tensor(o2, o2, over(sc[:, 5, :], 1, 32), ALU.mult))
            do(dve.tensor_tensor(o1, o1, o2, ALU.add))
            dve.tensor_tensor(w32, o1, over(sc[:, 6, :], 1, 32), ALU.mult).then_inc(c.aux_dve.sem, c.aux_dve.one())
            dve.wait_ge(c.aux_pe.sem, c.aux_pe.at(2))
            dve.tensor_copy(gT[0:32, :], ps[0:32, 5, 0:S]).then_inc(c.aux_dve.sem, c.aux_dve.one())
    c.small.issued += 64
    c.stored.issued += 16
    c.next_stage()
    c.taken = EXPERTS * S
    return spread_gates


class DilatedPlan:
    def __init__(self, c):
        s, a = c.stream, c.a
        w = a["attn_w_qkv_2"][0]
        self.qkv = [s.add(col_piece(w, CHUNK * i)) for i in range(18)]
        self.proj_end = len(s.loads)
        self.out = [s.add(row_piece(a["attn_w_o_2"][0], r * 2 * P)) for r in range(2)]
        self.end = len(s.loads)


def dilated_mixer(c, plan, load_norm):
    nc, s, ps, a = c.nc, c.stream, c.ps, c.a
    c.taken = 0
    c.etaken = 0
    qk = c.take(24 * S).rearrange("p (i n) -> p i n", i=24)
    raw = c.take(24 * 2 * HD).rearrange("p (u s d) -> p u s d", u=24, s=2)
    nm = c.take(48).rearrange("p (u s) -> p u s", s=2)
    lsum = c.take(48).rearrange("p (u s) -> p u s", s=2)
    cosT = c.take(S)
    sinT = c.take(S)
    rot = [c.take(512) for _ in range(1)][0]
    base_taken = c.taken
    v = c.etake(3 * 2 * 512).rearrange("p (g t n) -> p g t n", g=3, t=2)
    masks = c.etake(3 * 384).rearrange("p (g n) -> p g n", g=3)
    rotm = c.etake(P)
    pos_i = c.etake(S).bitcast(I32)
    ang = c.etake(S)
    red = c.etake(S)
    turns = c.etake(S)
    perm = c.etake(P)
    TWO_PI = 2 * np.pi
    C1 = 6.28125
    C2 = float(np.float32(TWO_PI - C1))
    C3 = float(TWO_PI - C1 - C2)
    MAGIC = 12582912.0

    def qk_group(g, part, i):
        pos = plan.qkv[g * 6 + part * 2 + i]
        t0 = g * 8 + part * 4 + 2 * i
        return feature_tiles(c, pos, lambda k, j: cols8(s.slot(pos))[:, k, j * P:(j + 1) * P], qk[:, t0:t0 + 2, :], "act", 1)

    def v_group(g, i):
        pos = plan.qkv[g * 6 + 4 + i]
        w = cols8(s.slot(pos))
        return Group(lambda bank: [[(bank[:, t * S:(t + 1) * S], c.xT[:, k, t * P:(t + 1) * P], w[:, k, :])
                                    for k in range(KT)] for t in range(TT)],
                     copier(v[:, g, :, i * CHUNK:(i + 1) * CHUNK], lambda bank: bank.rearrange("p (t n) -> p t n", t=2)),
                     "act", (pos,), 1)
    groups = []
    for g in range(3):
        groups += [qk_group(g, part, i) for part in range(2) for i in range(2)] + [v_group(g, i) for i in range(2)]

    with nc.Block() as block:
        @block.sync
        def _(sp):
            for dst, src in ((masks, a["c_dilated"]), (rotm, a["c_rot"]), (pos_i, a["positions_2"][0].partition_broadcast(P))):
                sp.dma_start(dst, src).then_inc(c.small.sem, 16)
            s.issue(sp, plan.proj_end + AHEAD)

        @block.tensor
        def _(pe):
            _, owed = run_projections(c, groups, pe=pe)
            settle(c, pe, owed)

        @block.scalar
        def _(act):
            run_projections(c, groups, act=act)
            act.wait_ge(c.aux_dve.sem, c.aux_dve.at(2))
            act.activation(sinT, sinT, ACT.Sin)
            act.activation(cosT, cosT, ACT.Sin)

        @block.vector
        def _(dve):
            ch = c.dve_chain
            dve.wait_ge(c.small.sem, c.small.at(48))
            ch.link(dve, dve.tensor_copy(ang, pos_i))
            ch.link(dve, dve.tensor_scalar(ang, ang, c.tiny[:, 1:2], None, ALU.mult))
            for out, shift in ((sinT, 0.0), (cosT, 0.25)):
                ch.link(dve, dve.tensor_scalar(turns, ang, 1.0 / TWO_PI, shift, ALU.mult, ALU.add))
                ch.link(dve, dve.tensor_scalar(turns, turns, MAGIC, None, ALU.add))
                ch.link(dve, dve.tensor_scalar(turns, turns, MAGIC, None, ALU.subtract))
                ch.link(dve, dve.scalar_tensor_tensor(red, turns, -C1, ang, ALU.mult, ALU.add))
                ch.link(dve, dve.scalar_tensor_tensor(red, turns, -C2, red, ALU.mult, ALU.add))
                ch.link(dve, dve.scalar_tensor_tensor(red, turns, -C3, red, ALU.mult, ALU.add))
                ch.link(dve, dve.tensor_scalar(red, red, shift * TWO_PI, 3.1415925, ALU.add, ALU.min))
                dve.tensor_scalar(out, red, -3.1415925, None, ALU.max).then_inc(c.aux_dve.sem, c.aux_dve.one())
    c.small.issued += 48
    c.next_stage()

    with nc.Block() as block:
        @block.tensor
        def _(pe):
            for i in range(24):
                if i >= 4:
                    pe.wait_ge(c.by_dve.sem, c.by_dve.at(i - 3))
                pe.matmul(ps[:, 4 + i % 4, 0:S], rotm, qk[:, i, :], start=True, stop=True).then_inc(c.aux_pe.sem, c.aux_pe.one())

        @block.vector
        def _(dve):
            ch = c.dve_chain
            for i in range(24):
                dve.wait_ge(c.aux_pe.sem, c.aux_pe.at(i + 1))
                ins = dve.tensor_tensor(rot[:, (i % 2) * S:(i % 2 + 1) * S], ps[:, 4 + i % 4, 0:S], sinT, ALU.mult)
                ins.then_inc(c.by_dve.sem, c.by_dve.one())
                ch.link(dve, dve.tensor_tensor(qk[:, i, :], qk[:, i, :], cosT, ALU.mult))
                dve.tensor_tensor(qk[:, i, :], qk[:, i, :], rot[:, (i % 2) * S:(i % 2 + 1) * S], ALU.add)
    c.next_stage()

    units = []
    for g in range(3):
        for h in range(8):
            i, lo = h // 2, 64 * (h % 2)
            q = (lambda t, g=g, i=i, lo=lo: qk[lo:lo + 64, g * 8 + i, t * P:(t + 1) * P])
            units.append(Unit(q, qk[lo:lo + 64, g * 8 + 4 + i, :], S, window(c.E[:, :], 3072 + g * 384, [[P, 2], [1, S]]),
                              [v[:, g, t, h * HD:(h + 1) * HD] for t in range(TT)]))
    c.taken = base_taken
    attention_stage(c, units, raw, nm, lsum)
    c.taken = base_taken

    w = c.take(48).rearrange("p (g n) -> p g n", g=3)
    top = c.take(16)
    den = c.take(16)
    rows = c.take(1024).rearrange("p (s n) -> p s n", s=2)
    outT = c.take(4 * S).rearrange("p (f n) -> p f n", f=4)
    nmv = nm.rearrange("p (g u) s -> p g (u s)", g=3)
    lv = lsum.rearrange("p (g u) s -> p g (u s)", g=3)
    tensor, scalar = transpose_mix(c, rows, outT, 4)
    with nc.Block() as block:
        @block.sync
        def _(sp):
            s.issue(sp, plan.end + AHEAD)

        @block.vector
        def _(dve):
            ch = c.dve_chain

            def do(ins):
                ch.link(dve, ins)
            do(dve.tensor_tensor(top, nmv[:, 0, :], nmv[:, 1, :], ALU.min))
            do(dve.tensor_tensor(top, top, nmv[:, 2, :], ALU.min))
            for g in range(3):
                ins = dve.tensor_tensor(w[:, g, :], top, nmv[:, g, :], ALU.subtract)
            ins.then_inc(c.aux_dve.sem, c.aux_dve.one())
            dve.wait_ge(c.aux_act.sem, c.aux_act.at(1))
            do(dve.tensor_tensor(lv, lv, w, ALU.mult))
            do(dve.tensor_tensor(den, lv[:, 0, :], lv[:, 1, :], ALU.add))
            do(dve.tensor_tensor(den, den, lv[:, 2, :], ALU.add))
            do(dve.reciprocal(den, den))
            for g in range(3):
                ins = dve.tensor_tensor(w[:, g, :], w[:, g, :], den, ALU.mult)
            do(ins)
            hr = rows.rearrange("p s (h d) -> p h s d", h=8)
            for g in range(3):
                rg = raw[:, 8 * g:8 * g + 8, :, :]
                ins = dve.tensor_tensor(hr if g == 0 else rg, rg, spread(w[:, g, :].rearrange("p (u s) -> p u s", s=2), HD), ALU.mult)
            do(ins)
            do(dve.tensor_tensor(raw[:, 8:16, :, :], raw[:, 8:16, :, :], raw[:, 16:24, :, :], ALU.add))
            dve.tensor_tensor(hr, hr, raw[:, 8:16, :, :], ALU.add).then_inc(c.mix.sem, c.mix.one())

        @block.scalar
        def _(act):
            load_norm(act)
            act.wait_ge(c.aux_dve.sem, c.aux_dve.at(1))
            act.activation(w, w, ACT.Exp).then_inc(c.aux_act.sem, c.aux_act.one())
            scalar(act)

        @block.tensor
        def _(pe):
            pe.wait_ge(c.mix.sem, c.mix.at(1))
            tensor(pe)
            pe.wait_ge(c.mixT.sem, c.mixT.at(2))
            for r in range(2):
                s.ready(pe, plan.out[r])
                wo = rows2(s.slot(plan.out[r]))
                for kk in range(2):
                    k = 2 * r + kk
                    for t in range(TT):
                        for half in range(2):
                            m = pe.matmul(ps[:, 2 * t + half, :], outT[:, k, t * P:(t + 1) * P],
                                          wo[:, kk, half * 512:(half + 1) * 512], start=(k == 0), stop=(k == 3))
                m.then_inc(s.used, 1)
    c.next_stage()


def ffn_plan(c, w1, w2):
    def source(n, i=0):
        c0 = (i * BODY + n) * CHUNK
        return [((lambda v: cols8(v)), w1[:, bass.ds(c0, CHUNK)].rearrange("(k p) n -> p k n", p=P)),
                ((lambda v: cols8(v)), w1[:, bass.ds(c0 + D_FF, CHUNK)].rearrange("(k p) n -> p k n", p=P)),
                (rows2, w2[bass.ds(c0, CHUNK), :].rearrange("(k p) n -> p k n", p=P))]
    return Mlp(c, D_FF // CHUNK, source)


def build(nc, a, out, until=None):
    with ExitStack() as ctx:
        c = Core(nc, ctx, a, out)
        plans = []
        for l in range(DEPTH):
            plans.append((ffn_plan(c, a["ffn1_w1"][l], a["ffn1_w2"][l]), MixPlan(c, l),
                          ffn_plan(c, a["ffn2_w1"][l], a["ffn2_w2"][l])))
        ssd, moe0 = SsdPlan(c), MoePlan(c, 0)
        dil, moe1 = DilatedPlan(c), MoePlan(c, 1)

        setup_stage(c)
        for l, (ffn1, mix, ffn2) in enumerate(plans):
            c.taken = 0
            mlp_stage(c, ffn1, norm_loader(c, a["ln1_g"][l], a["ln1_b"][l]))
            norm_stage(c, 0.5)
            if until == ("ffn1", l):
                return c
            token_mix(c, mix, l, norm_loader(c, a["ln2_g"][l], a["ln2_b"][l]))
            norm_stage(c, 1.0)
            if until == ("mix", l):
                return c
            c.taken = 0
            mlp_stage(c, ffn2, norm_loader(c, a["ln3_g"][l], a["ln3_b"][l]))
            norm_stage(c, 0.5)
        if until == "first":
            return c
        ssd_mixer(c, ssd, norm_loader(c, a["ln_g_2"][0, 0], a["ln_b_2"][0, 0]))
        norm_stage(c, 1.0)
        if until == "ssd":
            return c
        gates = router_stage(c, moe0, 0)
        mlp_stage(c, moe0.mlp, norm_loader(c, a["ln_g_2"][0, 1], a["ln_b_2"][0, 1]), gates)
        norm_stage(c, 1.0)
        if until == "moe0":
            return c
        dilated_mixer(c, dil, norm_loader(c, a["ln_g_2"][1, 0], a["ln_b_2"][1, 0]))
        norm_stage(c, 1.0)
        if until == "dil":
            return c
        gates = router_stage(c, moe1, 1)
        mlp_stage(c, moe1.mlp, norm_loader(c, a["ln_g_2"][1, 1], a["ln_b_2"][1, 1]), gates)
        norm_stage(c, 1.0, last=True)
        return c


def t5_bucket(dist):
    n = np.maximum(dist, 0)
    ratio = np.log(np.maximum(n, 1).astype(np.float32) / np.float32(16)) / np.float32(np.log(128 / 16))
    large = 16 + (ratio * 16).astype(np.int32)
    return np.where(n < 16, n, np.minimum(large, 31))


def constants():
    f = np.float32
    k = {}
    k["c_ident"] = np.eye(P, dtype=f)
    k["c_flip"] = np.eye(P, dtype=f)[::-1].copy()
    dist = 255 - np.arange(512)
    onehot = np.zeros((32, 512), f)
    onehot[t5_bucket(dist), np.arange(512)] = 1
    k["c_onehot"] = onehot * (dist >= 0)
    bmask = np.zeros((16, 512), f)
    bmask[:, dist < 0] = NEG
    bmask[8:, dist >= 128] = NEG
    k["c_bmask"] = bmask
    tok = np.arange(S)
    k["c_tri"] = (tok[:, None] <= tok[None]).astype(f).reshape(TT, P, S).transpose(1, 0, 2).copy()
    d = 128 + np.arange(P)[:, None] - np.arange(384)[None]
    k["c_causal"] = np.where(d >= 0, 0, NEG).astype(f)
    k["c_dilated"] = np.stack([np.where((d >= 0) & (d % r == 0) & (d <= 128 * r), 0, NEG) for r in (1, 4, 16)], 1).astype(f)
    rot = np.zeros((P, P), f)
    for b in (0, 64):
        for j in range(8):
            rot[b + j + 8, b + j] = -1
            rot[b + j, b + j + 8] = 1
    k["c_rot"] = rot
    inv = (f(500000.0) ** (-np.arange(0, 16, 2, dtype=f) / f(16))).astype(f)
    p = np.arange(P) % 64
    k["c_cols"] = np.stack([(np.arange(P) >= 31).astype(f), np.where(p < 16, inv[p % 8], 0).astype(f)], 1)
    first = np.concatenate([8 - np.arange(4), 64 - np.arange(32)]).astype(f)
    k["c_first"] = np.tile(first, (P, 1))
    return k


_DIRECT = ["x", "rel_bias", "ln1_g", "ln1_b", "ffn1_w1", "ffn1_w2", "w_in", "cmp_k_w1", "cmp_k_w2", "cmp_v_w1",
           "cmp_v_w2", "swa_sinks", "fox_b_f", "w_br_a", "w_br_b", "w_br_c", "w_gate", "w_out", "ln2_g", "ln2_b",
           "ffn2_w1", "ffn2_w2", "ln3_g", "ln3_b", "positions_2", "ssd_w_in_2", "ssd_dt_bias_2", "ssd_a_log_2",
           "ssd_w_out_2", "attn_w_qkv_2", "attn_w_o_2", "ln_g_2", "ln_b_2", "moe_w_router_group_2",
           "moe_b_router_group_2", "moe_w_router_expert_2", "moe_b_router_expert_2", "moe_w_gate_2",
           "moe_w_up_2", "moe_w_down_2"]


def lay_out(inputs):
    arrays = {n: np.ascontiguousarray(inputs[n]) for n in _DIRECT}
    pe = [np.asarray(inputs[n]).reshape(DEPTH, 16, P).transpose(0, 2, 1) for n in ("cmp_pe_k", "cmp_pe_v")]
    arrays["c_pe"] = np.ascontiguousarray(np.concatenate(pe, 2))
    arrays["c_bgate"] = np.ascontiguousarray(np.asarray(inputs["b_gate"]).reshape(DEPTH, 24, P).transpose(0, 2, 1))
    cw = np.asarray(inputs["ssd_conv_w_2"])[0].reshape(4, 24, P).transpose(2, 1, 0).reshape(P, 96)
    cbias = np.asarray(inputs["ssd_conv_b_2"])[0].reshape(24, P).T
    nw = np.asarray(inputs["ssd_norm_w_2"])[0].reshape(16, P).T
    dsk = np.repeat(np.asarray(inputs["ssd_d_2"])[0], HD).reshape(16, P).T
    arrays["c_ssd"] = np.ascontiguousarray(np.concatenate([cw, cbias, nw, dsk], 1))
    arrays.update(constants())
    return arrays


def kernel(**inputs):
    import concourse.bacc as bacc
    from concourse.bass_utils import run_bass_kernel_spmd

    nc = bacc.Bacc("TRN2", target_bir_lowering=False, num_devices=1)
    arrays = lay_out(inputs)
    a = {n: nc.dram_tensor(f"in_{n}", v.shape, mybir.dt.from_np(v.dtype), kind="ExternalInput").ap() for n, v in arrays.items()}
    out = nc.dram_tensor("out_x", (1, S, D), F32, kind="ExternalOutput").ap()
    build(nc, a, out)
    r = run_bass_kernel_spmd(nc, [{f"in_{n}": v for n, v in arrays.items()}], core_ids=[0])
    return r.results[0]["out_x"]
```

```python
from contextlib import ExitStack

import numpy as np

import concourse.bass as bass
from concourse import mybir

F32 = mybir.dt.float32
I32 = mybir.dt.int32
ALU = mybir.AluOpType
ACT = mybir.ActivationFunctionType
AX = mybir.AxisListType.X

P = 128
D = 1024
S = 256
KT = D // P
TT = S // P
DEPTH = 2
HD = 64
SCALE = HD ** -0.5
NEG = -1e30
D_FF = 2816
CHUNK = 256
EXPERTS = 32
HIDDEN = 512
ALPHA = (2 * DEPTH) ** 0.25
LN_EPS = 1e-5
NC_CMP = 15
RING = 12
SLOT = 2048
AHEAD = RING - 2
BODY = 4
SSD_T = 16
XBC_T = 24
N_UNITS = 40
SLOTS = 64


class Signal:

    def __init__(self, sem, credit=0):
        self.sem = sem
        self.base = credit
        self.issued = credit

    def one(self):
        self.issued += 1
        return 1

    def at(self, n):
        return self.base + n


class Chain:

    def __init__(self, sem):
        self.sem = sem
        self.n = 0

    def link(self, eng, ins):
        self.n += 1
        ins.then_inc(self.sem, 1)
        eng.wait_ge(self.sem, self.n)


class WeightStream:

    def __init__(self, ring, landed, used):
        self.ring = ring
        self.landed = landed
        self.used = used
        self.loads = [None] * RING
        self.value = [0] * RING
        self.total = [0] * RING
        self.issued = RING

    def slot(self, pos):
        return self.ring[:, pos % RING, :]

    def add(self, *loads):
        pos = len(self.loads)
        self.total[pos % RING] += 16 * len(loads)
        self.loads.append(loads)
        self.value.append(self.total[pos % RING])
        return pos

    def align(self):
        n = -len(self.loads) % RING
        self.loads += [None] * n
        self.value += [0] * n
        return n

    def issue(self, sp, upto):
        for pos in range(self.issued, min(upto, len(self.loads))):
            if self.loads[pos] is None:
                continue
            sp.wait_ge(self.used, pos - RING + 1)
            for into, src in self.loads[pos]:
                sp.dma_start(into(self.slot(pos)), src).then_inc(self.landed[pos % RING], 16)
        self.issued = max(self.issued, upto)

    def ready(self, pe, pos):
        pe.wait_ge(self.landed[pos % RING], self.value[pos])


def cols8(ap):
    return ap.rearrange("p (k n) -> p k n", k=8)


def rows2(ap):
    return ap.rearrange("p (k n) -> p k n", k=2)


def col_piece(w, c0, n=CHUNK):
    return (lambda s: cols8(s)[:, :, 0:n]), w[:, c0:c0 + n].rearrange("(k p) n -> p k n", p=P)


def row_piece(w, r0):
    return rows2, w[r0:r0 + 2 * P, :].rearrange("(k p) n -> p k n", p=P)


class DenseCounts:

    def __init__(self, c, l):
        self.hid_full = c.counted(f"dense_hidden_products_full_{l}").sem
        self.sg_full = c.counted(f"dense_silu_full_{l}").sem
        self.up_gated = c.counted(f"dense_up_gated_{l}").sem
        self.h_full = c.counted(f"dense_hidden_full_{l}").sem


class PackedCounts:

    def __init__(self, c, l):
        def pair(name):
            return [c.counted(f"packed_{name}_{l}_{e}").sem for e in range(2)]
        self.chosen = pair("tokens_chosen")
        self.gathered = pair("tokens_gathered")
        self.xe_full = pair("tokens_ready")
        self.hid_full = pair("hidden_products_full")
        self.sg_full = pair("silu_full")
        self.h_full = pair("hidden_full")
        self.scattered = c.counted(f"packed_scattered_{l}").sem
        self.weights = c.counted(f"packed_scatter_weights_ready_{l}").sem
        self.y_full = c.counted(f"packed_outputs_ready_{l}").sem


class Core:

    def __init__(self, nc, ctx, a, out):
        self.nc = nc
        self.a = a
        self.out = out
        self.counts = []
        self.ctx = ctx

        def sb(name, shape):
            return ctx.enter_context(nc.sbuf_tensor(name, shape, F32))

        self.ring = sb("ring", [P, RING, SLOT])
        self.x = sb("x_rows", [P, TT, D])
        self.xT = sb("xT", [P, KT, S])
        self.norm = sb("norm_params", [P, 2, D])
        self.E = sb("bias_tiles", [P, 17 * 384])
        self.ident = sb("ident", [P, P])
        self.ones = sb("ones", [P, P])
        self.zeros = sb("zeros", [P, 512])
        self.tri = sb("tri", [P, TT, S])
        self.tiny = sb("tiny", [P, 64])
        self.arena = sb("arena", [P, 14600])
        self.taken = 0
        self.etaken = 0
        self.ps = ctx.enter_context(nc.psum_tensor("ps", [P, 8, 512], F32))
        self.scratch = nc.dram_tensor("bias_scratch", [16, 512], F32, kind="Internal").ap()
        self.slots_dram = nc.dram_tensor("slots_scratch", [DEPTH, EXPERTS, S], F32, kind="Internal").ap()
        self.over = ctx.enter_context(nc.sbuf_tensor("slots_overrun", [1, 1], I32))
        self.gates_dram = nc.dram_tensor("gates_scratch", [DEPTH, EXPERTS, S], F32, kind="Internal").ap()

        self.small = self.counted("small_loads_landed")
        self.setup_dve = self.counted("setup_vector_done")
        self.setup_pe = self.counted("setup_tensor_done")
        self.setup_act = self.counted("setup_scalar_done")
        self.norm_loaded = self.counted("norm_params_landed")
        self.hid_full = self.counted("hidden_products_full")
        self.sg_full = self.counted("silu_full")
        self.h_full = self.counted("hidden_full", credit=4)
        self.stat = self.counted("variance_ready")
        self.std = self.counted("std_ready")
        self.x_new = self.counted("x_rows_ready")
        self.xT_ps = self.counted("xT_in_psum")
        self.xT_done = self.counted("xT_ready")
        self.proj_full = self.counted("projection_full")
        self.by_act = self.counted("evacuated_by_scalar")
        self.by_dve = self.counted("evacuated_by_vector")
        self.sc_full = self.counted("scores_full")
        self.s_ready = self.counted("logits_ready")
        self.nm_ready = self.counted("negative_max_ready")
        self.p_ready = self.counted("probs_ready")
        self.pt_ps = self.counted("probsT_in_psum")
        self.pt_ready = self.counted("probsT_ready")
        self.o_ps = self.counted("head_output_in_psum")
        self.o_raw = self.counted("head_output_kept")
        self.mix = self.counted("mixer_rows_ready")
        self.mixT_ps = self.counted("mixer_transposed_in_psum")
        self.mixT = self.counted("mixerT_ready")
        self.gate_act = self.counted("branch_gate_ready")
        self.merged = self.counted("merged_ready")
        self.aux_pe = self.counted("aux_tensor_steps")
        self.aux_act = self.counted("aux_scalar_steps")
        self.aux_dve = self.counted("aux_vector_steps")
        self.stored = self.counted("stores_landed")
        self.spread_landed = self.counted("spread_rows_landed")
        self.dve_chain = Chain(ctx.enter_context(nc.semaphore("vector_chain")))
        self.act_chain = Chain(ctx.enter_context(nc.semaphore("scalar_chain")))
        self.dense = [DenseCounts(self, l) for l in range(DEPTH)]
        self.packed = [PackedCounts(self, l) for l in range(DEPTH)]
        landed = [ctx.enter_context(nc.semaphore(f"weights_landed_{n}")) for n in range(RING)]
        used = ctx.enter_context(nc.semaphore("weights_used"))
        self.stream = WeightStream(self.ring, landed, used)

    def counted(self, name, credit=0):
        s = Signal(self.ctx.enter_context(self.nc.semaphore(name)), credit)
        self.counts.append(s)
        return s

    def next_stage(self):
        for s in self.counts:
            s.base = s.issued

    def take(self, n):
        v = self.arena[:, self.taken:self.taken + n]
        self.taken += n
        assert self.taken <= 14600, self.taken
        return v

    def etake(self, n):
        v = self.E[:, self.etaken:self.etaken + n]
        self.etaken += n
        assert self.etaken <= 17 * 384
        return v


def window(view, offset, dims):
    return bass.AP(view.tensor, view.offset + offset, [view.ap[0]] + dims)


def setup_stage(c):
    nc, a, ps = c.nc, c.a, c.ps
    c.taken = 0
    rb = c.take(16)
    onehot = c.take(512)
    bmask = c.take(512)
    brow = c.take(512)
    flip = c.take(P)
    hank = c.take(16 * 384)
    hank_v = hank.rearrange("p (h n) -> p h n", h=16)
    E_v = c.E[:, :].rearrange("p (h n) -> p h n", h=17)
    s = c.stream
    with nc.Block() as block:
        @block.sync
        def _(sp):
            sp.dma_start(c.x[:, :, :], a["x"][0].rearrange("(t p) n -> p t n", p=P)).then_inc(c.small.sem, 16)
            sp.dma_start(c.ident[:, :], a["c_ident"]).then_inc(c.small.sem, 16)
            sp.dma_start(rb[0:32, :], a["rel_bias"]).then_inc(c.small.sem, 16)
            sp.dma_start(onehot[0:32, :], a["c_onehot"]).then_inc(c.small.sem, 16)
            sp.dma_start(bmask[0:16, :], a["c_bmask"]).then_inc(c.small.sem, 16)
            sp.dma_start(flip, a["c_flip"]).then_inc(c.small.sem, 16)
            sp.dma_start(E_v[:, 16, :], a["c_causal"]).then_inc(c.small.sem, 16)
            sp.dma_start(c.tri[:, :, :], a["c_tri"]).then_inc(c.small.sem, 16)
            sp.dma_start(c.tiny[:, 0:2], a["c_cols"]).then_inc(c.small.sem, 16)
            s.issue(sp, RING + AHEAD)

        @block.scalar
        def _(act):
            act.wait_ge(c.setup_dve.sem, 2)
            act.dma_start(c.scratch, brow[0:16, :]).then_inc(c.stored.sem, 16)
            act.wait_ge(c.stored.sem, 16)
            act.dma_start(hank_v, bass.AP(c.scratch.tensor, 0, [[1, P], [512, 16], [1, 384]])).then_inc(c.setup_act.sem, 16)

        @block.tensor
        def _(pe):
            pe.wait_ge(c.small.sem, 16 * 9)
            pe.matmul(ps[0:16, 7, :], rb[0:32, :], onehot[0:32, :], start=True, stop=True).then_inc(c.setup_pe.sem, 1)
            for t in range(TT):
                for k in range(KT):
                    m = pe.transpose(ps[:, 2 * t + k // 4, (k % 4) * P:(k % 4 + 1) * P],
                                     c.x[:, t, k * P:(k + 1) * P], c.ident[:, :])
            m.then_inc(c.setup_pe.sem, 1)
            pe.wait_ge(c.setup_act.sem, 16)
            for h in range(16):
                if h >= 4:
                    pe.wait_ge(c.setup_dve.sem, 3 + h - 4 + 1)
                pe.matmul(ps[:, 4 + h % 4, 0:384], flip, hank_v[:, h, :], start=True, stop=True).then_inc(c.setup_pe.sem, 1)

        @block.vector
        def _(dve):
            dve.memset(c.ones[:, :], 1.0)
            dve.memset(c.zeros[:, :], 0.0)
            dve.memset(c.tiny[:, 2:3], 0.0).then_inc(s.used, RING)
            dve.memset(c.tiny[:, 3:4], 0.0).then_inc(c.h_full.sem, 4)
            dve.memset(c.tiny[:, 4:8], 0.0).then_inc(c.setup_dve.sem, 1)
            dve.wait_ge(c.setup_pe.sem, 1)
            dve.tensor_tensor(brow[0:16, :], ps[0:16, 7, :], bmask[0:16, :], ALU.add).then_inc(c.setup_dve.sem, 1)
            dve.wait_ge(c.setup_pe.sem, 2)
            for t in range(TT):
                m = dve.tensor_copy(c.xT[:, :, t * P:(t + 1) * P],
                                    ps[:, 2 * t:2 * t + 2, :].rearrange("p b (k n) -> p (b k) n", k=4))
            m.then_inc(c.setup_dve.sem, 1)
            for h in range(16):
                dve.wait_ge(c.setup_pe.sem, 2 + h + 1)
                dve.tensor_copy(E_v[:, h, :], ps[:, 4 + h % 4, 0:384]).then_inc(c.setup_dve.sem, 1)

    c.small.issued += 144
    c.stored.issued += 16
    c.next_stage()


class Mlp:

    def __init__(self, c, chunks, source):
        self.chunks = chunks
        self.source = source
        self.loops = chunks // BODY
        self.tail = chunks % BODY
        self.pad = c.stream.align()
        self.pos = len(c.stream.loads)
        for n in range(3 * chunks):
            c.stream.add(source(n % RING, n // RING))


def issue_mlp(s, sp, mlp):
    p0 = mlp.pos
    s.issue(sp, p0 + RING)
    if mlp.loops > 1:
        with sp.Fori(1, mlp.loops) as i:
            for q in range(RING):
                sp.wait_ge(s.used, i * RING + (p0 + q - RING + 1))
                into, src = mlp.source(q, i)
                sp.dma_start(into(s.slot(q)), src).then_inc(s.landed[q], 16)
    s.issued = max(s.issued, p0 + RING * mlp.loops)
    s.issue(sp, p0 + 3 * mlp.chunks + AHEAD)


def mlp_stage(c, mlp, load_norm):
    nc, ps, s = c.nc, c.ps, c.stream
    hid = [c.take(2 * S).rearrange("p (k n) -> p k n", k=2) for _ in range(2)]
    sg = [c.take(S) for _ in range(2)]
    p0 = mlp.pos
    slots0 = [s.value[p0 + q] for q in range(RING)]

    def bodies(eng, emit):
        if mlp.loops:
            with eng.Fori(0, mlp.loops) as i:
                for n in range(BODY):
                    emit(i, n)
        for n in range(mlp.tail):
            emit(mlp.loops, n)

    with nc.Block() as block:
        @block.sync
        def _(sp):
            issue_mlp(s, sp, mlp)

        @block.tensor
        def _(pe):
            for b in range(4):
                z = pe.matmul(ps[:, b, :], c.zeros[0:1, 0:P], c.zeros[0:1, :], start=True, stop=False)
                if b == 0:
                    owed = mlp.pad
                    if owed:
                        z.then_inc(s.used, owed)

            def chunk(i, n):
                for j in range(2):
                    m = 2 * n + j
                    bank = 4 + m % 4
                    pe.wait_ge(c.h_full.sem, i * 2 * BODY + c.h_full.at(m - 3))
                    for q in range(2):
                        slot = 3 * n + q
                        if j == 0:
                            pe.wait_ge(s.landed[slot], i * 16 + slots0[slot])
                        w = cols8(s.slot(slot))
                        for k in range(KT):
                            mm = pe.matmul(ps[:, bank, q * S:(q + 1) * S], w[:, k, j * P:(j + 1) * P],
                                           c.xT[:, k, :], start=(k == 0), stop=(k == KT - 1))
                        if q == 0 and j == 1:
                            mm.then_inc(s.used, 1)
                    mm.then_inc(c.hid_full.sem, 1)
                slot = 3 * n + 2
                pe.wait_ge(s.landed[slot], i * 16 + slots0[slot])
                w = rows2(s.slot(slot))
                for kk in range(2):
                    pe.wait_ge(c.h_full.sem, i * 2 * BODY + c.h_full.at(2 * n + kk + 1))
                    for t in range(TT):
                        for half in range(2):
                            mm = pe.matmul(ps[:, 2 * t + half, :], hid[n % 2][:, kk, t * P:(t + 1) * P],
                                           w[:, kk, half * 512:(half + 1) * 512], start=False, stop=False)
                            if kk == 0 and t == 0 and half == 0:
                                mm.then_inc(s.used, 1)
                mm.then_inc(s.used, 1)

            bodies(pe, chunk)
            for b in range(4):
                pe.matmul(ps[:, b, 0:1], c.zeros[0:1, 0:P], c.zeros[0:1, 0:1], start=False, stop=True)

        @block.scalar
        def _(act):
            load_norm(act)

            def chunk(i, n):
                for j in range(2):
                    m = 2 * n + j
                    act.wait_ge(c.hid_full.sem, i * 2 * BODY + c.hid_full.at(m + 1))
                    act.wait_ge(c.h_full.sem, i * 2 * BODY + c.h_full.at(m - 1))
                    act.activation(sg[m % 2], ps[:, 4 + m % 4, 0:S], ACT.Silu).then_inc(c.sg_full.sem, 1)

            bodies(act, chunk)

        @block.vector
        def _(dve):
            def chunk(i, n):
                for j in range(2):
                    m = 2 * n + j
                    up = ps[:, 4 + m % 4, S:2 * S]
                    if j == 0:
                        dve.wait_ge(s.used, i * RING + (p0 + 3 * n - 3))
                    dve.wait_ge(c.sg_full.sem, i * 2 * BODY + c.sg_full.at(m + 1))
                    dve.tensor_tensor(hid[n % 2][:, j, :], up, sg[m % 2], ALU.mult).then_inc(c.h_full.sem, 1)

            bodies(dve, chunk)

    for sig in (c.hid_full, c.sg_full, c.h_full):
        sig.issued += 2 * mlp.chunks
    c.next_stage()


def norm_loader(c, gamma, beta):
    def load(act):
        act.dma_start(c.norm[:, 0, :], gamma.partition_broadcast(P)).then_inc(c.norm_loaded.sem, 16)
        act.dma_start(c.norm[:, 1, :], beta.partition_broadcast(P)).then_inc(c.norm_loaded.sem, 16)
        c.norm_loaded.issued += 32
    return load


def norm_stage(c, weight, last=False):
    nc, ps, s = c.nc, c.ps, c.stream
    c.taken = 0
    stats = c.take(2 * 2 * 6).rearrange("p (t h n) -> p t h n", t=2, h=2)
    mv = c.take(4).rearrange("p (t n) -> p t n", t=2)
    rstd = c.take(4).rearrange("p (t n) -> p t n", t=2)
    with nc.Block() as block:
        @block.sync
        def _(sp):
            if last:
                for t in range(TT):
                    sp.wait_ge(c.x_new.sem, c.x_new.at(t + 1))
                    sp.dma_start(c.out[0, t * P:(t + 1) * P, :], c.x[:, t, :]).then_inc(c.stored.sem, 16)
                sp.wait_ge(c.stored.sem, c.stored.at(32))

        @block.vector
        def _(dve):
            ch = c.dve_chain
            for t in range(TT):
                ch.link(dve, dve.scalar_tensor_tensor(c.x[:, t, :], c.x[:, t, :], ALPHA / weight,
                                                      ps[:, 2 * t:2 * t + 2, :].rearrange("p b n -> p (b n)"),
                                                      ALU.mult, ALU.add))
                for half in range(2):
                    ins = dve.bn_stats(stats[:, t, half, :], c.x[:, t, half * 512:(half + 1) * 512])
                ch.link(dve, ins)
                ch.link(dve, dve.bn_aggr(mv[:, t, :], stats[:, t, :, :].rearrange("p h n -> p (h n)")))
                dve.tensor_scalar(rstd[:, t, 0:1], mv[:, t, 1:2], LN_EPS / weight ** 2, None, ALU.add).then_inc(c.stat.sem, c.stat.one())
            for t in range(TT):
                dve.wait_ge(c.std.sem, c.std.at(t + 1))
                ch.link(dve, dve.reciprocal(rstd[:, t, 0:1], rstd[:, t, 1:2]))
                ch.link(dve, dve.tensor_scalar(c.x[:, t, :], c.x[:, t, :], mv[:, t, 0:1], rstd[:, t, 0:1], ALU.subtract, ALU.mult))
                if t == 0:
                    dve.wait_ge(c.norm_loaded.sem, c.norm_loaded.at(0))
                ch.link(dve, dve.tensor_tensor(c.x[:, t, :], c.x[:, t, :], c.norm[:, 0, :], ALU.mult))
                dve.tensor_tensor(c.x[:, t, :], c.x[:, t, :], c.norm[:, 1, :], ALU.add).then_inc(c.x_new.sem, c.x_new.one())

        @block.scalar
        def _(act):
            for t in range(TT):
                act.wait_ge(c.stat.sem, c.stat.at(t + 1))
                act.activation(rstd[:, t, 1:2], rstd[:, t, 0:1], ACT.Sqrt).then_inc(c.std.sem, c.std.one())
            if not last:
                for t in range(TT):
                    act.wait_ge(c.xT_ps.sem, c.xT_ps.at(t + 1))
                    act.activation(c.xT[:, :, t * P:(t + 1) * P],
                                   ps[:, 4 + 2 * t:6 + 2 * t, :].rearrange("p b (k n) -> p (b k) n", k=4), ACT.Copy)

        @block.tensor
        def _(pe):
            if not last:
                for t in range(TT):
                    pe.wait_ge(c.x_new.sem, c.x_new.at(t + 1))
                    for k in range(KT):
                        m = pe.transpose(ps[:, 4 + 2 * t + k // 4, (k % 4) * P:(k % 4 + 1) * P],
                                         c.x[:, t, k * P:(k + 1) * P], c.ident[:, :])
                    m.then_inc(c.xT_ps.sem, c.xT_ps.one())
    if last:
        c.stored.issued += 32
    c.next_stage()


class Group:

    def __init__(self, products, copy, engine, needs=(), frees=0):
        self.products = products
        self.copy = copy
        self.engine = engine
        self.needs = needs
        self.frees = frees


def run_projections(c, groups, pe=None, act=None, dve=None, banks=(4, 5, 6, 7), owed=0):
    s = c.stream
    nb = len(banks)
    done = {"act": 0, "dve": 0}
    sigs = {"act": c.by_act, "dve": c.by_dve}
    freed = []
    for g, grp in enumerate(groups):
        bank = c.ps[:, banks[g % nb], :]
        if pe is not None:
            if g >= nb:
                eng, n = freed[g - nb]
                pe.wait_ge(sigs[eng].sem, sigs[eng].at(n))
            for pos in grp.needs:
                s.ready(pe, pos)
            for acc in grp.products(bank):
                for k, (o, lhsT, rhs) in enumerate(acc):
                    m = pe.matmul(o, lhsT, rhs, start=(k == 0), stop=(k == len(acc) - 1))
                    if owed and k == 0:
                        m.then_inc(s.used, owed)
                        owed = 0
            m.then_inc(c.proj_full.sem, c.proj_full.one())
            owed = grp.frees
        done[grp.engine] += 1
        freed.append((grp.engine, done[grp.engine]))
        if grp.engine == "act" and act is not None:
            act.wait_ge(c.proj_full.sem, c.proj_full.at(g + 1))
            grp.copy(act, bank).then_inc(c.by_act.sem, c.by_act.one())
        if grp.engine == "dve" and dve is not None:
            dve.wait_ge(c.proj_full.sem, c.proj_full.at(g + 1))
            grp.copy(dve, bank).then_inc(c.by_dve.sem, c.by_dve.one())
    return done, owed


def settle(c, pe, owed):
    if owed:
        pe.drain().then_inc(c.stream.used, owed)


def copier(dst, src):
    def copy(eng, bank):
        if eng.engine == mybir.EngineType.Activation:
            return eng.activation(dst, src(bank), ACT.Copy)
        return eng.tensor_copy(dst, src(bank))
    return copy


def feature_tiles(c, pos, cols, dst, engine, frees=0):
    def products(bank):
        return [[(bank[:, j * S:(j + 1) * S], cols(k, j), c.xT[:, k, :]) for k in range(KT)] for j in range(2)]
    return Group(products, copier(dst, lambda b: b.rearrange("p (j n) -> p j n", j=2)), engine, (pos,), frees)


class Unit:

    def __init__(self, q, k, nk, bias, values, extra=None, sink=None):
        self.q = q
        self.k = k
        self.nk = nk
        self.bias = bias
        self.values = values
        self.extra = extra
        self.sink = sink


def attention_stage(c, units, raw, nm, lsum, before=None):
    nc, ps, s = c.nc, c.ps, c.stream
    n = len(units)
    norm = c.norm[:, :, :].rearrange("p k n -> p (k n)")
    sb_s = [norm[:, i * 512:(i + 1) * 512] for i in range(3)]
    sb_pT = [norm[:, 1536:1920], c.take(384)]
    mx = [c.take(2) for _ in range(2)]

    def lay(u, v):
        return v[:, 0:2 * units[u].nk].rearrange("p (s k) -> p s k", s=2)

    def blocks(u):
        if units[u].nk == NC_CMP:
            return [(0, 0, 0), (1, 0, P)]
        return [(0, 0, 0), (0, P, P), (1, 0, 2 * P)]

    with nc.Block() as block:
        @block.tensor
        def _(pe):
            for step in range(n + 3):
                u = step
                if u < n:
                    un = units[u]
                    if u >= 2:
                        pe.wait_ge(c.s_ready.sem, c.s_ready.at(u - 1))
                    for slot in range(2):
                        t = 1 - slot
                        o = ps[:, u % 2, slot * un.nk:(slot + 1) * un.nk]
                        pairs = [(un.q(t), un.k)] + (un.extra(t) if un.extra else [])
                        for i, (lhsT, rhs) in enumerate(pairs):
                            m = pe.matmul(o, lhsT, rhs, start=(i == 0), stop=(i == len(pairs) - 1))
                    m.then_inc(c.sc_full.sem, c.sc_full.one())
                u = step - 2
                if 0 <= u < n:
                    pe.wait_ge(c.p_ready.sem, c.p_ready.at(u + 1))
                    if u >= 2:
                        pe.wait_ge(c.pt_ready.sem, c.pt_ready.at(u - 1))
                    nk = min(units[u].nk, P)
                    p = lay(u, sb_s[u % 3])
                    for slot, k0, col in blocks(u):
                        m = pe.transpose(ps[0:nk, 2 + u % 2, col:col + P], p[:, slot, k0:k0 + nk], c.ident[:, :])
                    m.then_inc(c.pt_ps.sem, c.pt_ps.one())
                u = step - 3
                if 0 <= u < n:
                    pe.wait_ge(c.pt_ready.sem, c.pt_ready.at(u + 1))
                    if u >= 2:
                        pe.wait_ge(c.o_raw.sem, c.o_raw.at(u - 1))
                    nk = min(units[u].nk, P)
                    seen = [0, 0]
                    for slot, k0, col in blocks(u):
                        last = seen[slot] + 1 == sum(1 for b in blocks(u) if b[0] == slot)
                        m = pe.matmul(ps[:, 4 + u % 2, slot * HD:(slot + 1) * HD], sb_pT[u % 2][0:nk, col:col + P],
                                      units[u].values[k0 // P], start=(seen[slot] == 0), stop=last)
                        seen[slot] += 1
                    m.then_inc(c.o_ps.sem, c.o_ps.one())

        @block.vector
        def _(dve):
            ch = c.dve_chain
            for step in range(n + 4):
                u = step
                if u < n:
                    un = units[u]
                    dve.wait_ge(c.sc_full.sem, c.sc_full.at(u + 1))
                    if u >= 3:
                        dve.wait_ge(c.pt_ps.sem, c.pt_ps.at(u - 2))
                    sv = lay(u, sb_s[u % 3])
                    ins = dve.scalar_tensor_tensor(sv, lay(u, ps[:, u % 2, :]), SCALE, un.bias, ALU.mult, ALU.add)
                    ins.then_inc(c.s_ready.sem, c.s_ready.one())
                    dve.wait_ge(c.s_ready.sem, c.s_ready.at(u + 1))
                    ch.link(dve, dve.tensor_reduce(mx[u % 2], sv, AX, ALU.max))
                    if un.sink is not None:
                        ins = dve.tensor_scalar(nm[:, u, :], mx[u % 2], -1.0, un.sink, ALU.mult, ALU.min)
                    else:
                        ins = dve.tensor_scalar(nm[:, u, :], mx[u % 2], -1.0, None, ALU.mult)
                    ins.then_inc(c.nm_ready.sem, c.nm_ready.one())
                u = step - 4
                if 0 <= u < n:
                    dve.wait_ge(c.o_ps.sem, c.o_ps.at(u + 1))
                    dve.tensor_copy(raw[:, u, :, :], ps[:, 4 + u % 2, 0:2 * HD].rearrange("p (s d) -> p s d", s=2)
                                    ).then_inc(c.o_raw.sem, c.o_raw.one())

        @block.scalar
        def _(act):
            for step in range(n + 2):
                u = step
                if u < n:
                    act.wait_ge(c.nm_ready.sem, c.nm_ready.at(u + 1))
                    sv = lay(u, sb_s[u % 3])
                    for slot in range(2):
                        ins = act.activation(sv[:, slot, :], sv[:, slot, :], ACT.Exp, bias=nm[:, u, slot:slot + 1],
                                             accum_out=lsum[:, u, slot:slot + 1])
                    ins.then_inc(c.p_ready.sem, c.p_ready.one())
                u = step - 2
                if 0 <= u < n:
                    act.wait_ge(c.pt_ps.sem, c.pt_ps.at(u + 1))
                    if u >= 2:
                        act.wait_ge(c.o_ps.sem, c.o_ps.at(u - 1))
                    nk = min(units[u].nk, P)
                    w = P * len(blocks(u))
                    act.activation(sb_pT[u % 2][0:nk, 0:w], ps[0:nk, 2 + u % 2, 0:w], ACT.Copy
                                   ).then_inc(c.pt_ready.sem, c.pt_ready.one())
    c.next_stage()


def transpose_mix(c, rows, outT, n):
    def tensor(pe):
        for g in range(n // 2):
            if g >= 4:
                pe.wait_ge(c.mixT.sem, c.mixT.at(g - 3))
            for f in range(2 * g, 2 * g + 2):
                for t in range(TT):
                    m = pe.transpose(c.ps[:, 4 + g % 4, (f % 2) * S + t * P:(f % 2) * S + (t + 1) * P],
                                     rows[:, 1 - t, f * P:(f + 1) * P], c.ident[:, :])
            m.then_inc(c.mixT_ps.sem, c.mixT_ps.one())

    def scalar(act):
        for g in range(n // 2):
            act.wait_ge(c.mixT_ps.sem, c.mixT_ps.at(g + 1))
            act.activation(outT[:, 2 * g:2 * g + 2, :], c.ps[:, 4 + g % 4, :].rearrange("p (f n) -> p f n", f=2),
                           ACT.Copy).then_inc(c.mixT.sem, c.mixT.one())
    return tensor, scalar


class MixPlan:

    def __init__(self, c, l):
        s, a = c.stream, c.a
        w = a["w_in"][l]

        def pair(c0, i):
            def part(g, h):
                lo, src = (2 * h + g) * HD, c0 + 256 * g + (2 * i + h) * HD
                return (lambda v: cols8(v)[:, :, lo:lo + HD]), w[:, src:src + HD].rearrange("(k p) n -> p k n", p=P)
            return s.add(*[part(g, h) for h in range(2) for g in range(2)])

        def straight(c0):
            return s.add(col_piece(w, c0))

        self.qa = [pair(0, i) for i in range(2)]
        self.cmp = straight(512)
        self.slc = straight(768)
        self.win = straight(1024)
        self.qb = [pair(1304, i) for i in range(2)]
        self.kvb = straight(1816)
        self.qc = [straight(2072 + CHUNK * i) for i in range(2)]
        self.kc = [straight(2584 + CHUNK * i) for i in range(2)]
        self.vc = [straight(3096 + CHUNK * i) for i in range(2)]
        self.gf = s.add(((lambda v: cols8(v)[:, :, 0:24]), w[:, 1280:1304].rearrange("(k p) n -> p k n", p=P)),
                        ((lambda v: cols8(v)[:, :, 24:32]), w[:, 3608:3616].rearrange("(k p) n -> p k n", p=P)))
        self.cw1 = [[s.add(col_piece(a[name][l][r * D:(r + 1) * D, :], 0)) for r in range(2)]
                    for name in ("cmp_k_w1", "cmp_v_w1")]
        self.cw2 = s.add(((lambda v: v[:, 0:P].rearrange("p (j n) -> p j n", j=2)), a["cmp_k_w2"][l].rearrange("(j p) n -> p j n", p=P)),
                         ((lambda v: v[:, P:2 * P].rearrange("p (j n) -> p j n", j=2)), a["cmp_v_w2"][l].rearrange("(j p) n -> p j n", p=P)))
        self.proj_end = len(s.loads)
        self.br = []
        self.gate = []
        for b, name in enumerate(("w_br_a", "w_br_b", "w_br_c")):
            self.br.append([s.add(row_piece(a[name][l], r * 2 * P)) for r in range(2)])
            self.gate.append([s.add(col_piece(a["w_gate"][l], b * D + CHUNK * i)) for i in range(4)])
        self.out = [s.add(row_piece(a["w_out"][l], r * 2 * P)) for r in range(4)]
        self.end = len(s.loads)


def mix_buffers(c):
    c.taken = 0
    b = {}
    b["qT"] = c.take(12 * S).rearrange("p (i n) -> p i n", i=12)
    b["kT"] = c.take(7 * S).rearrange("p (i n) -> p i n", i=7)
    b["v"] = c.take(3 * 2 * P).rearrange("p (v t n) -> p v t n", v=3, t=2)
    b["vc"] = c.take(2 * 512).rearrange("p (t n) -> p t n", t=2)
    b["z2"] = c.take(4 * P)
    b["gf"] = c.take(2 * 32).rearrange("p (t n) -> p t n", t=2)
    b["hidT"] = c.take(2 * 2 * 30).rearrange("p (v j n) -> p v j n", v=2, j=2)
    b["hb"] = c.take(4)
    b["kcT"] = c.take(15)
    b["vcmp"] = c.take(2 * HD).rearrange("p (g n) -> p g n", g=2)
    b["pe"] = c.take(32)
    b["bf"] = c.take(8)
    b["sinks"] = c.take(8)
    b["bgate"] = c.take(24)
    b["lf"] = c.take(16).rearrange("p (t n) -> p t n", t=2)
    b["lt"] = c.take(32).rearrange("p (k t n) -> p k t n", k=2, t=2)
    b["cT"] = c.take(2 * S).rearrange("p (k n) -> p k n", k=2)
    b["G"] = c.take(48).rearrange("p (s n) -> p s n", s=2)
    b["nm"] = c.take(2 * N_UNITS).rearrange("p (u s) -> p u s", s=2)
    b["lsum"] = c.take(2 * N_UNITS).rearrange("p (u s) -> p u s", s=2)
    b["es"] = c.take(16).rearrange("p (u s) -> p u s", s=2)
    b["raw"] = c.take(N_UNITS * 2 * HD).rearrange("p (u s d) -> p u s d", u=N_UNITS, s=2)
    return b


def mix_projection_stage(c, plan, b, l):
    nc, s, a = c.nc, c.stream, c.a

    def pair_tiles(pos, i0, last):
        def cols(k, j):
            return cols8(s.slot(pos))[:, k, j * P:(j + 1) * P]
        return feature_tiles(c, pos, cols, b["qT"][:, i0:i0 + 2, :], "act", 1)

    def straight_tiles(pos, dst):
        return feature_tiles(c, pos, lambda k, j: cols8(s.slot(pos))[:, k, j * P:(j + 1) * P], dst, "act", 1)

    def kv_tile(pos, ik, iv):
        w = cols8(s.slot(pos))
        keys = Group(lambda bank: [[(bank[:, 0:S], w[:, k, 0:P], c.xT[:, k, :]) for k in range(KT)]],
                     copier(b["kT"][:, ik, :], lambda bank: bank[:, 0:S]), "dve", (pos,), 0)
        vals = Group(lambda bank: [[(bank[:, t * P:(t + 1) * P], c.xT[:, k, t * P:(t + 1) * P], w[:, k, P:2 * P])
                                    for k in range(KT)] for t in range(TT)],
                     copier(b["v"][:, iv, :, :], lambda bank: bank[:, 0:S].rearrange("p (t n) -> p t n", t=2)), "dve", (), 1)
        return [keys, vals]

    def compress_input():
        w = cols8(s.slot(plan.cmp))
        return Group(lambda bank: [[(bank[64 * par:64 * par + 64, q * P:(q + 1) * P], w[:, k, q * HD:(q + 1) * HD],
                                     c.xT[:, k, par:S:2]) for k in range(KT)] for q in range(4) for par in range(2)],
                     copier(b["z2"], lambda bank: bank), "dve", (plan.cmp,), 1)

    def value_rows(pos, i):
        w = cols8(s.slot(pos))
        return Group(lambda bank: [[(bank[:, t * S:(t + 1) * S], c.xT[:, k, t * P:(t + 1) * P], w[:, k, :])
                                    for k in range(KT)] for t in range(TT)],
                     copier(b["vc"][:, :, i * CHUNK:(i + 1) * CHUNK], lambda bank: bank.rearrange("p (t n) -> p t n", t=2)),
                     "dve", (pos,), 1)

    wgf = cols8(s.slot(plan.gf))
    gf = Group(lambda bank: [[(bank[:, t * 32:(t + 1) * 32], c.xT[:, k, t * P:(t + 1) * P], wgf[:, k, 0:32])
                              for k in range(KT)] for t in range(TT)],
               copier(b["gf"], lambda bank: bank[:, 0:64].rearrange("p (t n) -> p t n", t=2)), "dve", (plan.gf,), 1)
    groups = ([pair_tiles(plan.qa[i], 2 * i, False) for i in range(2)] + [compress_input()]
              + kv_tile(plan.slc, 0, 0) + kv_tile(plan.win, 1, 1)
              + [pair_tiles(plan.qb[i], 4 + 2 * i, False) for i in range(2)] + kv_tile(plan.kvb, 2, 2)
              + [straight_tiles(plan.qc[i], b["qT"][:, 8 + 2 * i:10 + 2 * i, :]) for i in range(2)]
              + [straight_tiles(plan.kc[i], b["kT"][:, 3 + 2 * i:5 + 2 * i, :]) for i in range(2)]
              + [value_rows(plan.vc[i], i) for i in range(2)] + [gf])

    with nc.Block() as block:
        @block.sync
        def _(sp):
            s.issue(sp, plan.cw1[0][0] + AHEAD)

        @block.tensor
        def _(pe):
            _, owed = run_projections(c, groups, pe=pe)
            settle(c, pe, owed)

        @block.scalar
        def _(act):
            for dst, src in ((b["pe"], a["c_pe"][l]), (b["bf"], a["fox_b_f"][l].partition_broadcast(P)),
                             (b["sinks"], a["swa_sinks"][l].partition_broadcast(P)), (b["bgate"], a["c_bgate"][l])):
                act.dma_start(dst, src).then_inc(c.small.sem, 16)
            run_projections(c, groups, act=act)

        @block.vector
        def _(dve):
            run_projections(c, groups, dve=dve)
    c.small.issued += 64
    c.next_stage()


def mix_small_stage(c, plan, b):
    nc, s, ps = c.nc, c.stream, c.ps
    z2, hidT = b["z2"], b["hidT"]
    with nc.Block() as block:
        @block.sync
        def _(sp):
            s.issue(sp, plan.proj_end + AHEAD)

        @block.tensor
        def _(pe):
            pe.wait_ge(c.small.sem, c.small.at(0))
            for v in range(2):
                for r in range(2):
                    s.ready(pe, plan.cw1[v][r])
                for j in range(2):
                    def w1(m):
                        return cols8(s.slot(plan.cw1[v][m // 8]))[:, m % 8, j * P:(j + 1) * P]
                    for m in range(16):
                        pe.matmul(ps[:, 4 + v, j * 32:j * 32 + 30], w1(m), window(z2, v * 2 * P + m, [[P, 2], [8, NC_CMP]]),
                                  start=(m == 0), stop=(m == 15))
                    for m in range(16):
                        mm = pe.matmul(ps[:, 4 + v, j * 32 + 30:j * 32 + 31], w1(m), b["pe"][:, v * 16 + m:v * 16 + m + 1],
                                       start=(m == 0), stop=(m == 15))
                mm.then_inc(c.aux_pe.sem, c.aux_pe.one())
            pe.wait_ge(c.aux_dve.sem, c.aux_dve.at(3))
            for t in range(TT):
                mm = pe.matmul(ps[0:8, 6, 0:S], b["lf"][:, t, :], c.tri[:, t, :], start=(t == 0), stop=(t == 1))
                if t == 0:
                    mm.then_inc(s.used, 4)
            mm.then_inc(c.aux_pe.sem, c.aux_pe.one())
            s.ready(pe, plan.cw2)
            w2 = s.slot(plan.cw2).rearrange("p (v j n) -> p v j n", v=16, j=2)
            pe.wait_ge(c.aux_act.sem, c.aux_act.at(3))
            for g in range(2):
                for j in range(2):
                    pe.matmul(ps[64 * g:64 * g + 64, 7, 0:NC_CMP], w2[:, 0, j, :], hidT[:, 0, j, g * NC_CMP:(g + 1) * NC_CMP],
                              start=(j == 0), stop=(j == 1))
            for g in range(2):
                for j in range(2):
                    pe.matmul(ps[0:NC_CMP, 7, 64 + g * HD:64 + (g + 1) * HD], hidT[:, 1, j, g * NC_CMP:(g + 1) * NC_CMP],
                              w2[:, 1, j, :], start=(j == 0), stop=(j == 1))
            pe.drain().then_inc(c.aux_pe.sem, c.aux_pe.one())
            pe.drain().then_inc(s.used, 1)

        @block.scalar
        def _(act):
            ch = c.act_chain
            act.wait_ge(c.aux_dve.sem, c.aux_dve.at(1))
            ch.link(act, act.activation(b["lt"][:, 1, :, :], b["lt"][:, 1, :, :], ACT.Exp, scale=-1.0))
            act.activation(b["lt"][:, 1, :, :], b["lt"][:, 1, :, :], ACT.Ln, bias=c.ones[:, 0:1]).then_inc(c.aux_act.sem, c.aux_act.one())
            for v in range(2):
                act.wait_ge(c.aux_pe.sem, c.aux_pe.at(v + 1))
                for j in range(2):
                    ins = act.activation(b["hb"][:, 2 * v + j:2 * v + j + 1], ps[:, 4 + v, j * 32 + 30:j * 32 + 31], ACT.Copy)
                ch.link(act, ins)
                for j in range(2):
                    ins = act.activation(hidT[:, v, j, :], ps[:, 4 + v, j * 32:j * 32 + 30], ACT.Gelu_apprx_tanh,
                                         bias=b["hb"][:, 2 * v + j:2 * v + j + 1])
                ins.then_inc(c.aux_act.sem, c.aux_act.one())
            for t in range(TT):
                act.activation(b["G"][:, 1 - t, :], b["gf"][:, t, 0:24], ACT.Sigmoid)

        @block.vector
        def _(dve):
            ch = c.dve_chain
            dve.wait_ge(c.small.sem, c.small.at(0))
            for t in range(TT):
                ins = dve.tensor_tensor(b["lt"][:, 0, t, :], b["gf"][:, t, 24:32], b["bf"], ALU.add)
            ch.link(dve, ins)
            dve.scalar_tensor_tensor(b["lt"][:, 1, :, :], b["lt"][:, 0, :, :], -1.0, b["lt"][:, 0, :, :], ALU.mult, ALU.max).then_inc(c.aux_dve.sem, c.aux_dve.one())
            ch.link(dve, dve.tensor_scalar(b["sinks"], b["sinks"], -1.0, None, ALU.mult))
            dve.memset(c.tiny[:, 8:9], 0.0).then_inc(c.aux_dve.sem, c.aux_dve.one())
            dve.wait_ge(c.aux_act.sem, c.aux_act.at(1))
            dve.scalar_tensor_tensor(b["lf"], b["lt"][:, 0, :, :], 0.0, b["lt"][:, 1, :, :], ALU.min, ALU.subtract
                                     ).then_inc(c.aux_dve.sem, c.aux_dve.one())
            dve.wait_ge(c.aux_pe.sem, c.aux_pe.at(3))
            for k, sign in enumerate((1.0, -1.0)):
                dve.tensor_scalar(b["cT"][0:8, k, :], ps[0:8, 6, 0:S], sign / SCALE, None, ALU.mult)
            dve.wait_ge(c.aux_pe.sem, c.aux_pe.at(4))
            dve.tensor_copy(b["kcT"], ps[:, 7, 0:NC_CMP])
            dve.tensor_copy(b["vcmp"][0:NC_CMP, :, :], ps[0:NC_CMP, 7, 64:64 + 2 * HD].rearrange("p (g n) -> p g n", g=2))
    c.next_stage()


def mix_units(c, b):
    def bias(h):
        return window(c.E[:, :], h * 384, [[P, 2], [1, S]])

    units = []
    for branch in range(3):
        for h in range(8):
            g, i = h // 4, h % 4
            lo = 64 * g
            q = (lambda t, i=i, lo=lo: b["qT"][lo:lo + 64, i, t * P:(t + 1) * P])
            if branch < 2:
                units.append(Unit(q, b["kT"][lo:lo + 64, branch, :], S, bias(h),
                                  [b["v"][:, branch, t, g * HD:(g + 1) * HD] for t in range(TT)]))
            else:
                units.append(Unit(q, b["kcT"][lo:lo + 64, :], NC_CMP, window(c.E[:, :], h * 384 + 31, [[P, 2], [16, NC_CMP]]),
                                  [b["vcmp"][0:NC_CMP, g, :]]))
    for h in range(8):
        g, i = h // 4, h % 4
        lo = 64 * g
        q = (lambda t, i=i, lo=lo: b["qT"][lo:lo + 64, 4 + i, t * P:(t + 1) * P])
        units.append(Unit(q, b["kT"][lo:lo + 64, 2, :], S, bias(8 + h),
                          [b["v"][:, 2, t, g * HD:(g + 1) * HD] for t in range(TT)], sink=b["sinks"][:, h:h + 1]))
    for h in range(8):
        i, lo = h // 2, 64 * (h % 2)
        q = (lambda t, i=i, lo=lo: b["qT"][lo:lo + 64, 8 + i, t * P:(t + 1) * P])
        extra = (lambda t, h=h: [(b["cT"][0:8, 0, t * P:(t + 1) * P], c.ident[0:8, h:h + 1].to_broadcast([8, S])),
                                 (c.ident[0:8, h:h + 1].to_broadcast([8, P]), b["cT"][0:8, 1, :])])
        units.append(Unit(q, b["kT"][lo:lo + 64, 3 + i, :], S, bias(16),
                          [b["vc"][:, t, h * HD:(h + 1) * HD] for t in range(TT)], extra=extra))
    return units


def spread(v, n):
    return bass.AP(v.tensor, v.offset, list(v.ap) + [[0, n]])


def mix_combine_stage(c, b):
    nc = c.nc
    raw, nm, lsum, es, G = b["raw"], b["nm"], b["lsum"], b["es"], b["G"]
    rows = c.arena[:, 0:2 * 1536].rearrange("p (s n) -> p s n", s=2)
    outT_v = raw[:, 0:24, :, :].rearrange("p u s d -> p (u s d)").rearrange("p (f n) -> p f n", f=12)
    tensor, scalar = transpose_mix(c, rows, outT_v, 12)
    with nc.Block() as block:
        @block.vector
        def _(dve):
            ch = c.dve_chain
            dve.tensor_tensor(es, nm[:, 24:32, :], spread(b["sinks"], 2), ALU.subtract).then_inc(c.aux_dve.sem, c.aux_dve.one())
            dve.wait_ge(c.aux_act.sem, c.aux_act.at(1))
            ch.link(dve, dve.tensor_tensor(lsum[:, 24:32, :], lsum[:, 24:32, :], es, ALU.add))
            ch.link(dve, dve.tensor_scalar(lsum, lsum, 1e-30, None, ALU.max))
            ch.link(dve, dve.reciprocal(lsum, lsum))
            ch.link(dve, dve.tensor_scalar(lsum[:, 16:24, 1], lsum[:, 16:24, 1], c.tiny[:, 0:1], None, ALU.mult))
            for br, col in ((0, 1), (1, 2), (2, 0)):
                gv = bass.AP(G.tensor, G.offset + col, [G.ap[0], [3, 8], [24, 2]])
                ins = dve.tensor_tensor(lsum[:, 8 * br:8 * br + 8, :], lsum[:, 8 * br:8 * br + 8, :], gv, ALU.mult)
            ch.link(dve, ins)

            def head_rows(m):
                return rows[:, :, m * 512:(m + 1) * 512].rearrange("p s (h d) -> p h s d", h=8)

            def scaled(dst, u0):
                return dve.tensor_tensor(dst, raw[:, u0:u0 + 8, :, :], spread(lsum[:, u0:u0 + 8, :], HD), ALU.mult)
            scaled(head_rows(1), 24)
            scaled(head_rows(2), 32)
            scaled(head_rows(0), 0)
            scaled(raw[:, 8:16, :, :], 8)
            ch.link(dve, scaled(raw[:, 16:24, :, :], 16))
            ch.link(dve, dve.tensor_tensor(raw[:, 8:16, :, :], raw[:, 8:16, :, :], raw[:, 16:24, :, :], ALU.add))
            dve.tensor_tensor(head_rows(0), head_rows(0), raw[:, 8:16, :, :], ALU.add).then_inc(c.mix.sem, c.mix.one())

        @block.scalar
        def _(act):
            act.wait_ge(c.aux_dve.sem, c.aux_dve.at(1))
            act.activation(es, es, ACT.Exp).then_inc(c.aux_act.sem, c.aux_act.one())
            scalar(act)

        @block.tensor
        def _(pe):
            pe.wait_ge(c.mix.sem, c.mix.at(1))
            tensor(pe)
    c.next_stage()
    return outT_v


def mix_merge_stage(c, plan, b, outT, load_norm):
    nc, s, ps = c.nc, c.stream, c.ps
    mT = c.arena[:, 0:8 * S].rearrange("p (f n) -> p f n", f=8)
    sgm = [c.arena[:, (8 + i) * S:(9 + i) * S] for i in range(2)]
    tmps = [c.arena[:, (10 + i) * S:(11 + i) * S] for i in range(2)]
    with nc.Block() as block:
        @block.sync
        def _(sp):
            s.issue(sp, plan.end + AHEAD)

        @block.tensor
        def _(pe):
            for g in range(24):
                br, f = g // 8, g % 8
                bank = 4 + g % 4
                if g >= 4:
                    pe.wait_ge(c.merged.sem, c.merged.at(g - 3))
                if f == 0:
                    for pos in plan.br[br]:
                        s.ready(pe, pos)
                if f % 2 == 0:
                    s.ready(pe, plan.gate[br][f // 2])
                w = cols8(s.slot(plan.gate[br][f // 2]))
                for k in range(KT):
                    m = pe.matmul(ps[:, bank, 0:S], w[:, k, (f % 2) * P:(f % 2 + 1) * P], c.xT[:, k, :],
                                  start=(k == 0), stop=(k == KT - 1))
                    if k == 0 and f == 0 and br > 0:
                        m.then_inc(s.used, 6)
                for k in range(4):
                    w = rows2(s.slot(plan.br[br][k // 2]))
                    m = pe.matmul(ps[:, bank, S:2 * S], w[:, k % 2, f * P:(f + 1) * P], outT[:, 4 * br + k, :],
                                  start=(k == 0), stop=(k == 3))
                m.then_inc(c.proj_full.sem, c.proj_full.one())
            pe.wait_ge(c.merged.sem, c.merged.at(24))
            for r in range(4):
                s.ready(pe, plan.out[r])
                w = rows2(s.slot(plan.out[r]))
                for kk in range(2):
                    for t in range(TT):
                        for half in range(2):
                            k = 2 * r + kk
                            m = pe.matmul(ps[:, 2 * t + half, :], mT[:, k, t * P:(t + 1) * P],
                                          w[:, kk, half * 512:(half + 1) * 512], start=(k == 0), stop=(k == 7))
                            if k == 0 and t == 0 and half == 0:
                                m.then_inc(s.used, 6)
                m.then_inc(s.used, 1)

        @block.scalar
        def _(act):
            load_norm(act)
            for g in range(24):
                act.wait_ge(c.proj_full.sem, c.proj_full.at(g + 1))
                if g >= 2:
                    act.wait_ge(c.merged.sem, c.merged.at(g - 1))
                act.activation(sgm[g % 2], ps[:, 4 + g % 4, 0:S], ACT.Sigmoid, bias=b["bgate"][:, g:g + 1]
                               ).then_inc(c.gate_act.sem, c.gate_act.one())

        @block.vector
        def _(dve):
            ch = c.dve_chain
            for g in range(24):
                br, f = g // 8, g % 8
                dve.wait_ge(c.gate_act.sem, c.gate_act.at(g + 1))
                out = ps[:, 4 + g % 4, S:2 * S]
                if br == 0:
                    dve.tensor_tensor(mT[:, f, :], out, sgm[g % 2], ALU.mult).then_inc(c.merged.sem, c.merged.one())
                else:
                    tmp = tmps[g % 2]
                    dve.wait_ge(c.merged.sem, c.merged.at(g - 1))
                    ch.link(dve, dve.tensor_tensor(tmp, out, sgm[g % 2], ALU.mult))
                    dve.tensor_tensor(mT[:, f, :], mT[:, f, :], tmp, ALU.add).then_inc(c.merged.sem, c.merged.one())
    c.next_stage()


def token_mix(c, plan, l, load_norm):
    b = mix_buffers(c)
    mix_projection_stage(c, plan, b, l)
    mix_small_stage(c, plan, b)
    attention_stage(c, mix_units(c, b), b["raw"], b["nm"], b["lsum"])
    outT = mix_combine_stage(c, b)
    mix_merge_stage(c, plan, b, outT, load_norm)


class SsdPlan:
    def __init__(self, c):
        s, a = c.stream, c.a
        w = a["ssd_w_in_2"][0]
        self.z = [s.add(col_piece(w, CHUNK * i)) for i in range(8)]
        self.xbc = [s.add(col_piece(w, 2048 + CHUNK * i)) for i in range(12)]
        self.dt = s.add(col_piece(w, 5120, 32))
        self.proj_end = len(s.loads)
        self.out = [s.add(row_piece(a["ssd_w_out_2"][0], r * 2 * P)) for r in range(8)]
        self.end = len(s.loads)


def ssd_mixer(c, plan, load_norm):
    nc, s, ps, a = c.nc, c.stream, c.ps, c.a
    c.taken = 0
    c.etaken = 0
    NH, PG = 32, 4
    zT = c.take(16 * S).rearrange("p (i n) -> p i n", i=16)
    xbc = c.take(24 * S).rearrange("p (i n) -> p i n", i=24)
    conv = [c.take(S) for _ in range(2)]
    dt = c.take(64).rearrange("p (t n) -> p t n", t=2)
    da = c.take(64).rearrange("p (t n) -> p t n", t=2)
    dt1 = c.take(64).rearrange("p (t n) -> p t n", t=2)
    ncs = c.take(64).rearrange("p (t n) -> p t n", t=2)
    csT = c.take(S)
    dtb = c.take(32)
    alog = c.take(32)
    cols = c.take(6 * 24 + 32)
    diff = [c.take(384) for _ in range(2)]
    dec = [c.take(384) for _ in range(2)]
    rstd = c.take(S)
    xr = c.etake(2 * 2048).rearrange("p (t n) -> p t n", t=2)
    cb = c.etake(4 * 384).rearrange("p (g n) -> p g n", g=4)
    conv_w = cols[:, 0:96].rearrange("p (i k) -> p i k", i=24)
    conv_b = cols[:, 96:120]
    norm_w = cols[:, 120:136]
    dskip = cols[:, 136:152]

    def z_group(i):
        w = cols8(s.slot(plan.z[i]))

        def copy(eng, bank):
            return eng.activation(zT[:, 2 * i:2 * i + 2, :], bank.rearrange("p (j n) -> p j n", j=2), ACT.Silu)
        return Group(lambda bank: [[(bank[:, j * S:(j + 1) * S], w[:, k, j * P:(j + 1) * P], c.xT[:, k, :])
                                    for k in range(KT)] for j in range(2)], copy, "act", (plan.z[i],), 1)

    with nc.Block() as block:
        @block.sync
        def _(sp):
            for dst, src in ((cols[:, 0:152], a["c_ssd"]), (dtb, a["ssd_dt_bias_2"][0].partition_broadcast(P)),
                             (alog, a["ssd_a_log_2"][0].partition_broadcast(P))):
                sp.dma_start(dst, src).then_inc(c.small.sem, 16)
            s.issue(sp, plan.proj_end + AHEAD)

        @block.tensor
        def _(pe):
            owed = 0
            for g in range(8 + 24):
                is_z = g < 8
                bank = 4 + g % 4
                if g >= 4:
                    if g - 4 < 8:
                        pe.wait_ge(c.by_act.sem, c.by_act.at(g - 3))
                    else:
                        pe.wait_ge(c.by_dve.sem, c.by_dve.at(g - 4 - 8 + 1))
                if is_z:
                    s.ready(pe, plan.z[g])
                    w = cols8(s.slot(plan.z[g]))
                    tiles = [(ps[:, bank, j * S:(j + 1) * S], j) for j in range(2)]
                    free = 1
                else:
                    i = g - 8
                    if i % 2 == 0:
                        s.ready(pe, plan.xbc[i // 2])
                    w = cols8(s.slot(plan.xbc[i // 2]))
                    tiles = [(ps[:, bank, 0:S], i % 2)]
                    free = i % 2
                for o, j in tiles:
                    for k in range(KT):
                        m = pe.matmul(o, w[:, k, j * P:(j + 1) * P], c.xT[:, k, :], start=(k == 0), stop=(k == KT - 1))
                        if owed and k == 0:
                            m.then_inc(s.used, owed)
                            owed = 0
                m.then_inc(c.proj_full.sem, c.proj_full.one())
                owed = free
            pe.wait_ge(c.by_dve.sem, c.by_dve.at(21))
            s.ready(pe, plan.dt)
            w = cols8(s.slot(plan.dt))
            for t in range(TT):
                for k in range(KT):
                    m = pe.matmul(ps[:, 4, t * 32:(t + 1) * 32], c.xT[:, k, t * P:(t + 1) * P], w[:, k, 0:32],
                                  start=(k == 0), stop=(k == KT - 1))
                    if owed and k == 0:
                        m.then_inc(s.used, owed)
                        owed = 0
            m.then_inc(c.proj_full.sem, c.proj_full.one())
            settle(c, pe, 1)

        @block.scalar
        def _(act):
            for g in range(8):
                act.wait_ge(c.proj_full.sem, c.proj_full.at(g + 1))
                act.activation(zT[:, 2 * g:2 * g + 2, :], ps[:, 4 + g % 4, :].rearrange("p (j n) -> p j n", j=2),
                               ACT.Silu).then_inc(c.by_act.sem, c.by_act.one())
            for i in range(24):
                act.wait_ge(c.by_dve.sem, c.by_dve.at(i + 1))
                act.activation(xbc[:, i, :], conv[i % 2], ACT.Silu).then_inc(c.aux_act.sem, c.aux_act.one())

        @block.vector
        def _(dve):
            ch = c.dve_chain
            dve.wait_ge(c.small.sem, c.small.at(48))
            for i in range(24):
                dve.wait_ge(c.proj_full.sem, c.proj_full.at(8 + i + 1))
                if i >= 2:
                    dve.wait_ge(c.aux_act.sem, c.aux_act.at(i - 1))
                u, y = ps[:, 4 + i % 4, 0:S], conv[i % 2]
                ch.link(dve, dve.tensor_scalar(y, u, conv_w[:, i, 3:4], conv_b[:, i:i + 1], ALU.mult, ALU.add))
                for k in (2, 1, 0):
                    d = 3 - k
                    ins = dve.scalar_tensor_tensor(y[:, d:S], u[:, 0:S - d], conv_w[:, i, k:k + 1], y[:, d:S], ALU.mult, ALU.add)
                    if k:
                        ch.link(dve, ins)
                ins.then_inc(c.by_dve.sem, c.by_dve.one())
            dve.wait_ge(c.proj_full.sem, c.proj_full.at(33))
            v = ps[:, 4, 0:64].rearrange("p (t n) -> p t n", t=2)
            dve.tensor_tensor(dt, v, bass.AP(dtb.tensor, dtb.offset, [dtb.ap[0], [0, 2], [1, 32]]), ALU.add)
    c.small.issued += 48
    c.next_stage()

    with nc.Block() as block:
        @block.scalar
        def _(act):
            ch = c.act_chain
            act.wait_ge(c.aux_dve.sem, c.aux_dve.at(1))
            ch.link(act, act.activation(dt1, dt1, ACT.Exp, scale=-1.0))
            act.activation(alog, alog, ACT.Exp).then_inc(c.aux_act.sem, c.aux_act.one())
            act.activation(dt1, dt1, ACT.Ln, bias=c.ones[:, 0:1]).then_inc(c.aux_act.sem, c.aux_act.one())

        @block.vector
        def _(dve):
            ch = c.dve_chain
            dve.scalar_tensor_tensor(dt1, dt, -1.0, dt, ALU.mult, ALU.max).then_inc(c.aux_dve.sem, c.aux_dve.one())
            dve.wait_ge(c.aux_act.sem, c.aux_act.at(2))
            ch.link(dve, dve.scalar_tensor_tensor(dt, dt, 0.0, dt1, ALU.max, ALU.add))
            dve.scalar_tensor_tensor(da, dt, -1.0, bass.AP(alog.tensor, alog.offset, [alog.ap[0], [0, 2], [1, 32]]),
                                     ALU.mult, ALU.mult).then_inc(c.aux_dve.sem, c.aux_dve.one())
            for q in range(8):
                t, f = q % 2, q // 2
                dve.wait_ge(c.mixT_ps.sem, c.mixT_ps.at(q + 1))
                dve.tensor_tensor(xr[:, t, f * 512:(f + 1) * 512].rearrange("p (h d) -> p h d", h=8),
                                  ps[:, q % 4, :].rearrange("p (h d) -> p h d", h=8),
                                  spread(dt[:, t, 8 * f:8 * f + 8], HD), ALU.mult).then_inc(c.mixT.sem, c.mixT.one())
            for g in range(PG):
                dve.wait_ge(c.aux_pe.sem, c.aux_pe.at(g + 1))
                dve.tensor_tensor(cb[:, g, 0:S], ps[:, 4 + g % 4, 0:S], c.tri[:, 0, :], ALU.mult)
                dve.tensor_tensor(cb[:, g, S:384], ps[:, 4 + g % 4, S:384], c.tri[:, 1, P:S], ALU.mult).then_inc(c.by_dve.sem, c.by_dve.one())
            dve.wait_ge(c.aux_pe.sem, c.aux_pe.at(5))
            for t in range(TT):
                dve.tensor_scalar(ncs[:, t, :], ps[:, 4, 64 * t:64 * t + 32], -1.0, None, ALU.mult)
            dve.tensor_copy(csT[0:32, :], ps[0:32, 5, 0:S])

        @block.tensor
        def _(pe):
            for q in range(8):
                t, f = q % 2, q // 2
                if q >= 4:
                    pe.wait_ge(c.mixT.sem, c.mixT.at(q - 3))
                for i in range(4):
                    m = pe.transpose(ps[:, q % 4, i * P:(i + 1) * P], xbc[:, 4 * f + i, t * P:(t + 1) * P], c.ident[:, :])
                m.then_inc(c.mixT_ps.sem, c.mixT_ps.one())
            for g in range(PG):
                pe.matmul(ps[:, 4 + g, 0:S], xbc[:, 16 + g, 0:P], xbc[:, 20 + g, :], start=True, stop=True)
                pe.matmul(ps[:, 4 + g, S:384], xbc[:, 16 + g, P:S], xbc[:, 20 + g, P:S], start=True, stop=True
                          ).then_inc(c.aux_pe.sem, c.aux_pe.one())
            pe.wait_ge(c.aux_dve.sem, c.aux_dve.at(2))
            pe.wait_ge(c.by_dve.sem, c.by_dve.at(2))
            for t in range(TT):
                for u in range(TT):
                    pe.matmul(ps[:, 4, 64 * t:64 * t + 32], c.tri[:, u, t * P:(t + 1) * P], da[:, u, :], start=(u == 0), stop=(u == 1))
            for u in range(TT):
                m = pe.matmul(ps[0:32, 5, 0:S], da[:, u, :], c.tri[:, u, :], start=(u == 0), stop=(u == 1))
            m.then_inc(c.aux_pe.sem, c.aux_pe.one())
    c.next_stage()

    with nc.Block() as block:
        @block.tensor
        def _(pe):
            for step in range(NH + 2):
                h = step
                if h < NH:
                    if h >= 2:
                        pe.wait_ge(c.s_ready.sem, c.s_ready.at(h - 1))
                    pe.matmul(ps[:, h % 2, 0:S], c.ident[0:32, h:h + 1].to_broadcast([32, P]), csT[0:32, :],
                              start=True, stop=True).then_inc(c.sc_full.sem, c.sc_full.one())
                h = step - 2
                if h >= 0:
                    i, lo = h // 2, 64 * (h % 2)
                    if h % 2 == 0 and i >= 2:
                        pe.wait_ge(c.o_raw.sem, c.o_raw.at(i - 1))
                    pe.wait_ge(c.p_ready.sem, c.p_ready.at(h + 1))
                    pe.matmul(ps[lo:lo + 64, 2 + i % 2, 0:S], xr[:, 0, h * HD:(h + 1) * HD], diff[h % 2][:, 0:S], start=True, stop=False)
                    pe.matmul(ps[lo:lo + 64, 2 + i % 2, P:S], xr[:, 1, h * HD:(h + 1) * HD], diff[h % 2][:, S:384],
                              start=False, stop=True).then_inc(c.o_ps.sem, c.o_ps.one())

        @block.vector
        def _(dve):
            ch = c.dve_chain
            for step in range(NH + 3):
                h = step
                if h < NH:
                    dve.wait_ge(c.sc_full.sem, c.sc_full.at(h + 1))
                    if h >= 2:
                        dve.wait_ge(c.o_ps.sem, c.o_ps.at(h - 1))
                    dve.tensor_scalar(diff[h % 2][:, 0:S], ps[:, h % 2, 0:S], ncs[:, 0, h:h + 1], 0.0, ALU.add, ALU.min)
                    dve.tensor_scalar(diff[h % 2][:, S:384], ps[:, h % 2, P:S], ncs[:, 1, h:h + 1], 0.0, ALU.add, ALU.min
                                      ).then_inc(c.s_ready.sem, c.s_ready.one())
                h = step - 1
                if 0 <= h < NH:
                    dve.wait_ge(c.pt_ready.sem, c.pt_ready.at(h + 1))
                    dve.tensor_tensor(diff[h % 2], dec[h % 2], cb[:, h // 8, :], ALU.mult).then_inc(c.p_ready.sem, c.p_ready.one())
                h = step - 3
                if h >= 0 and h % 2 == 1:
                    i = h // 2
                    dve.wait_ge(c.o_ps.sem, c.o_ps.at(h + 1))
                    ins = dve.scalar_tensor_tensor(xbc[:, i, :], xbc[:, i, :], dskip[:, i:i + 1], ps[:, 2 + i % 2, 0:S], ALU.mult, ALU.add)
                    ins.then_inc(c.o_raw.sem, c.o_raw.one())
                    dve.wait_ge(c.o_raw.sem, c.o_raw.at(i + 1))
                    dve.tensor_tensor(zT[:, i, :], zT[:, i, :], xbc[:, i, :], ALU.mult)

        @block.scalar
        def _(act):
            for h in range(NH):
                act.wait_ge(c.s_ready.sem, c.s_ready.at(h + 1))
                if h >= 2:
                    act.wait_ge(c.p_ready.sem, c.p_ready.at(h - 1))
                act.activation(dec[h % 2], diff[h % 2], ACT.Exp).then_inc(c.pt_ready.sem, c.pt_ready.one())
    c.next_stage()

    with nc.Block() as block:
        @block.sync
        def _(sp):
            s.issue(sp, plan.end + AHEAD)

        @block.scalar
        def _(act):
            load_norm(act)
            for i in range(16):
                act.activation(xbc[:, i, :], zT[:, i, :], ACT.Square).then_inc(c.aux_act.sem, c.aux_act.one())
            for g in range(PG):
                act.wait_ge(c.stat.sem, c.stat.at(g + 1))
                act.activation(diff[0][:, 0:S], diff[1][:, 0:S], ACT.Sqrt).then_inc(c.std.sem, c.std.one())

        @block.tensor
        def _(pe):
            for g in range(PG):
                for i in range(4):
                    pe.wait_ge(c.aux_act.sem, c.aux_act.at(4 * g + i + 1))
                    m = pe.matmul(ps[:, 4 + g, 0:S], c.ones[:, :], xbc[:, 4 * g + i, :], start=(i == 0), stop=(i == 3))
                m.then_inc(c.aux_pe.sem, c.aux_pe.one())
            for r in range(8):
                pe.wait_ge(c.mix.sem, c.mix.at(r // 2 + 1))
                s.ready(pe, plan.out[r])
                w = rows2(s.slot(plan.out[r]))
                for kk in range(2):
                    k = 2 * r + kk
                    for t in range(TT):
                        for half in range(2):
                            m = pe.matmul(ps[:, 2 * t + half, :], zT[:, k, t * P:(t + 1) * P],
                                          w[:, kk, half * 512:(half + 1) * 512], start=(k == 0), stop=(k == 15))
                m.then_inc(s.used, 1)

        @block.vector
        def _(dve):
            ch = c.dve_chain
            for g in range(PG):
                dve.wait_ge(c.aux_pe.sem, c.aux_pe.at(g + 1))
                if g:
                    dve.wait_ge(c.std.sem, c.std.at(g))
                dve.tensor_scalar(diff[1][:, 0:S], ps[:, 4 + g, 0:S], 1.0 / 512, 1e-5, ALU.mult, ALU.add).then_inc(c.stat.sem, c.stat.one())
                dve.wait_ge(c.std.sem, c.std.at(g + 1))
                ch.link(dve, dve.reciprocal(rstd, diff[0][:, 0:S]))
                for i in range(4):
                    k = 4 * g + i
                    ins = dve.scalar_tensor_tensor(zT[:, k, :], zT[:, k, :], norm_w[:, k:k + 1], rstd, ALU.mult, ALU.mult)
                ins.then_inc(c.mix.sem, c.mix.one())
    c.next_stage()


class MoePlan:
    def __init__(self, c, l):
        s, a = c.stream, c.a
        self.router = s.add(((lambda v: cols8(v)[:, :, 0:4]), a["moe_w_router_group_2"][l].rearrange("(k p) n -> p k n", p=P)),
                            ((lambda v: cols8(v)[:, :, 4:36]), a["moe_w_router_expert_2"][l].rearrange("(k p) n -> p k n", p=P)))
        self.router_end = len(s.loads)
        wg, wu, wd = a["moe_w_gate_2"][l], a["moe_w_up_2"][l], a["moe_w_down_2"][l]

        def source(q, i):
            e, half = (i * 2 + q // 4, q % 4 // 2) if q < 8 else (i * 2 + (q - 8) // 2, q % 2)
            rows = slice(half * CHUNK, (half + 1) * CHUNK)
            if q < 8:
                return cols8, (wg, wu)[q % 2][bass.ds(e, 1), :, rows].rearrange("o (k p) n -> p (o k) n", p=P)
            return rows2, wd[bass.ds(e, 1), rows, :].rearrange("o (k p) n -> p (o k) n", p=P)
        self.mlp = Mlp(c, 2 * EXPERTS, source)
        self.end = len(s.loads)


def router_stage(c, plan, l):
    nc, s, ps, a = c.nc, c.stream, c.ps, c.a
    c.taken = EXPERTS * S
    slots = c.take(2 * (EXPERTS + 2)).rearrange("p (t n) -> p t n", t=2)
    iota = c.take(SLOTS + 1)
    kept = c.taken
    mask = c.take(64).rearrange("p (t n) -> p t n", t=2)
    most = c.take(4)
    sT = c.take(S)
    lg = c.take(2 * 36).rearrange("p (t n) -> p t n", t=2)
    bias = c.take(36)
    first = c.take(36)
    eg = c.take(8).rearrange("p (t n) -> p t n", t=2)
    e32 = c.take(64).rearrange("p (t n) -> p t n", t=2)
    o1 = c.take(64).rearrange("p (t n) -> p t n", t=2)
    o2 = c.take(64).rearrange("p (t n) -> p t n", t=2)
    w32 = c.take(64).rearrange("p (t n) -> p t n", t=2)
    sc = c.take(32).rearrange("p (k t) -> p k t", t=2)
    gT = c.take(S)

    def over(v, t_step, n):
        return bass.AP(v.tensor, v.offset, [v.ap[0], [t_step, 2], [0, n]])

    with nc.Block() as block:
        @block.sync
        def _(sp):
            sp.dma_start(bias[:, 0:4], a["moe_b_router_group_2"][l].partition_broadcast(P)).then_inc(c.small.sem, 16)
            sp.dma_start(bias[:, 4:36], a["moe_b_router_expert_2"][l].partition_broadcast(P)).then_inc(c.small.sem, 16)
            sp.dma_start(first, a["c_first"]).then_inc(c.small.sem, 16)
            sp.dma_start(iota, a["c_iota"]).then_inc(c.small.sem, 16)
            s.issue(sp, plan.router_end + AHEAD)
            sp.wait_ge(c.aux_dve.sem, c.aux_dve.at(7))
            sp.dma_start(c.gates_dram[l], gT[0:32, :]).then_inc(c.stored.sem, 16)
            sp.dma_start(c.slots_dram[l], sT[0:32, :]).then_inc(c.stored.sem, 16)
            sp.wait_ge(c.stored.sem, c.stored.at(32))

        @block.tensor
        def _(pe):
            s.ready(pe, plan.router)
            w = cols8(s.slot(plan.router))
            for t in range(TT):
                for k in range(KT):
                    m = pe.matmul(ps[:, 4, t * 64:t * 64 + 36], c.xT[:, k, t * P:(t + 1) * P], w[:, k, 0:36],
                                  start=(k == 0), stop=(k == KT - 1))
            m.then_inc(c.aux_pe.sem, c.aux_pe.one())
            settle(c, pe, 1)
            pe.wait_ge(c.aux_dve.sem, c.aux_dve.at(2))
            for t in range(TT):
                for u in range(TT):
                    m = pe.matmul(ps[:, 6, t * 64:t * 64 + 32], c.tri[:, u, t * P:(t + 1) * P], mask[:, u, :],
                                  start=(u == 0), stop=(u == 1))
            m.then_inc(c.aux_pe.sem, c.aux_pe.one())
            pe.wait_ge(c.aux_dve.sem, c.aux_dve.at(5))
            for t in range(TT):
                pe.transpose(ps[0:32, 5, t * P:(t + 1) * P], w32[:, t, :], c.ident[:, :])
                pe.transpose(ps[0:32, 5, S + t * P:S + (t + 1) * P], slots[:, t, 0:32], c.ident[:, :])
            pe.transpose(ps[0:1, 7, 0:P], most[:, 0:1], c.ident[:, :]).then_inc(c.aux_pe.sem, c.aux_pe.one())

        @block.scalar
        def _(act):
            act.wait_ge(c.aux_dve.sem, c.aux_dve.at(1))
            act.activation(eg, eg, ACT.Exp).then_inc(c.aux_act.sem, c.aux_act.one())
            act.wait_ge(c.aux_dve.sem, c.aux_dve.at(3))
            act.activation(sc[:, 5, :], sc[:, 5, :], ACT.Exp).then_inc(c.aux_act.sem, c.aux_act.one())

        @block.vector
        def _(dve):
            ch = c.dve_chain

            def do(ins):
                ch.link(dve, ins)

            def first_of_largest(onehot, v, idx, n):
                do(dve.tensor_reduce(sc[:, 0, :], v, AX, ALU.max))
                do(dve.tensor_tensor(onehot, v, over(sc[:, 0, :], 1, n), ALU.is_equal))
                do(dve.tensor_tensor(onehot, onehot, bass.AP(idx.tensor, idx.offset, [idx.ap[0], [0, 2], [1, n]]), ALU.mult))
                do(dve.tensor_reduce(sc[:, 1, :], onehot, AX, ALU.max))
                do(dve.tensor_tensor(onehot, onehot, over(sc[:, 1, :], 1, n), ALU.is_equal))

            dve.wait_ge(c.small.sem, c.small.at(64))
            dve.wait_ge(c.aux_pe.sem, c.aux_pe.at(1))
            do(dve.tensor_tensor(lg, ps[:, 4, 0:128].rearrange("p (t n) -> p t n", t=2)[:, :, 0:36],
                                 bass.AP(bias.tensor, bias.offset, [bias.ap[0], [0, 2], [1, 36]]), ALU.add))
            og = o1[:, :, 0:4]
            first_of_largest(og, lg[:, :, 0:4], first[:, 0:4], 4)
            dve.tensor_tensor(eg, lg[:, :, 0:4], over(sc[:, 0, :], 1, 4), ALU.subtract).then_inc(c.aux_dve.sem, c.aux_dve.one())
            do(dve.tensor_scalar(og, og, 1.0, -NEG, ALU.subtract, ALU.mult))
            for t in range(TT):
                ins = dve.tensor_tensor(e32[:, t, :].rearrange("p (g n) -> p g n", g=4), lg[:, t, 4:36].rearrange("p (g n) -> p g n", g=4),
                                        spread(o1[:, t, 0:4], 8), ALU.add)
            do(ins)
            dve.wait_ge(c.aux_act.sem, c.aux_act.at(1))
            do(dve.tensor_reduce(sc[:, 2, :], eg, AX, ALU.add))
            first_of_largest(o1, e32, first[:, 4:36], 32)
            do(dve.tensor_copy(sc[:, 3, :], sc[:, 0, :]))
            do(dve.scalar_tensor_tensor(e32, o1, 3 * NEG, e32, ALU.mult, ALU.add))
            first_of_largest(o2, e32, first[:, 4:36], 32)
            dve.tensor_tensor(mask, o1, o2, ALU.add).then_inc(c.aux_dve.sem, c.aux_dve.one())
            dve.tensor_tensor(sc[:, 5, :], sc[:, 0, :], sc[:, 3, :], ALU.subtract).then_inc(c.aux_dve.sem, c.aux_dve.one())
            dve.wait_ge(c.aux_act.sem, c.aux_act.at(2))
            do(dve.scalar_tensor_tensor(sc[:, 6, :], sc[:, 5, :], 1.0, sc[:, 2, :], ALU.add, ALU.mult))
            do(dve.reciprocal(sc[:, 6, :], sc[:, 6, :]))
            do(dve.tensor_tensor(o2, o2, over(sc[:, 5, :], 1, 32), ALU.mult))
            do(dve.tensor_tensor(o1, o1, o2, ALU.add))
            dve.tensor_tensor(w32, o1, over(sc[:, 6, :], 1, 32), ALU.mult).then_inc(c.aux_dve.sem, c.aux_dve.one())
            dve.wait_ge(c.aux_pe.sem, c.aux_pe.at(2))
            dve.memset(slots[:, :, 32:34], -1.0)
            cnt = ps[:, 6, 0:P].rearrange("p (t n) -> p t n", t=2)[:, :, 0:32]
            do(dve.tensor_tensor(slots[:, :, 0:32], cnt, mask, ALU.mult))
            do(dve.tensor_scalar(slots[:, :, 0:32], slots[:, :, 0:32], 1.0, None, ALU.subtract))
            dve.tensor_reduce(most[:, 0:1], slots[:, :, 0:32], mybir.AxisListType.XY, ALU.max).then_inc(c.aux_dve.sem, c.aux_dve.one())
            dve.wait_ge(c.aux_pe.sem, c.aux_pe.at(3))
            do(dve.tensor_copy(gT[0:32, :], ps[0:32, 5, 0:S]))
            do(dve.tensor_reduce(most[0:1, 2:3], ps[0:1, 7, 0:P], AX, ALU.max))
            dve.tensor_copy(sT[0:32, :], ps[0:32, 5, S:2 * S]).then_inc(c.aux_dve.sem, c.aux_dve.one())
            dve.tensor_scalar(c.over[0:1, 0:1], most[0:1, 2:3], float(SLOTS), None, ALU.is_ge).then_inc(c.aux_dve.sem, c.aux_dve.one())
    c.small.issued += 64
    c.stored.issued += 32
    c.next_stage()
    c.taken = kept
    return slots, iota


def experts_stage(c, mlp, l, load_norm, slots, iota):
    nc, ps, s = c.nc, c.ps, c.stream
    p0 = mlp.pos
    landed0 = [s.value[p0 + q] for q in range(RING)]
    start = c.taken
    TURNS = EXPERTS // 2
    assert mlp.loops == TURNS and mlp.tail == 0
    over_max = 1

    slots_sp = c.arena[:, 0:TURNS * S]
    gates_sp = c.arena[:, TURNS * S:2 * TURNS * S]
    xe = [c.take(KT * SLOTS).rearrange("p (k n) -> p k n", k=KT) for _ in range(2)]
    y = c.take(D)
    chosen = [c.take(2 * SLOTS).rearrange("p (t n) -> p t n", t=2) for _ in range(2)]
    back = c.take(S)
    h = [c.take(4 * SLOTS).rearrange("p (j n) -> p j n", j=4) for _ in range(2)]
    sgp = [c.take(4 * SLOTS) for _ in range(2)]
    c.taken = start
    gates_all = c.arena[:, 0:EXPERTS * S]
    hid = [c.take(2 * S).rearrange("p (k n) -> p k n", k=2) for _ in range(BODY)]
    sg = [c.take(S) for _ in range(2)]
    upg = [c.take(S) for _ in range(2)]
    K, DN = c.packed[l], c.dense[l]

    def branch(eng, packed, dense):
        overrun = eng.value_load(c.over[0:1, 0:1], min_val=0, max_val=over_max)
        with eng.If(overrun == 0):
            packed()
        with eng.Else():
            dense()

    def open_accumulators(pe):
        for b in range(4):
            z = pe.matmul(ps[:, b, :], c.zeros[0:1, 0:P], c.zeros[0:1, :], start=True, stop=False)
            if b == 0 and mlp.pad:
                z.then_inc(s.used, mlp.pad)

    def close_accumulators(pe):
        for b in range(4):
            z = pe.matmul(ps[:, b, 0:1], c.zeros[0:1, 0:P], c.zeros[0:1, 0:1], start=False, stop=True)
        return z

    with nc.Block() as block:
        @block.sync
        def _(sp):
            issue_mlp(s, sp, mlp)

        @block.tensor
        def _(pe):
            def packed():
                def gather(e, count):
                    pe.wait_ge(K.chosen[e], count)
                    for k in range(KT):
                        for t in range(TT):
                            m = pe.matmul(ps[:, 4 + e, k * SLOTS:(k + 1) * SLOTS], c.x[:, t, k * P:(k + 1) * P],
                                          chosen[e][:, t, :], start=(t == 0), stop=(t == 1))
                    m.then_inc(K.gathered[e], 1)

                def hidden(i, e, owed):
                    pe.wait_ge(K.xe_full[e], i + 1)
                    pe.wait_ge(K.h_full[e], i + 1)
                    for j in range(4):
                        for q in range(2):
                            slot = 4 * e + 2 * (j // 2) + q
                            if j % 2 == 0:
                                pe.wait_ge(s.landed[slot], i * 16 + landed0[slot])
                            w = cols8(s.slot(slot))
                            for k in range(KT):
                                m = pe.matmul(ps[:, 6 + e, q * S + j * SLOTS:q * S + (j + 1) * SLOTS],
                                              w[:, k, (j % 2) * P:(j % 2 + 1) * P], xe[e][:, k, :], start=(k == 0), stop=(k == KT - 1))
                                if owed and j == 0 and q == 0 and k == 0:
                                    m.then_inc(s.used, owed)
                            if j % 2 == 1 and (j, q) != (3, 1):
                                m.then_inc(s.used, 1)
                    m.then_inc(K.hid_full[e], 1)

                def scatter(count, owed):
                    pe.wait_ge(K.weights, count)
                    pe.wait_ge(K.y_full, count)
                    for t in range(TT):
                        for half in range(2):
                            m = pe.matmul(ps[:, 2 * t + half, :], back[:, t * P:(t + 1) * P], y[:, half * 512:(half + 1) * 512],
                                          start=False, stop=False)
                            if owed and t == 0 and half == 0:
                                m.then_inc(s.used, owed)
                    m.then_inc(K.scattered, 1)

                def down(i, e):
                    pe.wait_ge(K.h_full[e], i + 2)
                    for half in range(2):
                        if e == 0:
                            pe.wait_ge(K.xe_full[half], i + 2)
                        for kk in range(4):
                            slot = 8 + 2 * e + kk // 2
                            if half == 0 and kk % 2 == 0:
                                pe.wait_ge(s.landed[slot], i * 16 + landed0[slot])
                            m = pe.matmul(ps[64 * e:64 * e + 64, 4 + half, :], h[e][:, kk, :],
                                          rows2(s.slot(slot))[:, kk % 2, half * 512:(half + 1) * 512], start=(kk == 0), stop=(kk == 3))
                            if half == 1 and kk % 2 == 1:
                                m.then_inc(s.used, 1)

                open_accumulators(pe)
                for e in range(2):
                    gather(e, 1)
                with pe.Fori(0, TURNS) as i:
                    hidden(i, 0, 0)
                    scatter(i + 1, 1)
                    gather(0, i + 2)
                    hidden(i, 1, 0)
                    pe.wait_ge(K.chosen[1], i + 2)
                    for k in range(KT):
                        for t in range(TT):
                            m = pe.matmul(ps[:, 5, k * SLOTS:(k + 1) * SLOTS], c.x[:, t, k * P:(k + 1) * P],
                                          chosen[1][:, t, :], start=(t == 0), stop=(t == 1))
                            if k == 0 and t == 0:
                                m.then_inc(s.used, 1)
                    m.then_inc(K.gathered[1], 1)
                    down(i, 0)
                    down(i, 1)
                scatter(TURNS + 1, 0)
                close_accumulators(pe)

            def dense():
                open_accumulators(pe)
                with pe.Fori(0, TURNS) as i:
                    for n in range(BODY):
                        for j in range(2):
                            m_ = 2 * n + j
                            bank = 4 + m_ % 4
                            pe.wait_ge(DN.h_full, i * 2 * BODY + m_ + 1)
                            for q in range(2):
                                slot = 4 * (n // 2) + 2 * (n % 2) + q
                                if j == 0:
                                    pe.wait_ge(s.landed[slot], i * 16 + landed0[slot])
                                w = cols8(s.slot(slot))
                                for k in range(KT):
                                    m = pe.matmul(ps[:, bank, q * S:(q + 1) * S], w[:, k, j * P:(j + 1) * P],
                                                  c.xT[:, k, :], start=(k == 0), stop=(k == KT - 1))
                                    if n > 0 and j == 0 and q == 0 and k == 0:
                                        m.then_inc(s.used, 1)
                                if q == 0 and j == 1:
                                    m.then_inc(s.used, 1)
                            m.then_inc(DN.hid_full, 1)
                    for n in range(BODY):
                        slot = 8 + n
                        pe.wait_ge(s.landed[slot], i * 16 + landed0[slot])
                        w = rows2(s.slot(slot))
                        for kk in range(2):
                            pe.wait_ge(DN.h_full, i * 2 * BODY + 4 + 2 * n + kk + 1)
                            for t in range(TT):
                                for half in range(2):
                                    m = pe.matmul(ps[:, 2 * t + half, :], hid[n][:, kk, t * P:(t + 1) * P],
                                                  w[:, kk, half * 512:(half + 1) * 512], start=False, stop=False)
                                    if n == 0 and kk == 0 and t == 0 and half == 0:
                                        m.then_inc(s.used, 1)
                        m.then_inc(s.used, 1)
                close_accumulators(pe)
            branch(pe, packed, dense)

        @block.scalar
        def _(act):
            load_norm(act)

            def spread_loads(parts, sem):
                for dst, src in parts:
                    act.dma_start(dst, src).then_inc(sem, 16)

            def packed():
                def halves(dst, dram):
                    for e in range(2):
                        v = dram[l].rearrange("(i e) n -> e i n", e=2)[e]
                        yield (dst[64 * e:64 * e + 64, :].rearrange("p (i n) -> p i n", i=TURNS), v.partition_broadcast(64))
                spread_loads(list(halves(slots_sp, c.slots_dram)) + list(halves(gates_sp, c.gates_dram)), c.spread_landed.sem)

                def tokens_out(e, count):
                    act.wait_ge(K.gathered[e], count)
                    act.activation(xe[e], ps[:, 4 + e, :].rearrange("p (k n) -> p k n", k=KT), ACT.Copy).then_inc(K.xe_full[e], 1)

                def silu(i, e):
                    act.wait_ge(K.hid_full[e], i + 1)
                    act.wait_ge(K.h_full[e], i + 1)
                    act.activation(sgp[e], ps[:, 6 + e, 0:S], ACT.Silu).then_inc(K.sg_full[e], 1)

                for e in range(2):
                    tokens_out(e, 1)
                with act.Fori(0, TURNS) as i:
                    for e in range(2):
                        silu(i, e)
                        tokens_out(e, i + 2)
                    act.wait_ge(s.used, i * RING + (p0 + RING))
                    act.activation(y, ps[:, 4:6, :].rearrange("p b n -> p (b n)"), ACT.Copy).then_inc(K.y_full, 1)

            def dense():
                spread_loads([(gates_all[:, q * 8 * S:(q + 1) * 8 * S],
                               c.gates_dram[l, 8 * q:8 * q + 8, :].rearrange("e n -> (e n)").partition_broadcast(P)) for q in range(4)],
                             c.spread_landed.sem)
                with act.Fori(0, TURNS) as i:
                    for m in range(2 * BODY):
                        act.wait_ge(DN.hid_full, i * 2 * BODY + m + 1)
                        act.wait_ge(DN.h_full, i * 2 * BODY + m + 3)
                        act.activation(sg[m % 2], ps[:, 4 + m % 4, 0:S], ACT.Silu).then_inc(DN.sg_full, 1)
            branch(act, packed, dense)

        @block.vector
        def _(dve):
            def packed():
                def choose(e, expert):
                    sl = slots[:, :, bass.ds(expert, 1)]
                    return dve.tensor_tensor(chosen[e], bass.AP(iota.tensor, iota.offset, [iota.ap[0], [0, 2], [1, SLOTS]]),
                                             bass.AP(sl.tensor, sl.offset, [sl.ap[0], sl.ap[1], [0, SLOTS]]), ALU.is_equal)
                dve.memset(back, 0.0).then_inc(K.weights, 1)
                dve.memset(y, 0.0).then_inc(K.y_full, 1)
                for e in range(2):
                    dve.memset(h[e], 0.0).then_inc(K.h_full[e], 1)
                    choose(e, e).then_inc(K.chosen[e], 1)
                dve.wait_ge(c.spread_landed.sem, 64 * (l + 1))
                with dve.Fori(0, TURNS) as i:
                    for e in range(2):
                        dve.wait_ge(K.gathered[e], i + 1)
                        choose(e, i * 2 + 2 + e).then_inc(K.chosen[e], 1)
                    for e in range(2):
                        dve.wait_ge(s.used, i * RING + p0)
                        dve.wait_ge(K.sg_full[e], i + 1)
                        dve.tensor_tensor(h[e].rearrange("p j n -> p (j n)"), ps[:, 6 + e, S:2 * S], sgp[e], ALU.mult).then_inc(K.h_full[e], 1)
                        if e == 0:
                            dve.wait_ge(K.scattered, i + 1)
                            dve.scalar_tensor_tensor(back, slots_sp[:, bass.ds(i * S, S)], iota[:, SLOTS:SLOTS + 1],
                                                     gates_sp[:, bass.ds(i * S, S)], ALU.is_equal, ALU.mult).then_inc(K.weights, 1)

            def dense():
                dve.memset(sg[0], 0.0).then_inc(DN.h_full, 4)
                dve.wait_ge(c.spread_landed.sem, 64 * (l + 1))
                with dve.Fori(0, TURNS) as i:
                    for n in range(BODY):
                        for j in range(2):
                            m = 2 * n + j
                            dve.wait_ge(s.used, i * RING + p0)
                            dve.wait_ge(DN.sg_full, i * 2 * BODY + m + 1)
                            dve.tensor_tensor(upg[m % 2], ps[:, 4 + m % 4, S:2 * S], gates_all[:, bass.ds((i * 2 + n // 2) * S, S)],
                                              ALU.mult).then_inc(DN.up_gated, 1)
                            dve.wait_ge(DN.up_gated, i * 2 * BODY + m + 1)
                            dve.tensor_tensor(hid[n][:, j, :], upg[m % 2], sg[m % 2], ALU.mult).then_inc(DN.h_full, 1)
            branch(dve, packed, dense)
    c.next_stage()


class DilatedPlan:
    def __init__(self, c):
        s, a = c.stream, c.a
        w = a["attn_w_qkv_2"][0]
        self.qkv = [s.add(col_piece(w, CHUNK * i)) for i in range(18)]
        self.proj_end = len(s.loads)
        self.out = [s.add(row_piece(a["attn_w_o_2"][0], r * 2 * P)) for r in range(2)]
        self.end = len(s.loads)


def dilated_mixer(c, plan, load_norm):
    nc, s, ps, a = c.nc, c.stream, c.ps, c.a
    c.taken = 0
    c.etaken = 0
    qk = c.take(24 * S).rearrange("p (i n) -> p i n", i=24)
    raw = c.take(24 * 2 * HD).rearrange("p (u s d) -> p u s d", u=24, s=2)
    nm = c.take(48).rearrange("p (u s) -> p u s", s=2)
    lsum = c.take(48).rearrange("p (u s) -> p u s", s=2)
    cosT = c.take(S)
    sinT = c.take(S)
    rot = [c.take(512) for _ in range(1)][0]
    base_taken = c.taken
    v = c.etake(3 * 2 * 512).rearrange("p (g t n) -> p g t n", g=3, t=2)
    masks = c.etake(3 * 384).rearrange("p (g n) -> p g n", g=3)
    rotm = c.etake(P)
    pos_i = c.etake(S).bitcast(I32)
    ang = c.etake(S)
    red = c.etake(S)
    turns = c.etake(S)
    perm = c.etake(P)
    TWO_PI = 2 * np.pi
    C1 = 6.28125
    C2 = float(np.float32(TWO_PI - C1))
    C3 = float(TWO_PI - C1 - C2)
    MAGIC = 12582912.0

    def qk_group(g, part, i):
        pos = plan.qkv[g * 6 + part * 2 + i]
        t0 = g * 8 + part * 4 + 2 * i
        return feature_tiles(c, pos, lambda k, j: cols8(s.slot(pos))[:, k, j * P:(j + 1) * P], qk[:, t0:t0 + 2, :], "act", 1)

    def v_group(g, i):
        pos = plan.qkv[g * 6 + 4 + i]
        w = cols8(s.slot(pos))
        return Group(lambda bank: [[(bank[:, t * S:(t + 1) * S], c.xT[:, k, t * P:(t + 1) * P], w[:, k, :])
                                    for k in range(KT)] for t in range(TT)],
                     copier(v[:, g, :, i * CHUNK:(i + 1) * CHUNK], lambda bank: bank.rearrange("p (t n) -> p t n", t=2)),
                     "act", (pos,), 1)
    groups = []
    for g in range(3):
        groups += [qk_group(g, part, i) for part in range(2) for i in range(2)] + [v_group(g, i) for i in range(2)]

    with nc.Block() as block:
        @block.sync
        def _(sp):
            for dst, src in ((masks, a["c_dilated"]), (rotm, a["c_rot"]), (pos_i, a["positions_2"][0].partition_broadcast(P))):
                sp.dma_start(dst, src).then_inc(c.small.sem, 16)
            s.issue(sp, plan.proj_end + AHEAD)

        @block.tensor
        def _(pe):
            _, owed = run_projections(c, groups, pe=pe)
            settle(c, pe, owed)

        @block.scalar
        def _(act):
            run_projections(c, groups, act=act)
            act.wait_ge(c.aux_dve.sem, c.aux_dve.at(2))
            act.activation(sinT, sinT, ACT.Sin)
            act.activation(cosT, cosT, ACT.Sin)

        @block.vector
        def _(dve):
            ch = c.dve_chain
            dve.wait_ge(c.small.sem, c.small.at(48))
            ch.link(dve, dve.tensor_copy(ang, pos_i))
            ch.link(dve, dve.tensor_scalar(ang, ang, c.tiny[:, 1:2], None, ALU.mult))
            for out, shift in ((sinT, 0.0), (cosT, 0.25)):
                ch.link(dve, dve.tensor_scalar(turns, ang, 1.0 / TWO_PI, shift, ALU.mult, ALU.add))
                ch.link(dve, dve.tensor_scalar(turns, turns, MAGIC, None, ALU.add))
                ch.link(dve, dve.tensor_scalar(turns, turns, MAGIC, None, ALU.subtract))
                ch.link(dve, dve.scalar_tensor_tensor(red, turns, -C1, ang, ALU.mult, ALU.add))
                ch.link(dve, dve.scalar_tensor_tensor(red, turns, -C2, red, ALU.mult, ALU.add))
                ch.link(dve, dve.scalar_tensor_tensor(red, turns, -C3, red, ALU.mult, ALU.add))
                ch.link(dve, dve.tensor_scalar(red, red, shift * TWO_PI, 3.1415925, ALU.add, ALU.min))
                dve.tensor_scalar(out, red, -3.1415925, None, ALU.max).then_inc(c.aux_dve.sem, c.aux_dve.one())
    c.small.issued += 48
    c.next_stage()

    with nc.Block() as block:
        @block.tensor
        def _(pe):
            for i in range(24):
                if i >= 4:
                    pe.wait_ge(c.by_dve.sem, c.by_dve.at(i - 3))
                pe.matmul(ps[:, 4 + i % 4, 0:S], rotm, qk[:, i, :], start=True, stop=True).then_inc(c.aux_pe.sem, c.aux_pe.one())

        @block.vector
        def _(dve):
            ch = c.dve_chain
            for i in range(24):
                dve.wait_ge(c.aux_pe.sem, c.aux_pe.at(i + 1))
                ins = dve.tensor_tensor(rot[:, (i % 2) * S:(i % 2 + 1) * S], ps[:, 4 + i % 4, 0:S], sinT, ALU.mult)
                ins.then_inc(c.by_dve.sem, c.by_dve.one())
                ch.link(dve, dve.tensor_tensor(qk[:, i, :], qk[:, i, :], cosT, ALU.mult))
                dve.tensor_tensor(qk[:, i, :], qk[:, i, :], rot[:, (i % 2) * S:(i % 2 + 1) * S], ALU.add)
    c.next_stage()

    units = []
    for g in range(3):
        for h in range(8):
            i, lo = h // 2, 64 * (h % 2)
            q = (lambda t, g=g, i=i, lo=lo: qk[lo:lo + 64, g * 8 + i, t * P:(t + 1) * P])
            units.append(Unit(q, qk[lo:lo + 64, g * 8 + 4 + i, :], S, window(c.E[:, :], 3072 + g * 384, [[P, 2], [1, S]]),
                              [v[:, g, t, h * HD:(h + 1) * HD] for t in range(TT)]))
    c.taken = base_taken
    attention_stage(c, units, raw, nm, lsum)
    c.taken = base_taken

    w = c.take(48).rearrange("p (g n) -> p g n", g=3)
    top = c.take(16)
    den = c.take(16)
    rows = c.take(1024).rearrange("p (s n) -> p s n", s=2)
    outT = c.take(4 * S).rearrange("p (f n) -> p f n", f=4)
    nmv = nm.rearrange("p (g u) s -> p g (u s)", g=3)
    lv = lsum.rearrange("p (g u) s -> p g (u s)", g=3)
    tensor, scalar = transpose_mix(c, rows, outT, 4)
    with nc.Block() as block:
        @block.sync
        def _(sp):
            s.issue(sp, plan.end + AHEAD)

        @block.vector
        def _(dve):
            ch = c.dve_chain

            def do(ins):
                ch.link(dve, ins)
            do(dve.tensor_tensor(top, nmv[:, 0, :], nmv[:, 1, :], ALU.min))
            do(dve.tensor_tensor(top, top, nmv[:, 2, :], ALU.min))
            for g in range(3):
                ins = dve.tensor_tensor(w[:, g, :], top, nmv[:, g, :], ALU.subtract)
            ins.then_inc(c.aux_dve.sem, c.aux_dve.one())
            dve.wait_ge(c.aux_act.sem, c.aux_act.at(1))
            do(dve.tensor_tensor(lv, lv, w, ALU.mult))
            do(dve.tensor_tensor(den, lv[:, 0, :], lv[:, 1, :], ALU.add))
            do(dve.tensor_tensor(den, den, lv[:, 2, :], ALU.add))
            do(dve.reciprocal(den, den))
            for g in range(3):
                ins = dve.tensor_tensor(w[:, g, :], w[:, g, :], den, ALU.mult)
            do(ins)
            hr = rows.rearrange("p s (h d) -> p h s d", h=8)
            for g in range(3):
                rg = raw[:, 8 * g:8 * g + 8, :, :]
                ins = dve.tensor_tensor(hr if g == 0 else rg, rg, spread(w[:, g, :].rearrange("p (u s) -> p u s", s=2), HD), ALU.mult)
            do(ins)
            do(dve.tensor_tensor(raw[:, 8:16, :, :], raw[:, 8:16, :, :], raw[:, 16:24, :, :], ALU.add))
            dve.tensor_tensor(hr, hr, raw[:, 8:16, :, :], ALU.add).then_inc(c.mix.sem, c.mix.one())

        @block.scalar
        def _(act):
            load_norm(act)
            act.wait_ge(c.aux_dve.sem, c.aux_dve.at(1))
            act.activation(w, w, ACT.Exp).then_inc(c.aux_act.sem, c.aux_act.one())
            scalar(act)

        @block.tensor
        def _(pe):
            pe.wait_ge(c.mix.sem, c.mix.at(1))
            tensor(pe)
            pe.wait_ge(c.mixT.sem, c.mixT.at(2))
            for r in range(2):
                s.ready(pe, plan.out[r])
                wo = rows2(s.slot(plan.out[r]))
                for kk in range(2):
                    k = 2 * r + kk
                    for t in range(TT):
                        for half in range(2):
                            m = pe.matmul(ps[:, 2 * t + half, :], outT[:, k, t * P:(t + 1) * P],
                                          wo[:, kk, half * 512:(half + 1) * 512], start=(k == 0), stop=(k == 3))
                m.then_inc(s.used, 1)
    c.next_stage()


def ffn_plan(c, w1, w2):
    def source(q, i):
        c0 = (i * BODY + q // 3) * CHUNK
        if q % 3 == 2:
            return rows2, w2[bass.ds(c0, CHUNK), :].rearrange("(k p) n -> p k n", p=P)
        return cols8, w1[:, bass.ds(c0 + D_FF * (q % 3), CHUNK)].rearrange("(k p) n -> p k n", p=P)
    return Mlp(c, D_FF // CHUNK, source)


def build(nc, a, out, until=None):
    with ExitStack() as ctx:
        c = Core(nc, ctx, a, out)
        plans = []
        for l in range(DEPTH):
            plans.append((ffn_plan(c, a["ffn1_w1"][l], a["ffn1_w2"][l]), MixPlan(c, l),
                          ffn_plan(c, a["ffn2_w1"][l], a["ffn2_w2"][l])))
        ssd, moe0 = SsdPlan(c), MoePlan(c, 0)
        dil, moe1 = DilatedPlan(c), MoePlan(c, 1)

        setup_stage(c)
        for l, (ffn1, mix, ffn2) in enumerate(plans):
            c.taken = 0
            mlp_stage(c, ffn1, norm_loader(c, a["ln1_g"][l], a["ln1_b"][l]))
            norm_stage(c, 0.5)
            if until == ("ffn1", l):
                return c
            token_mix(c, mix, l, norm_loader(c, a["ln2_g"][l], a["ln2_b"][l]))
            norm_stage(c, 1.0)
            if until == ("mix", l):
                return c
            c.taken = 0
            mlp_stage(c, ffn2, norm_loader(c, a["ln3_g"][l], a["ln3_b"][l]))
            norm_stage(c, 0.5)
        if until == "first":
            return c
        ssd_mixer(c, ssd, norm_loader(c, a["ln_g_2"][0, 0], a["ln_b_2"][0, 0]))
        norm_stage(c, 1.0)
        if until == "ssd":
            return c
        slots, iota = router_stage(c, moe0, 0)
        experts_stage(c, moe0.mlp, 0, norm_loader(c, a["ln_g_2"][0, 1], a["ln_b_2"][0, 1]), slots, iota)
        norm_stage(c, 1.0)
        if until == "moe0":
            return c
        dilated_mixer(c, dil, norm_loader(c, a["ln_g_2"][1, 0], a["ln_b_2"][1, 0]))
        norm_stage(c, 1.0)
        if until == "dil":
            return c
        slots, iota = router_stage(c, moe1, 1)
        experts_stage(c, moe1.mlp, 1, norm_loader(c, a["ln_g_2"][1, 1], a["ln_b_2"][1, 1]), slots, iota)
        norm_stage(c, 1.0, last=True)
        return c


def t5_bucket(dist):
    n = np.maximum(dist, 0)
    ratio = np.log(np.maximum(n, 1).astype(np.float32) / np.float32(16)) / np.float32(np.log(128 / 16))
    large = 16 + (ratio * 16).astype(np.int32)
    return np.where(n < 16, n, np.minimum(large, 31))


def constants():
    f = np.float32
    k = {}
    k["c_ident"] = np.eye(P, dtype=f)
    k["c_flip"] = np.eye(P, dtype=f)[::-1].copy()
    dist = 255 - np.arange(512)
    onehot = np.zeros((32, 512), f)
    onehot[t5_bucket(dist), np.arange(512)] = 1
    k["c_onehot"] = onehot * (dist >= 0)
    bmask = np.zeros((16, 512), f)
    bmask[:, dist < 0] = NEG
    bmask[8:, dist >= 128] = NEG
    k["c_bmask"] = bmask
    tok = np.arange(S)
    k["c_tri"] = (tok[:, None] <= tok[None]).astype(f).reshape(TT, P, S).transpose(1, 0, 2).copy()
    d = 128 + np.arange(P)[:, None] - np.arange(384)[None]
    k["c_causal"] = np.where(d >= 0, 0, NEG).astype(f)
    k["c_dilated"] = np.stack([np.where((d >= 0) & (d % r == 0) & (d <= 128 * r), 0, NEG) for r in (1, 4, 16)], 1).astype(f)
    rot = np.zeros((P, P), f)
    for b in (0, 64):
        for j in range(8):
            rot[b + j + 8, b + j] = -1
            rot[b + j, b + j + 8] = 1
    k["c_rot"] = rot
    inv = (f(500000.0) ** (-np.arange(0, 16, 2, dtype=f) / f(16))).astype(f)
    p = np.arange(P) % 64
    k["c_cols"] = np.stack([(np.arange(P) >= 31).astype(f), np.where(p < 16, inv[p % 8], 0).astype(f)], 1)
    k["c_iota"] = np.concatenate([np.tile(np.arange(SLOTS, dtype=f), (P, 1)), (np.arange(P) % SLOTS)[:, None].astype(f)], 1)
    first = np.concatenate([8 - np.arange(4), 64 - np.arange(32)]).astype(f)
    k["c_first"] = np.tile(first, (P, 1))
    return k


_DIRECT = ["x", "rel_bias", "ln1_g", "ln1_b", "ffn1_w1", "ffn1_w2", "w_in", "cmp_k_w1", "cmp_k_w2", "cmp_v_w1",
           "cmp_v_w2", "swa_sinks", "fox_b_f", "w_br_a", "w_br_b", "w_br_c", "w_gate", "w_out", "ln2_g", "ln2_b",
           "ffn2_w1", "ffn2_w2", "ln3_g", "ln3_b", "positions_2", "ssd_w_in_2", "ssd_dt_bias_2", "ssd_a_log_2",
           "ssd_w_out_2", "attn_w_qkv_2", "attn_w_o_2", "ln_g_2", "ln_b_2", "moe_w_router_group_2",
           "moe_b_router_group_2", "moe_w_router_expert_2", "moe_b_router_expert_2", "moe_w_gate_2",
           "moe_w_up_2", "moe_w_down_2"]


def lay_out(inputs):
    arrays = {n: np.ascontiguousarray(inputs[n]) for n in _DIRECT}
    pe = [np.asarray(inputs[n]).reshape(DEPTH, 16, P).transpose(0, 2, 1) for n in ("cmp_pe_k", "cmp_pe_v")]
    arrays["c_pe"] = np.ascontiguousarray(np.concatenate(pe, 2))
    arrays["c_bgate"] = np.ascontiguousarray(np.asarray(inputs["b_gate"]).reshape(DEPTH, 24, P).transpose(0, 2, 1))
    cw = np.asarray(inputs["ssd_conv_w_2"])[0].reshape(4, 24, P).transpose(2, 1, 0).reshape(P, 96)
    cbias = np.asarray(inputs["ssd_conv_b_2"])[0].reshape(24, P).T
    nw = np.asarray(inputs["ssd_norm_w_2"])[0].reshape(16, P).T
    dsk = np.repeat(np.asarray(inputs["ssd_d_2"])[0], HD).reshape(16, P).T
    arrays["c_ssd"] = np.ascontiguousarray(np.concatenate([cw, cbias, nw, dsk], 1))
    arrays.update(constants())
    return arrays


def kernel(**inputs):
    import concourse.bacc as bacc
    from concourse.bass_utils import run_bass_kernel_spmd

    nc = bacc.Bacc("TRN2", target_bir_lowering=False, num_devices=1)
    arrays = lay_out(inputs)
    a = {n: nc.dram_tensor(f"in_{n}", v.shape, mybir.dt.from_np(v.dtype), kind="ExternalInput").ap() for n, v in arrays.items()}
    out = nc.dram_tensor("out_x", (1, S, D), F32, kind="ExternalOutput").ap()
    build(nc, a, out)
    r = run_bass_kernel_spmd(nc, [{f"in_{n}": v for n, v in arrays.items()}], core_ids=[0])
    return r.results[0]["out_x"]
```

```python
from contextlib import ExitStack

import numpy as np

import concourse.bass as bass
from concourse import mybir

F32 = mybir.dt.float32
F32R = mybir.dt.float32r
I32 = mybir.dt.int32
ALU = mybir.AluOpType
ACT = mybir.ActivationFunctionType
AX = mybir.AxisListType.X

P = 128
D = 1024
S = 256
KT = D // P
TT = S // P
DEPTH = 2
HD = 64
SCALE = HD ** -0.5
NEG = -1e30
D_FF = 2816
CHUNK = 256
EXPERTS = 32
HIDDEN = 512
ALPHA = (2 * DEPTH) ** 0.25
LN_EPS = 1e-5
NC_CMP = 15
RING = 12
SLOT = 2048
AHEAD = RING - 2
BODY = 4
UNITS = 4
UNIT = SLOT // 2
ARENA = 14440
CLOCK_START, CLOCK_UNIT, CLOCK_SHORT = 4096, 384, 512
NORMS = 10
SSD_T = 16
XBC_T = 24
N_UNITS = 40
SLOTS = 64


class Signal:

    def __init__(self, sem, credit=0):
        self.sem = sem
        self.base = credit
        self.issued = credit

    def one(self):
        self.issued += 1
        return 1

    def at(self, n):
        return self.base + n


class Chain:

    def __init__(self, sem):
        self.sem = sem
        self.n = 0

    def link(self, eng, ins):
        self.n += 1
        ins.then_inc(self.sem, 1)
        eng.wait_ge(self.sem, self.n)


class WeightStream:

    def __init__(self, ring, landed, used):
        self.ring = ring
        self.landed = landed
        self.used = used
        self.loads = [None] * RING
        self.value = [0] * RING
        self.total = [0] * RING
        self.issued = RING

    def slot(self, pos):
        return self.ring[:, pos % RING, :]

    def add(self, *loads):
        pos = len(self.loads)
        self.total[pos % RING] += 16 * len(loads)
        self.loads.append(loads)
        self.value.append(self.total[pos % RING])
        return pos

    def align(self):
        n = -len(self.loads) % RING
        self.loads += [None] * n
        self.value += [0] * n
        return n

    def issue(self, sp, upto):
        for pos in range(self.issued, min(upto, len(self.loads))):
            if self.loads[pos] is None:
                continue
            sp.wait_ge(self.used, pos - RING + 1)
            for into, src in self.loads[pos]:
                sp.dma_start(into(self.slot(pos)), src).then_inc(self.landed[pos % RING], 16)
        self.issued = max(self.issued, upto)

    def ready(self, pe, pos):
        pe.wait_ge(self.landed[pos % RING], self.value[pos])


def cols8(ap):
    return ap.rearrange("p (k n) -> p k n", k=8)


def rows4(ap):
    return ap.rearrange("p (k n) -> p k n", k=4)


def rows2(ap):
    return ap.rearrange("p (k n) -> p k n", k=2)


def col_piece(w, c0, n=CHUNK):
    return (lambda s: cols8(s)[:, :, 0:n]), w[:, c0:c0 + n].rearrange("(k p) n -> p k n", p=P)


def row_piece(w, r0):
    return rows2, w[r0:r0 + 2 * P, :].rearrange("(k p) n -> p k n", p=P)


class DenseCounts:

    def __init__(self, c, l):
        self.hid_full = c.counted(f"dense_hidden_products_full_{l}").sem
        self.sg_full = c.counted(f"dense_silu_full_{l}").sem
        self.up_gated = c.counted(f"dense_up_gated_{l}").sem
        self.h_full = c.counted(f"dense_hidden_full_{l}").sem


class PackedCounts:

    def __init__(self, c, l):
        def sem(name):
            return c.counted(f"packed_{name}_{l}").sem
        self.chosen = sem("tokens_chosen")
        self.gathered = sem("tokens_gathered")
        self.xe_full = sem("tokens_ready")
        self.hid_full = sem("hidden_products_full")
        self.sg_full = sem("silu_full")
        self.h_full = sem("hidden_full")
        self.hT_ps = sem("hidden_transposed_in_psum")
        self.hT_full = sem("hidden_transposed")
        self.y0_ps = sem("first_half_outputs_in_psum")
        self.y_full = [sem("first_half_outputs_ready"), sem("second_half_outputs_ready")]
        self.weights = sem("scatter_weights_ready")
        self.scattered = sem("scattered")


class Core:

    def __init__(self, nc, ctx, a, out):
        self.nc = nc
        self.a = a
        self.out = out
        self.counts = []
        self.ctx = ctx

        def sb(name, shape):
            return ctx.enter_context(nc.sbuf_tensor(name, shape, F32))

        self.ring = sb("ring", [P, RING, SLOT])
        self.x = sb("x_rows", [P, TT, D])
        self.xT = sb("xT", [P, KT, S])
        self.norm = sb("norm_params", [P, 2, D])
        self.E = sb("bias_tiles", [P, 17 * 384])
        self.ident = sb("ident", [P, P])
        self.ones = sb("ones", [P, P])
        self.zeros = sb("zeros", [P, 512])
        self.tri = sb("tri", [P, TT, S])
        self.tiny = sb("tiny", [P, 64])
        self.normT = sb("norm_params_transposed", [P, NORMS * 2 * KT])
        self.norms_done = 0
        self.taken = 0
        self.etaken = 0
        self.ps = ctx.enter_context(nc.psum_tensor("ps", [P, 8, 512], F32))
        self.scratch = nc.dram_tensor("bias_scratch", [16, 512], F32, kind="Internal").ap()
        self.slots_dram = nc.dram_tensor("slots_scratch", [DEPTH, EXPERTS, S], F32, kind="Internal").ap()
        self.over = ctx.enter_context(nc.sbuf_tensor("slots_overrun", [1, 1], I32))
        self.lent = 0
        self.open_arena()
        ctx.callback(self.close_arena)
        self.gates_dram = nc.dram_tensor("gates_scratch", [DEPTH, EXPERTS, S], F32, kind="Internal").ap()

        self.small = self.counted("small_loads_landed")
        self.setup_dve = self.counted("setup_vector_done")
        self.setup_pe = self.counted("setup_tensor_done")
        self.bias_landed = self.counted("bias_tiles_landed")
        self.norm_loaded = self.counted("norm_params_landed")
        self.hid_full = self.counted("hidden_products_full")
        self.sg_full = self.counted("silu_full")
        self.h_full = self.counted("hidden_full", credit=4)
        self.stat = self.counted("variance_ready")
        self.std = self.counted("std_ready")
        self.rstd = self.counted("norm_scales_ready")
        self.rows = self.counted("rows_scaled")
        self.rows_pending = 0
        self.x_hi = self.counted("x_upper_parts_ready")
        self.x_split = self.counted("x_parts_ready")
        self.w_hi = self.counted("weight_upper_part_ready")
        self.w_split = self.counted("weight_parts_ready")
        self.units_done = self.counted("weight_unit_products_done", credit=UNITS)
        self.h_hi = self.counted("hidden_upper_part_ready")
        self.x_new = self.counted("x_rows_ready")
        self.xT_ps = self.counted("xT_in_psum")
        self.xT_done = self.counted("xT_ready")
        self.proj_full = self.counted("projection_full")
        self.by_act = self.counted("evacuated_by_scalar")
        self.by_dve = self.counted("evacuated_by_vector")
        self.sc_full = self.counted("scores_full")
        self.s_ready = self.counted("logits_ready")
        self.nm_ready = self.counted("negative_max_ready")
        self.p_ready = self.counted("probs_ready")
        self.pt_ps = self.counted("probsT_in_psum")
        self.pt_ready = self.counted("probsT_ready")
        self.o_ps = self.counted("head_output_in_psum")
        self.o_raw = self.counted("head_output_kept")
        self.mix = self.counted("mixer_rows_ready")
        self.mixT_ps = self.counted("mixer_transposed_in_psum")
        self.mixT = self.counted("mixerT_ready")
        self.gate_act = self.counted("branch_gate_ready")
        self.merged = self.counted("merged_ready")
        self.aux_pe = self.counted("aux_tensor_steps")
        self.aux_act = self.counted("aux_scalar_steps")
        self.aux_dve = self.counted("aux_vector_steps")
        self.stored = self.counted("stores_landed")
        self.spread_landed = self.counted("spread_rows_landed")
        self.dve_chain = Chain(ctx.enter_context(nc.semaphore("vector_chain")))
        self.act_chain = Chain(ctx.enter_context(nc.semaphore("scalar_chain")))
        self.dense = [DenseCounts(self, l) for l in range(DEPTH)]
        self.packed = [PackedCounts(self, l) for l in range(DEPTH)]
        landed = [ctx.enter_context(nc.semaphore(f"weights_landed_{n}")) for n in range(RING)]
        used = ctx.enter_context(nc.semaphore("weights_used"))
        self.stream = WeightStream(self.ring, landed, used)

    def open_arena(self):
        self.arena_scope = ExitStack()
        self.arena = self.arena_scope.enter_context(self.nc.sbuf_tensor(f"arena_{self.lent}", [P, ARENA], F32))
        self.taken = 0

    def close_arena(self):
        self.arena_scope.close()
        self.lent += 1

    def counted(self, name, credit=0):
        s = Signal(self.ctx.enter_context(self.nc.semaphore(name)), credit)
        self.counts.append(s)
        return s

    def next_stage(self):
        for s in self.counts:
            s.base = s.issued

    def take(self, n):
        v = self.arena[:, self.taken:self.taken + n]
        self.taken += n
        assert self.taken <= ARENA, self.taken
        return v

    def etake(self, n):
        v = self.E[:, self.etaken:self.etaken + n]
        self.etaken += n
        assert self.etaken <= 17 * 384
        return v


def window(view, offset, dims):
    return bass.AP(view.tensor, view.offset + offset, [view.ap[0]] + dims)


def setup_stage(c):
    nc, a, ps = c.nc, c.a, c.ps
    c.taken = 0
    rb = c.take(16)
    onehot = c.take(512)
    bmask = c.take(512)
    brow = c.E[:, 0:512]
    E_v = c.E[:, :].rearrange("p (h n) -> p h n", h=17)
    s = c.stream
    with nc.Block() as block:
        @block.sync
        def _(sp):
            sp.dma_start(c.x[:, :, :], a["x"][0].rearrange("(t p) n -> p t n", p=P)).then_inc(c.small.sem, 16)
            sp.dma_start(c.ident[:, :], a["c_ident"]).then_inc(c.small.sem, 16)
            sp.dma_start(c.normT[:, :], a["c_norms"]).then_inc(c.small.sem, 16)
            sp.dma_start(rb[0:32, :], a["rel_bias"]).then_inc(c.small.sem, 16)
            sp.dma_start(onehot[0:32, :], a["c_onehot"]).then_inc(c.small.sem, 16)
            sp.dma_start(bmask[0:16, :], a["c_bmask"]).then_inc(c.small.sem, 16)
            sp.dma_start(E_v[:, 16, :], a["c_causal"]).then_inc(c.small.sem, 16)
            sp.dma_start(c.tri[:, :, :], a["c_tri"]).then_inc(c.small.sem, 16)
            sp.dma_start(c.tiny[:, 0:2], a["c_cols"]).then_inc(c.small.sem, 16)
            s.issue(sp, RING + AHEAD)

        @block.scalar
        def _(act):
            act.wait_ge(c.setup_dve.sem, 2)
            act.dma_start(c.scratch, brow[0:16, :]).then_inc(c.stored.sem, 16)

        @block.tensor
        def _(pe):
            pe.wait_ge(c.small.sem, 16 * 9)
            pe.matmul(ps[0:16, 7, :], rb[0:32, :], onehot[0:32, :], start=True, stop=True).then_inc(c.setup_pe.sem, 1)
            for t in range(TT):
                for k in range(KT):
                    m = pe.transpose(ps[:, 2 * t + k // 4, (k % 4) * P:(k % 4 + 1) * P],
                                     c.x[:, t, k * P:(k + 1) * P], c.ident[:, :])
            m.then_inc(c.setup_pe.sem, 1)

        @block.vector
        def _(dve):
            dve.memset(c.ones[:, :], 1.0)
            dve.memset(c.zeros[:, :], 0.0)
            dve.memset(c.tiny[:, 2:3], 0.0).then_inc(s.used, RING)
            dve.memset(c.tiny[:, 3:4], 0.0).then_inc(c.h_full.sem, 4)
            dve.memset(c.tiny[:, 8:9], 0.0).then_inc(c.units_done.sem, UNITS)
            dve.memset(c.tiny[:, 4:8], 0.0).then_inc(c.setup_dve.sem, 1)
            dve.wait_ge(c.setup_pe.sem, 1)
            dve.tensor_tensor(brow[0:16, :], ps[0:16, 7, :], bmask[0:16, :], ALU.add).then_inc(c.setup_dve.sem, 1)
            dve.wait_ge(c.setup_pe.sem, 2)
            for t in range(TT):
                m = dve.tensor_copy(c.xT[:, :, t * P:(t + 1) * P],
                                    ps[:, 2 * t:2 * t + 2, :].rearrange("p b (k n) -> p (b k) n", k=4))
            m.then_inc(c.setup_dve.sem, 1)

    c.small.issued += 144
    c.stored.issued += 16
    c.next_stage()


class Mlp:

    def __init__(self, c, chunks, source):
        self.chunks = chunks
        self.source = source
        self.loops = chunks // BODY
        self.tail = chunks % BODY
        self.pad = c.stream.align()
        self.pos = len(c.stream.loads)
        for n in range(3 * chunks):
            c.stream.add(source(n % RING, n // RING))


def issue_mlp(s, sp, mlp):
    p0 = mlp.pos
    s.issue(sp, p0 + RING)
    if mlp.loops > 1:
        with sp.Fori(1, mlp.loops) as i:
            for q in range(RING):
                sp.wait_ge(s.used, i * RING + (p0 + q - RING + 1))
                into, src = mlp.source(q, i)
                sp.dma_start(into(s.slot(q)), src).then_inc(s.landed[q], 16)
    s.issued = max(s.issued, p0 + RING * mlp.loops)
    s.issue(sp, p0 + 3 * mlp.chunks + AHEAD)


def load_bias_tiles(c, sp):
    E_v = c.E[:, :].rearrange("p (h n) -> p h n", h=17)
    sp.wait_ge(c.stored.sem, 16)
    sp.dma_start(E_v[:, 0:16, :], bass.AP(c.scratch.tensor, 0, [[1, P], [512, 16], [1, 384]])).then_inc(c.bias_landed.sem, 16)


def flip_bias_stage(c):
    c.taken = 0
    flip = c.take(P)
    E_v = c.E[:, :].rearrange("p (h n) -> p h n", h=17)
    N_TILES = 16
    with c.nc.Block() as block:
        @block.sync
        def _(sp):
            sp.dma_start(flip, c.a["c_flip"]).then_inc(c.small.sem, 16)

        @block.tensor
        def _(pe):
            pe.wait_ge(c.bias_landed.sem, 16)
            pe.wait_ge(c.small.sem, c.small.at(16))
            for h in range(N_TILES):
                if h >= 8:
                    sig = (c.aux_dve, c.aux_act)[h % 2]
                    pe.wait_ge(sig.sem, sig.at(h // 2 - 3))
                pe.matmul(c.ps[:, h % 8, 0:384], flip, E_v[:, h, :], start=True, stop=True).then_inc(c.aux_pe.sem, c.aux_pe.one())

        @block.vector
        def _(dve):
            for h in range(0, N_TILES, 2):
                dve.wait_ge(c.aux_pe.sem, c.aux_pe.at(h + 1))
                dve.tensor_copy(E_v[:, h, :], c.ps[:, h % 8, 0:384]).then_inc(c.aux_dve.sem, c.aux_dve.one())

        @block.scalar
        def _(act):
            for h in range(1, N_TILES, 2):
                act.wait_ge(c.aux_pe.sem, c.aux_pe.at(h + 1))
                act.activation(E_v[:, h, :], c.ps[:, h % 8, 0:384], ACT.Copy).then_inc(c.aux_act.sem, c.aux_act.one())
    c.small.issued += 16
    c.next_stage()


def mlp_stage(c, mlp, load_norm, load_first=None):
    c.close_arena()
    with ExitStack() as scope:
        def sb(name, shape, dtype=F32R):
            return scope.enter_context(c.nc.sbuf_tensor(f"{name}_{c.lent}", shape, dtype))

        w_parts = [[sb(f"weight_{part}_{b}", [P, UNIT]) for part in ("upper", "lower")] for b in range(UNITS)]
        x_parts = [sb(f"x_{part}", [P, KT, S]) for part in ("upper", "lower")]
        h_parts = [sb(f"hidden_{part}", [P, 2, S]) for part in ("upper", "lower")]
        hid = [sb(f"hidden_{b}", [P, S], F32) for b in range(2)]
        sg = [sb(f"silu_{b}", [P, S], F32) for b in range(2)]
        mlp_programs(c, mlp, load_norm, load_first, w_parts, x_parts, h_parts, hid, sg)
    c.open_arena()


PARTS = ((0, 0), (1, 0), (0, 1))


def mlp_programs(c, mlp, load_norm, load_first, w_parts, x_parts, h_parts, hid, sg):
    nc, ps, s = c.nc, c.ps, c.stream
    rows_pending = c.rows_pending
    p0 = mlp.pos
    slots0 = [s.value[p0 + q] for q in range(RING)]
    TURN = 2 * BODY

    def units(n):
        order = ((0, 0), (1, 0), (0, 1), (1, 1), (2, 0), (2, 1))
        return [(3 * n + q, half, (6 * n + u) % UNITS) for u, (q, half) in enumerate(order)]

    def source(slot, half):
        v = s.slot(slot)
        return rows2(v)[:, half, :] if slot % 3 == 2 else cols8(v)[:, :, half * P:(half + 1) * P]

    def part(b, which, slot):
        v = w_parts[b][which][:, :]
        return v if slot % 3 == 2 else cols8(v)

    def bodies(eng, emit):
        if mlp.loops:
            with eng.Fori(0, mlp.loops) as i:
                for n in range(BODY):
                    emit(i, n)
        for n in range(mlp.tail):
            emit(mlp.loops, n)

    with nc.Block() as block:
        @block.sync
        def _(sp):
            if load_first:
                load_first(c, sp)
            issue_mlp(s, sp, mlp)

        @block.tensor
        def _(pe):
            for b in range(4):
                z = pe.matmul(ps[:, b, :], c.zeros[0:1, 0:P], c.zeros[0:1, :], start=True, stop=False)
                if b == 0 and mlp.pad:
                    z.then_inc(s.used, mlp.pad)

            def chunk(i, n):
                for u, (slot, half, b) in enumerate(units(n)):
                    pe.wait_ge(c.w_split.sem, i * 6 * BODY + c.w_split.at(6 * n + u + 1))
                    w = [part(b, which, slot) for which in range(2)]
                    if u < 4:
                        m = 2 * n + half
                        if u % 2 == 0:
                            pe.wait_ge(c.h_full.sem, i * TURN + c.h_full.at(m - 3))
                        for k in range(KT):
                            for of_w, of_x in PARTS:
                                mm = pe.matmul(ps[:, 4 + m % 4, u % 2 * S:(u % 2 + 1) * S], w[of_w][:, k, :],
                                               x_parts[of_x][:, k, :], start=(k == 0 and (of_w, of_x) == PARTS[0]),
                                               stop=(k == KT - 1 and (of_w, of_x) == PARTS[-1]))
                    else:
                        pe.wait_ge(c.h_full.sem, i * TURN + c.h_full.at(2 * n + half + 1))
                        for t in range(TT):
                            for cols in range(2):
                                for of_w, of_h in PARTS:
                                    mm = pe.matmul(ps[:, 2 * t + cols, :], h_parts[of_h][:, half, t * P:(t + 1) * P],
                                                   w[of_w][:, cols * 512:(cols + 1) * 512], start=False, stop=False)
                    mm.then_inc(c.units_done.sem, 1)

            pe.wait_ge(c.x_split.sem, c.x_split.at(4))
            bodies(pe, chunk)
            for b in range(4):
                pe.matmul(ps[:, b, 0:1], c.zeros[0:1, 0:P], c.zeros[0:1, 0:1], start=False, stop=True)

        @block.gpsimd
        def _(pool):
            finish_rows(c, pool)

        @block.scalar
        def _(act):

            def chunk(i, n):
                for u, (slot, half, b) in enumerate(units(n)):
                    if half == 0:
                        act.wait_ge(s.landed[slot], i * 16 + slots0[slot])
                    act.wait_ge(c.units_done.sem, i * 6 * BODY + c.units_done.at(6 * n + u - UNITS + 1))
                    act.activation(part(b, 0, slot), source(slot, half), ACT.Copy).then_inc(c.w_hi.sem, 1)
                for j in range(2):
                    m = 2 * n + j
                    act.wait_ge(c.units_done.sem, i * 6 * BODY + c.units_done.at(6 * n + 2 * j + 2))
                    act.wait_ge(c.h_full.sem, i * TURN + c.h_full.at(m - 1))
                    act.activation(sg[m % 2][:, :], ps[:, 4 + m % 4, 0:S], ACT.Silu).then_inc(c.sg_full.sem, 1)

            for part_k in range(4):
                k = slice(2 * part_k, 2 * part_k + 2)
                act.activation(x_parts[0][:, k, :], c.xT[:, k, :], ACT.Copy).then_inc(c.x_hi.sem, 1)
            bodies(act, chunk)
            if rows_pending:
                act.wait_ge(c.rows.sem, c.rows.at(2))
            load_norm(act)

        @block.vector
        def _(dve):
            def chunk(i, n):
                for u, (slot, half, b) in enumerate(units(n)):
                    dve.wait_ge(c.w_hi.sem, i * 6 * BODY + c.w_hi.at(6 * n + u + 1))
                    dve.tensor_tensor(part(b, 1, slot), source(slot, half), part(b, 0, slot).bitcast(F32),
                                      ALU.subtract).then_inc(c.w_split.sem, 1)
                for j in range(2):
                    m = 2 * n + j
                    up = ps[:, 4 + m % 4, S:2 * S]
                    dve.wait_ge(c.sg_full.sem, i * TURN + c.sg_full.at(m + 1))
                    upper = dve.tensor_tensor(h_parts[0][:, j, :], up, sg[m % 2][:, :], ALU.mult)
                    if j == 0:
                        upper.then_inc(s.used, 3)
                    dve.tensor_tensor(hid[m % 2][:, :], up, sg[m % 2][:, :], ALU.mult).then_inc(c.h_hi.sem, 1)
                    dve.wait_ge(c.h_hi.sem, i * TURN + c.h_hi.at(m + 1))
                    dve.tensor_tensor(h_parts[1][:, j, :], hid[m % 2][:, :], h_parts[0][:, j, :].bitcast(F32),
                                      ALU.subtract).then_inc(c.h_full.sem, 1)

            for part_k in range(4):
                k = slice(2 * part_k, 2 * part_k + 2)
                dve.wait_ge(c.x_hi.sem, c.x_hi.at(part_k + 1))
                dve.tensor_tensor(x_parts[1][:, k, :], c.xT[:, k, :], x_parts[0][:, k, :].bitcast(F32),
                                  ALU.subtract).then_inc(c.x_split.sem, 1)
            bodies(dve, chunk)

    for sig in (c.sg_full, c.h_full, c.h_hi):
        sig.issued += 2 * mlp.chunks
    for sig in (c.w_hi, c.w_split, c.units_done):
        sig.issued += 6 * mlp.chunks
    c.x_hi.issued += 4
    c.x_split.issued += 4
    c.next_stage()


def norm_loader(c, gamma, beta):
    def load(act):
        act.dma_start(c.norm[:, 0, :], gamma.partition_broadcast(P)).then_inc(c.norm_loaded.sem, 16)
        act.dma_start(c.norm[:, 1, :], beta.partition_broadcast(P)).then_inc(c.norm_loaded.sem, 16)
        c.norm_loaded.issued += 32
    return load


def norm_stage(c, weight, last=False):
    nc, ps = c.nc, c.ps
    c.taken = 0
    stats = c.take(2 * 2 * 6).rearrange("p (t h n) -> p t h n", t=2, h=2)
    mv = c.take(4).rearrange("p (t n) -> p t n", t=2)
    st = c.take(8).rearrange("p (t n) -> p t n", t=2)
    gT = c.normT[:, c.norms_done * 2 * KT:(c.norms_done + 1) * 2 * KT]
    c.norms_done += 1

    def out_of_psum(t, k):
        return c.xT[:, k, t * P:(t + 1) * P], ps[:, 4 + 2 * t + k // 4, (k % 4) * P:(k % 4 + 1) * P]

    with nc.Block() as block:
        @block.sync
        def _(sp):
            if last:
                for t in range(TT):
                    sp.wait_ge(c.mix.sem, c.mix.at(t + 1))
                    sp.dma_start(c.out[0, t * P:(t + 1) * P, :], c.x[:, t, :]).then_inc(c.stored.sem, 16)
                sp.wait_ge(c.stored.sem, c.stored.at(32))

        @block.vector
        def _(dve):
            ch = c.dve_chain

            def sums(t):
                ch.link(dve, dve.scalar_tensor_tensor(c.x[:, t, :], c.x[:, t, :], ALPHA / weight,
                                                      ps[:, 2 * t:2 * t + 2, :].rearrange("p b n -> p (b n)"),
                                                      ALU.mult, ALU.add))

            def variance(t):
                for half in range(2):
                    ins = dve.bn_stats(stats[:, t, half, :], c.x[:, t, half * 512:(half + 1) * 512])
                ch.link(dve, ins)
                ch.link(dve, dve.bn_aggr(mv[:, t, :], stats[:, t, :, :].rearrange("p h n -> p (h n)")))
                dve.tensor_scalar(st[:, t, 0:1], mv[:, t, 1:2], LN_EPS / weight ** 2, None, ALU.add).then_inc(c.stat.sem, c.stat.one())

            def scales(t):
                dve.wait_ge(c.std.sem, c.std.at(t + 1))
                ch.link(dve, dve.reciprocal(st[:, t, 2:3], st[:, t, 1:2]))
                dve.scalar_tensor_tensor(st[:, t, 3:4], mv[:, t, 0:1], -1.0, st[:, t, 2:3], ALU.mult, ALU.mult
                                         ).then_inc(c.rstd.sem, c.rstd.one())

            sums(0)
            variance(0)
            sums(1)
            scales(0)
            variance(1)
            scales(1)
            for t in range(TT):
                if last:
                    dve.wait_ge(c.x_new.sem, c.x_new.at(t + 1))
                    if t == 0:
                        dve.wait_ge(c.norm_loaded.sem, c.norm_loaded.at(0))
                    ch.link(dve, dve.tensor_tensor(c.x[:, t, :], c.x[:, t, :], c.norm[:, 0, :], ALU.mult))
                    dve.tensor_tensor(c.x[:, t, :], c.x[:, t, :], c.norm[:, 1, :], ALU.add).then_inc(c.mix.sem, c.mix.one())
                else:
                    dve.wait_ge(c.xT_ps.sem, c.xT_ps.at(2 * t + 1))
                    for k in range(4):
                        dst, src = out_of_psum(t, k)
                        dve.tensor_scalar(dst, src, gT[:, k:k + 1], gT[:, KT + k:KT + k + 1], ALU.mult, ALU.add)

        @block.scalar
        def _(act):
            for t in range(TT):
                act.wait_ge(c.stat.sem, c.stat.at(t + 1))
                act.activation(st[:, t, 1:2], st[:, t, 0:1], ACT.Sqrt).then_inc(c.std.sem, c.std.one())
                act.wait_ge(c.rstd.sem, c.rstd.at(t + 1))
                act.activation(c.x[:, t, :], c.x[:, t, :], ACT.Identity, scale=st[:, t, 2:3], bias=st[:, t, 3:4]
                               ).then_inc(c.x_new.sem, c.x_new.one())
            if not last:
                for t in range(TT):
                    act.wait_ge(c.xT_ps.sem, c.xT_ps.at(2 * t + 2))
                    for k in range(4, KT):
                        dst, src = out_of_psum(t, k)
                        act.activation(dst, src, ACT.Identity, scale=gT[:, k:k + 1], bias=gT[:, KT + k:KT + k + 1])

        @block.tensor
        def _(pe):
            if not last:
                for t in range(TT):
                    pe.wait_ge(c.x_new.sem, c.x_new.at(t + 1))
                    for k in range(KT):
                        m = pe.transpose(ps[:, 4 + 2 * t + k // 4, (k % 4) * P:(k % 4 + 1) * P],
                                         c.x[:, t, k * P:(k + 1) * P], c.ident[:, :])
                        if k % 4 == 3:
                            m.then_inc(c.xT_ps.sem, c.xT_ps.one())
    if last:
        c.stored.issued += 32
    c.next_stage()
    c.rows_pending = c.norm_loaded.issued


def finish_rows(c, pool):
    if c.rows_pending:
        pool.wait_ge(c.norm_loaded.sem, c.rows_pending)
        for which, op in ((0, ALU.mult), (1, ALU.add)):
            for t in range(TT):
                ins = pool.tensor_tensor(c.x[:, t, :], c.x[:, t, :], c.norm[:, which, :], op)
            ins.then_inc(c.rows.sem, c.rows.one())
            if which == 0:
                pool.wait_ge(c.rows.sem, c.rows.at(1))
    c.rows_pending = 0


class Group:

    def __init__(self, products, copy, engine, needs=(), frees=0):
        self.products = products
        self.copy = copy
        self.engine = engine
        self.needs = needs
        self.frees = frees


def run_projections(c, groups, pe=None, act=None, dve=None, banks=(4, 5, 6, 7), owed=0):
    s = c.stream
    nb = len(banks)
    done = {"act": 0, "dve": 0}
    sigs = {"act": c.by_act, "dve": c.by_dve}
    freed = []
    for g, grp in enumerate(groups):
        bank = c.ps[:, banks[g % nb], :]
        if pe is not None:
            if g >= nb:
                eng, n = freed[g - nb]
                pe.wait_ge(sigs[eng].sem, sigs[eng].at(n))
            for pos in grp.needs:
                s.ready(pe, pos)
            for acc in grp.products(bank):
                for k, (o, lhsT, rhs) in enumerate(acc):
                    m = pe.matmul(o, lhsT, rhs, start=(k == 0), stop=(k == len(acc) - 1))
                    if owed and k == 0:
                        m.then_inc(s.used, owed)
                        owed = 0
            m.then_inc(c.proj_full.sem, c.proj_full.one())
            owed = grp.frees
        done[grp.engine] += 1
        freed.append((grp.engine, done[grp.engine]))
        if grp.engine == "act" and act is not None:
            act.wait_ge(c.proj_full.sem, c.proj_full.at(g + 1))
            grp.copy(act, bank).then_inc(c.by_act.sem, c.by_act.one())
        if grp.engine == "dve" and dve is not None:
            dve.wait_ge(c.proj_full.sem, c.proj_full.at(g + 1))
            grp.copy(dve, bank).then_inc(c.by_dve.sem, c.by_dve.one())
    return done, owed


def settle(c, pe, owed):
    if owed:
        pe.drain().then_inc(c.stream.used, owed)


def copier(dst, src):
    def copy(eng, bank):
        if eng.engine == mybir.EngineType.Activation:
            return eng.activation(dst, src(bank), ACT.Copy)
        return eng.tensor_copy(dst, src(bank))
    return copy


def feature_tiles(c, pos, cols, dst, engine, frees=0):
    def products(bank):
        return [[(bank[:, j * S:(j + 1) * S], cols(k, j), c.xT[:, k, :]) for k in range(KT)] for j in range(2)]
    return Group(products, copier(dst, lambda b: b.rearrange("p (j n) -> p j n", j=2)), engine, (pos,), frees)


def keep_clock(c, pe, columns):
    for n in range(0, columns, 512):
        w = min(512, columns - n)
        pe.matmul(c.ps[:, 7, 0:w], c.zeros[:, 0:P], c.zeros[:, 0:w], start=True, stop=True)


class Unit:

    def __init__(self, q, k, nk, bias, values, extra=None, sink=None):
        self.q = q
        self.k = k
        self.nk = nk
        self.bias = bias
        self.values = values
        self.extra = extra
        self.sink = sink


def attention_stage(c, units, raw, nm, lsum):
    nc, ps, s = c.nc, c.ps, c.stream
    n = len(units)
    norm = c.norm[:, :, :].rearrange("p k n -> p (k n)")
    sb_s = [norm[:, i * 512:(i + 1) * 512] for i in range(3)]
    sb_pT = [norm[:, 1536:1920], c.take(384)]
    mx = [c.take(2) for _ in range(2)]

    def seen_keys(u, slot):
        return units[u].nk if slot == 0 else min(units[u].nk, P)

    def lay(u, v, slot):
        nk = units[u].nk
        return v[:, slot * nk:slot * nk + seen_keys(u, slot)]

    def blocks(u):
        if units[u].nk == NC_CMP:
            return [(0, 0, 0), (1, 0, P)]
        return [(0, 0, 0), (0, P, P), (1, 0, 2 * P)]

    with nc.Block() as block:
        @block.tensor
        def _(pe):
            keep_clock(c, pe, CLOCK_START)
            for step in range(n + 3):
                u = step
                if u < n:
                    un = units[u]
                    keep_clock(c, pe, CLOCK_SHORT if un.nk == NC_CMP else CLOCK_UNIT)
                    if u >= 2:
                        pe.wait_ge(c.s_ready.sem, c.s_ready.at(u - 1))
                    for slot in range(2):
                        t = 1 - slot
                        o = lay(u, ps[:, u % 2, :], slot)
                        pairs = [(un.q(t), un.k)] + (un.extra(t) if un.extra else [])
                        for i, (lhsT, rhs) in enumerate(pairs):
                            m = pe.matmul(o, lhsT, rhs[:, 0:seen_keys(u, slot)], start=(i == 0), stop=(i == len(pairs) - 1))
                    m.then_inc(c.sc_full.sem, c.sc_full.one())
                u = step - 2
                if 0 <= u < n:
                    pe.wait_ge(c.p_ready.sem, c.p_ready.at(u + 1))
                    if u >= 2:
                        pe.wait_ge(c.pt_ready.sem, c.pt_ready.at(u - 1))
                    nk = min(units[u].nk, P)
                    for slot, k0, col in blocks(u):
                        m = pe.transpose(ps[0:nk, 2 + u % 2, col:col + P], lay(u, sb_s[u % 3], slot)[:, k0:k0 + nk], c.ident[:, :])
                    m.then_inc(c.pt_ps.sem, c.pt_ps.one())
                u = step - 3
                if 0 <= u < n:
                    pe.wait_ge(c.pt_ready.sem, c.pt_ready.at(u + 1))
                    if u >= 2:
                        pe.wait_ge(c.o_raw.sem, c.o_raw.at(u - 1))
                    nk = min(units[u].nk, P)
                    seen = [0, 0]
                    for slot, k0, col in blocks(u):
                        last = seen[slot] + 1 == sum(1 for b in blocks(u) if b[0] == slot)
                        m = pe.matmul(ps[:, 4 + u % 2, slot * HD:(slot + 1) * HD], sb_pT[u % 2][0:nk, col:col + P],
                                      units[u].values[k0 // P], start=(seen[slot] == 0), stop=last)
                        seen[slot] += 1
                    m.then_inc(c.o_ps.sem, c.o_ps.one())

        @block.vector
        def _(dve):
            ch = c.dve_chain
            for step in range(n + 4):
                u = step
                if u < n:
                    un = units[u]
                    dve.wait_ge(c.sc_full.sem, c.sc_full.at(u + 1))
                    if u >= 3:
                        dve.wait_ge(c.pt_ps.sem, c.pt_ps.at(u - 2))
                    for slot in range(2):
                        ins = dve.scalar_tensor_tensor(lay(u, sb_s[u % 3], slot), lay(u, ps[:, u % 2, :], slot), SCALE,
                                                       un.bias[:, slot, 0:seen_keys(u, slot)], ALU.mult, ALU.add)
                    ins.then_inc(c.s_ready.sem, c.s_ready.one())
                    dve.wait_ge(c.s_ready.sem, c.s_ready.at(u + 1))
                    for slot in range(2):
                        ins = dve.tensor_reduce(mx[u % 2][:, slot:slot + 1], lay(u, sb_s[u % 3], slot), AX, ALU.max)
                    ch.link(dve, ins)
                    if un.sink is not None:
                        ins = dve.tensor_scalar(nm[:, u, :], mx[u % 2], -1.0, un.sink, ALU.mult, ALU.min)
                    else:
                        ins = dve.tensor_scalar(nm[:, u, :], mx[u % 2], -1.0, None, ALU.mult)
                    ins.then_inc(c.nm_ready.sem, c.nm_ready.one())
                u = step - 4
                if 0 <= u < n:
                    dve.wait_ge(c.o_ps.sem, c.o_ps.at(u + 1))
                    dve.tensor_copy(raw[:, u, :, :], ps[:, 4 + u % 2, 0:2 * HD].rearrange("p (s d) -> p s d", s=2)
                                    ).then_inc(c.o_raw.sem, c.o_raw.one())

        @block.scalar
        def _(act):
            for step in range(n + 2):
                u = step
                if u < n:
                    act.wait_ge(c.nm_ready.sem, c.nm_ready.at(u + 1))
                    for slot in range(2):
                        sv = lay(u, sb_s[u % 3], slot)
                        ins = act.activation(sv, sv, ACT.Exp, bias=nm[:, u, slot:slot + 1],
                                             accum_out=lsum[:, u, slot:slot + 1])
                    ins.then_inc(c.p_ready.sem, c.p_ready.one())
                u = step - 2
                if 0 <= u < n:
                    act.wait_ge(c.pt_ps.sem, c.pt_ps.at(u + 1))
                    if u >= 2:
                        act.wait_ge(c.o_ps.sem, c.o_ps.at(u - 1))
                    nk = min(units[u].nk, P)
                    w = P * len(blocks(u))
                    act.activation(sb_pT[u % 2][0:nk, 0:w], ps[0:nk, 2 + u % 2, 0:w], ACT.Copy
                                   ).then_inc(c.pt_ready.sem, c.pt_ready.one())
    c.next_stage()


def transpose_mix(c, rows, outT, n):
    def tensor(pe):
        for g in range(n // 2):
            if g >= 4:
                pe.wait_ge(c.mixT.sem, c.mixT.at(g - 3))
            for f in range(2 * g, 2 * g + 2):
                for t in range(TT):
                    m = pe.transpose(c.ps[:, 4 + g % 4, (f % 2) * S + t * P:(f % 2) * S + (t + 1) * P],
                                     rows[:, 1 - t, f * P:(f + 1) * P], c.ident[:, :])
            m.then_inc(c.mixT_ps.sem, c.mixT_ps.one())

    def scalar(act):
        for g in range(n // 2):
            act.wait_ge(c.mixT_ps.sem, c.mixT_ps.at(g + 1))
            act.activation(outT[:, 2 * g:2 * g + 2, :], c.ps[:, 4 + g % 4, :].rearrange("p (f n) -> p f n", f=2),
                           ACT.Copy).then_inc(c.mixT.sem, c.mixT.one())
    return tensor, scalar


class MixPlan:

    def __init__(self, c, l):
        s, a = c.stream, c.a
        w = a["w_in"][l]

        def pair(c0, i):
            def part(g, h):
                lo, src = (2 * h + g) * HD, c0 + 256 * g + (2 * i + h) * HD
                return (lambda v: cols8(v)[:, :, lo:lo + HD]), w[:, src:src + HD].rearrange("(k p) n -> p k n", p=P)
            return s.add(*[part(g, h) for h in range(2) for g in range(2)])

        def straight(c0):
            return s.add(col_piece(w, c0))

        self.qa = [pair(0, i) for i in range(2)]
        self.cmp = straight(512)
        self.slc = straight(768)
        self.win = straight(1024)
        self.qb = [pair(1304, i) for i in range(2)]
        self.kvb = straight(1816)
        self.qc = [straight(2072 + CHUNK * i) for i in range(2)]
        self.kc = [straight(2584 + CHUNK * i) for i in range(2)]
        self.vc = [straight(3096 + CHUNK * i) for i in range(2)]
        self.gf = s.add(((lambda v: cols8(v)[:, :, 0:24]), w[:, 1280:1304].rearrange("(k p) n -> p k n", p=P)),
                        ((lambda v: cols8(v)[:, :, 24:32]), w[:, 3608:3616].rearrange("(k p) n -> p k n", p=P)))
        self.cw1 = [[s.add(col_piece(a[name][l][r * D:(r + 1) * D, :], 0)) for r in range(2)]
                    for name in ("cmp_k_w1", "cmp_v_w1")]
        self.cw2 = s.add(((lambda v: v[:, 0:P].rearrange("p (j n) -> p j n", j=2)), a["cmp_k_w2"][l].rearrange("(j p) n -> p j n", p=P)),
                         ((lambda v: v[:, P:2 * P].rearrange("p (j n) -> p j n", j=2)), a["cmp_v_w2"][l].rearrange("(j p) n -> p j n", p=P)))
        self.proj_end = len(s.loads)
        self.br = []
        self.gate = []
        for b, name in enumerate(("w_br_a", "w_br_b", "w_br_c")):
            self.br.append([s.add(row_piece(a[name][l], r * 2 * P)) for r in range(2)])
            self.gate.append([s.add(col_piece(a["w_gate"][l], b * D + CHUNK * i)) for i in range(4)])
        self.out = [s.add(row_piece(a["w_out"][l], r * 2 * P)) for r in range(4)]
        self.end = len(s.loads)


def mix_buffers(c):
    c.taken = 0
    b = {}
    b["qT"] = c.take(12 * S).rearrange("p (i n) -> p i n", i=12)
    b["kT"] = c.take(7 * S).rearrange("p (i n) -> p i n", i=7)
    b["v"] = c.take(3 * 2 * P).rearrange("p (v t n) -> p v t n", v=3, t=2)
    b["vc"] = c.take(2 * 512).rearrange("p (t n) -> p t n", t=2)
    b["z2"] = c.take(4 * P)
    b["gf"] = c.take(2 * 32).rearrange("p (t n) -> p t n", t=2)
    b["hidT"] = c.take(2 * 2 * 30).rearrange("p (v j n) -> p v j n", v=2, j=2)
    b["hrow"] = c.take(CHUNK)
    b["kcT"] = c.take(15)
    b["vcmp"] = c.take(2 * HD).rearrange("p (g n) -> p g n", g=2)
    b["pe"] = c.take(32)
    b["bf"] = c.take(8)
    b["sinks"] = c.take(8)
    b["bgate"] = c.take(24)
    b["lf"] = c.take(16).rearrange("p (t n) -> p t n", t=2)
    b["lt"] = c.take(32).rearrange("p (k t n) -> p k t n", k=2, t=2)
    b["cT"] = c.take(2 * S).rearrange("p (k n) -> p k n", k=2)
    b["G"] = c.take(48).rearrange("p (s n) -> p s n", s=2)
    b["nm"] = c.take(2 * N_UNITS).rearrange("p (u s) -> p u s", s=2)
    b["lsum"] = c.take(2 * N_UNITS).rearrange("p (u s) -> p u s", s=2)
    b["es"] = c.take(16).rearrange("p (u s) -> p u s", s=2)
    b["raw"] = c.take(N_UNITS * 2 * HD).rearrange("p (u s d) -> p u s d", u=N_UNITS, s=2)
    return b


def mix_projection_stage(c, plan, b, l):
    nc, s, a = c.nc, c.stream, c.a

    def pair_tiles(pos, i0, last):
        def cols(k, j):
            return cols8(s.slot(pos))[:, k, j * P:(j + 1) * P]
        return feature_tiles(c, pos, cols, b["qT"][:, i0:i0 + 2, :], "act", 1)

    def straight_tiles(pos, dst):
        return feature_tiles(c, pos, lambda k, j: cols8(s.slot(pos))[:, k, j * P:(j + 1) * P], dst, "act", 1)

    def kv_tile(pos, ik, iv):
        w = cols8(s.slot(pos))
        keys = Group(lambda bank: [[(bank[:, 0:S], w[:, k, 0:P], c.xT[:, k, :]) for k in range(KT)]],
                     copier(b["kT"][:, ik, :], lambda bank: bank[:, 0:S]), "dve", (pos,), 0)
        vals = Group(lambda bank: [[(bank[:, t * P:(t + 1) * P], c.xT[:, k, t * P:(t + 1) * P], w[:, k, P:2 * P])
                                    for k in range(KT)] for t in range(TT)],
                     copier(b["v"][:, iv, :, :], lambda bank: bank[:, 0:S].rearrange("p (t n) -> p t n", t=2)), "dve", (), 1)
        return [keys, vals]

    def compress_input():
        w = cols8(s.slot(plan.cmp))
        return Group(lambda bank: [[(bank[64 * par:64 * par + 64, q * P:(q + 1) * P], w[:, k, q * HD:(q + 1) * HD],
                                     c.xT[:, k, par:S:2]) for k in range(KT)] for q in range(4) for par in range(2)],
                     copier(b["z2"], lambda bank: bank), "dve", (plan.cmp,), 1)

    def value_rows(pos, i):
        w = cols8(s.slot(pos))
        return Group(lambda bank: [[(bank[:, t * S:(t + 1) * S], c.xT[:, k, t * P:(t + 1) * P], w[:, k, :])
                                    for k in range(KT)] for t in range(TT)],
                     copier(b["vc"][:, :, i * CHUNK:(i + 1) * CHUNK], lambda bank: bank.rearrange("p (t n) -> p t n", t=2)),
                     "dve", (pos,), 1)

    wgf = cols8(s.slot(plan.gf))
    gf = Group(lambda bank: [[(bank[:, t * 32:(t + 1) * 32], c.xT[:, k, t * P:(t + 1) * P], wgf[:, k, 0:32])
                              for k in range(KT)] for t in range(TT)],
               copier(b["gf"], lambda bank: bank[:, 0:64].rearrange("p (t n) -> p t n", t=2)), "dve", (plan.gf,), 1)
    groups = ([pair_tiles(plan.qa[i], 2 * i, False) for i in range(2)] + [compress_input()]
              + kv_tile(plan.slc, 0, 0) + kv_tile(plan.win, 1, 1)
              + [pair_tiles(plan.qb[i], 4 + 2 * i, False) for i in range(2)] + kv_tile(plan.kvb, 2, 2)
              + [straight_tiles(plan.qc[i], b["qT"][:, 8 + 2 * i:10 + 2 * i, :]) for i in range(2)]
              + [straight_tiles(plan.kc[i], b["kT"][:, 3 + 2 * i:5 + 2 * i, :]) for i in range(2)]
              + [value_rows(plan.vc[i], i) for i in range(2)] + [gf])

    with nc.Block() as block:
        @block.sync
        def _(sp):
            s.issue(sp, plan.cw1[0][0] + AHEAD)

        @block.gpsimd
        def _(pool):
            finish_rows(c, pool)

        @block.tensor
        def _(pe):
            _, owed = run_projections(c, groups, pe=pe)
            settle(c, pe, owed)

        @block.scalar
        def _(act):
            for dst, src in ((b["pe"], a["c_pe"][l]), (b["bf"], a["fox_b_f"][l].partition_broadcast(P)),
                             (b["sinks"], a["swa_sinks"][l].partition_broadcast(P)), (b["bgate"], a["c_bgate"][l])):
                act.dma_start(dst, src).then_inc(c.small.sem, 16)
            run_projections(c, groups, act=act)

        @block.vector
        def _(dve):
            run_projections(c, groups, dve=dve)
    c.small.issued += 64
    c.next_stage()


def mix_small_stage(c, plan, b):
    nc, s, ps = c.nc, c.stream, c.ps
    z2, hidT, hrow = b["z2"], b["hidT"], b["hrow"]
    zc = window(b["raw"], 0, [[16 * 2 * NC_CMP, 2], [2 * NC_CMP, 16], [1, 2 * NC_CMP]])
    with nc.Block() as block:
        @block.sync
        def _(sp):
            s.issue(sp, plan.proj_end + AHEAD)

        @block.tensor
        def _(pe):
            pe.wait_ge(c.aux_dve.sem, c.aux_dve.at(1))
            for m in range(16):
                for v in range(2):
                    if m % 8 == 0:
                        s.ready(pe, plan.cw1[v][m // 8])
                    mm = pe.matmul(ps[64 * v:64 * v + 2 * NC_CMP, 4 + v, 0:CHUNK], zc[:, v, m, :], cols8(s.slot(plan.cw1[v][m // 8]))[:, m % 8, :],
                                   start=(m == 0), stop=(m == 15))
            mm.then_inc(c.aux_pe.sem, c.aux_pe.one())
            pe.wait_ge(c.aux_dve.sem, c.aux_dve.at(3))
            for t in range(TT):
                mm = pe.matmul(ps[0:8, 6, 0:S], b["lf"][:, t, :], c.tri[:, t, :], start=(t == 0), stop=(t == 1))
                if t == 0:
                    mm.then_inc(s.used, 4)
            mm.then_inc(c.aux_pe.sem, c.aux_pe.one())
            pe.wait_ge(c.aux_act.sem, c.aux_act.at(2))
            for v in range(2):
                r = slice(64 * v, 64 * v + 2 * NC_CMP)
                for j in range(2):
                    mm = pe.transpose(ps[:, 4 + v, j * 32:j * 32 + 2 * NC_CMP], hrow[r, j * P:(j + 1) * P], c.ident[r, r])
            mm.then_inc(c.aux_pe.sem, c.aux_pe.one())
            s.ready(pe, plan.cw2)
            w2 = s.slot(plan.cw2).rearrange("p (v j n) -> p v j n", v=16, j=2)
            pe.wait_ge(c.aux_act.sem, c.aux_act.at(3))
            for g in range(2):
                for j in range(2):
                    pe.matmul(ps[64 * g:64 * g + 64, 7, 0:NC_CMP], w2[:, 0, j, :], hidT[:, 0, j, g * NC_CMP:(g + 1) * NC_CMP],
                              start=(j == 0), stop=(j == 1))
            for g in range(2):
                for j in range(2):
                    pe.matmul(ps[0:NC_CMP, 7, 64 + g * HD:64 + (g + 1) * HD], hidT[:, 1, j, g * NC_CMP:(g + 1) * NC_CMP],
                              w2[:, 1, j, :], start=(j == 0), stop=(j == 1))
            pe.drain().then_inc(c.aux_pe.sem, c.aux_pe.one())
            pe.drain().then_inc(s.used, 1)

        @block.scalar
        def _(act):
            ch = c.act_chain
            act.wait_ge(c.aux_dve.sem, c.aux_dve.at(2))
            ch.link(act, act.activation(b["lt"][:, 1, :, :], b["lt"][:, 1, :, :], ACT.Exp, scale=-1.0))
            act.activation(b["lt"][:, 1, :, :], b["lt"][:, 1, :, :], ACT.Ln, bias=c.ones[:, 0:1]).then_inc(c.aux_act.sem, c.aux_act.one())
            act.wait_ge(c.aux_pe.sem, c.aux_pe.at(1))
            for v in range(2):
                r = slice(64 * v, 64 * v + 2 * NC_CMP)
                ins = act.activation(hrow[r, :], ps[r, 4 + v, 0:CHUNK], ACT.Gelu_apprx_tanh)
            ins.then_inc(c.aux_act.sem, c.aux_act.one())
            act.wait_ge(c.aux_pe.sem, c.aux_pe.at(3))
            act.activation(hidT, ps[:, 4:6, 0:64].rearrange("p v (j n) -> p v j n", j=2)[:, :, :, 0:2 * NC_CMP],
                           ACT.Copy).then_inc(c.aux_act.sem, c.aux_act.one())
            for t in range(TT):
                act.activation(b["G"][:, 1 - t, :], b["gf"][:, t, 0:24], ACT.Sigmoid)

        @block.vector
        def _(dve):
            ch = c.dve_chain
            dve.wait_ge(c.small.sem, c.small.at(0))
            for v in range(2):
                ins = dve.tensor_tensor(window(b["raw"], v * 16 * 2 * NC_CMP, [[2 * NC_CMP, 16], [NC_CMP, 2], [1, NC_CMP]]),
                                        window(z2, v * 2 * P, [[1, 16], [P, 2], [8, NC_CMP]]),
                                        window(b["pe"], v * 16, [[1, 16], [0, 2], [0, NC_CMP]]), ALU.add)
            ins.then_inc(c.aux_dve.sem, c.aux_dve.one())
            for t in range(TT):
                ins = dve.tensor_tensor(b["lt"][:, 0, t, :], b["gf"][:, t, 24:32], b["bf"], ALU.add)
            ch.link(dve, ins)
            dve.scalar_tensor_tensor(b["lt"][:, 1, :, :], b["lt"][:, 0, :, :], -1.0, b["lt"][:, 0, :, :], ALU.mult, ALU.max).then_inc(c.aux_dve.sem, c.aux_dve.one())
            ch.link(dve, dve.tensor_scalar(b["sinks"], b["sinks"], -1.0, None, ALU.mult))
            dve.wait_ge(c.aux_act.sem, c.aux_act.at(1))
            dve.scalar_tensor_tensor(b["lf"], b["lt"][:, 0, :, :], 0.0, b["lt"][:, 1, :, :], ALU.min, ALU.subtract
                                     ).then_inc(c.aux_dve.sem, c.aux_dve.one())
            dve.wait_ge(c.aux_pe.sem, c.aux_pe.at(2))
            for k, sign in enumerate((1.0, -1.0)):
                dve.tensor_scalar(b["cT"][0:8, k, :], ps[0:8, 6, 0:S], sign / SCALE, None, ALU.mult)
            dve.wait_ge(c.aux_pe.sem, c.aux_pe.at(4))
            dve.tensor_copy(b["kcT"], ps[:, 7, 0:NC_CMP])
            dve.tensor_copy(b["vcmp"][0:NC_CMP, :, :], ps[0:NC_CMP, 7, 64:64 + 2 * HD].rearrange("p (g n) -> p g n", g=2))
    c.next_stage()


def mix_units(c, b):
    def bias(h):
        return window(c.E[:, :], h * 384, [[P, 2], [1, S]])

    units = []
    for branch in range(3):
        for h in range(8):
            g, i = h // 4, h % 4
            lo = 64 * g
            q = (lambda t, i=i, lo=lo: b["qT"][lo:lo + 64, i, t * P:(t + 1) * P])
            if branch < 2:
                units.append(Unit(q, b["kT"][lo:lo + 64, branch, :], S, bias(h),
                                  [b["v"][:, branch, t, g * HD:(g + 1) * HD] for t in range(TT)]))
            else:
                units.append(Unit(q, b["kcT"][lo:lo + 64, :], NC_CMP, window(c.E[:, :], h * 384 + 31, [[P, 2], [16, NC_CMP]]),
                                  [b["vcmp"][0:NC_CMP, g, :]]))
    for h in range(8):
        g, i = h // 4, h % 4
        lo = 64 * g
        q = (lambda t, i=i, lo=lo: b["qT"][lo:lo + 64, 4 + i, t * P:(t + 1) * P])
        units.append(Unit(q, b["kT"][lo:lo + 64, 2, :], S, bias(8 + h),
                          [b["v"][:, 2, t, g * HD:(g + 1) * HD] for t in range(TT)], sink=b["sinks"][:, h:h + 1]))
    for h in range(8):
        i, lo = h // 2, 64 * (h % 2)
        q = (lambda t, i=i, lo=lo: b["qT"][lo:lo + 64, 8 + i, t * P:(t + 1) * P])
        extra = (lambda t, h=h: [(b["cT"][0:8, 0, t * P:(t + 1) * P], c.ident[0:8, h:h + 1].to_broadcast([8, S])),
                                 (c.ident[0:8, h:h + 1].to_broadcast([8, P]), b["cT"][0:8, 1, :])])
        units.append(Unit(q, b["kT"][lo:lo + 64, 3 + i, :], S, bias(16),
                          [b["vc"][:, t, h * HD:(h + 1) * HD] for t in range(TT)], extra=extra))
    return units


def spread(v, n):
    return bass.AP(v.tensor, v.offset, list(v.ap) + [[0, n]])


def mix_combine_stage(c, b):
    nc = c.nc
    raw, nm, lsum, es, G = b["raw"], b["nm"], b["lsum"], b["es"], b["G"]
    rows = c.arena[:, 0:2 * 1536].rearrange("p (s n) -> p s n", s=2)
    outT_v = raw[:, 0:24, :, :].rearrange("p u s d -> p (u s d)").rearrange("p (f n) -> p f n", f=12)
    tensor, scalar = transpose_mix(c, rows, outT_v, 12)
    with nc.Block() as block:
        @block.vector
        def _(dve):
            ch = c.dve_chain
            dve.tensor_tensor(es, nm[:, 24:32, :], spread(b["sinks"], 2), ALU.subtract).then_inc(c.aux_dve.sem, c.aux_dve.one())
            dve.wait_ge(c.aux_act.sem, c.aux_act.at(1))
            ch.link(dve, dve.tensor_tensor(lsum[:, 24:32, :], lsum[:, 24:32, :], es, ALU.add))
            ch.link(dve, dve.tensor_scalar(lsum, lsum, 1e-30, None, ALU.max))
            ch.link(dve, dve.reciprocal(lsum, lsum))
            ch.link(dve, dve.tensor_scalar(lsum[:, 16:24, 1], lsum[:, 16:24, 1], c.tiny[:, 0:1], None, ALU.mult))
            for br, col in ((0, 1), (1, 2), (2, 0)):
                gv = bass.AP(G.tensor, G.offset + col, [G.ap[0], [3, 8], [24, 2]])
                ins = dve.tensor_tensor(lsum[:, 8 * br:8 * br + 8, :], lsum[:, 8 * br:8 * br + 8, :], gv, ALU.mult)
            ch.link(dve, ins)

            def head_rows(m):
                return rows[:, :, m * 512:(m + 1) * 512].rearrange("p s (h d) -> p h s d", h=8)

            def scaled(dst, u0):
                return dve.tensor_tensor(dst, raw[:, u0:u0 + 8, :, :], spread(lsum[:, u0:u0 + 8, :], HD), ALU.mult)
            scaled(head_rows(1), 24)
            scaled(head_rows(2), 32)
            scaled(head_rows(0), 0)
            scaled(raw[:, 8:16, :, :], 8)
            ch.link(dve, scaled(raw[:, 16:24, :, :], 16))
            ch.link(dve, dve.tensor_tensor(raw[:, 8:16, :, :], raw[:, 8:16, :, :], raw[:, 16:24, :, :], ALU.add))
            dve.tensor_tensor(head_rows(0), head_rows(0), raw[:, 8:16, :, :], ALU.add).then_inc(c.mix.sem, c.mix.one())

        @block.scalar
        def _(act):
            act.wait_ge(c.aux_dve.sem, c.aux_dve.at(1))
            act.activation(es, es, ACT.Exp).then_inc(c.aux_act.sem, c.aux_act.one())
            scalar(act)

        @block.tensor
        def _(pe):
            pe.wait_ge(c.mix.sem, c.mix.at(1))
            tensor(pe)
    c.next_stage()
    return outT_v


def mix_merge_stage(c, plan, b, outT, load_norm):
    nc, s, ps = c.nc, c.stream, c.ps
    mT = c.arena[:, 0:8 * S].rearrange("p (f n) -> p f n", f=8)
    sgm = [c.arena[:, (8 + i) * S:(9 + i) * S] for i in range(2)]
    tmps = [c.arena[:, (10 + i) * S:(11 + i) * S] for i in range(2)]
    with nc.Block() as block:
        @block.sync
        def _(sp):
            s.issue(sp, plan.end + AHEAD)

        @block.tensor
        def _(pe):
            for g in range(24):
                br, f = g // 8, g % 8
                bank = 4 + g % 4
                if g >= 4:
                    pe.wait_ge(c.merged.sem, c.merged.at(g - 3))
                if f == 0:
                    for pos in plan.br[br]:
                        s.ready(pe, pos)
                if f % 2 == 0:
                    s.ready(pe, plan.gate[br][f // 2])
                w = cols8(s.slot(plan.gate[br][f // 2]))
                for k in range(KT):
                    m = pe.matmul(ps[:, bank, 0:S], w[:, k, (f % 2) * P:(f % 2 + 1) * P], c.xT[:, k, :],
                                  start=(k == 0), stop=(k == KT - 1))
                    if k == 0 and f == 0 and br > 0:
                        m.then_inc(s.used, 6)
                for k in range(4):
                    w = rows2(s.slot(plan.br[br][k // 2]))
                    m = pe.matmul(ps[:, bank, S:2 * S], w[:, k % 2, f * P:(f + 1) * P], outT[:, 4 * br + k, :],
                                  start=(k == 0), stop=(k == 3))
                m.then_inc(c.proj_full.sem, c.proj_full.one())
            pe.wait_ge(c.merged.sem, c.merged.at(24))
            for r in range(4):
                s.ready(pe, plan.out[r])
                w = rows2(s.slot(plan.out[r]))
                for kk in range(2):
                    for t in range(TT):
                        for half in range(2):
                            k = 2 * r + kk
                            m = pe.matmul(ps[:, 2 * t + half, :], mT[:, k, t * P:(t + 1) * P],
                                          w[:, kk, half * 512:(half + 1) * 512], start=(k == 0), stop=(k == 7))
                            if k == 0 and t == 0 and half == 0:
                                m.then_inc(s.used, 6)
                m.then_inc(s.used, 1)

        @block.scalar
        def _(act):
            load_norm(act)
            for g in range(24):
                act.wait_ge(c.proj_full.sem, c.proj_full.at(g + 1))
                if g >= 2:
                    act.wait_ge(c.merged.sem, c.merged.at(g - 1))
                act.activation(sgm[g % 2], ps[:, 4 + g % 4, 0:S], ACT.Sigmoid, bias=b["bgate"][:, g:g + 1]
                               ).then_inc(c.gate_act.sem, c.gate_act.one())

        @block.vector
        def _(dve):
            ch = c.dve_chain
            for g in range(24):
                br, f = g // 8, g % 8
                dve.wait_ge(c.gate_act.sem, c.gate_act.at(g + 1))
                out = ps[:, 4 + g % 4, S:2 * S]
                if br == 0:
                    dve.tensor_tensor(mT[:, f, :], out, sgm[g % 2], ALU.mult).then_inc(c.merged.sem, c.merged.one())
                else:
                    tmp = tmps[g % 2]
                    dve.wait_ge(c.merged.sem, c.merged.at(g - 1))
                    ch.link(dve, dve.tensor_tensor(tmp, out, sgm[g % 2], ALU.mult))
                    dve.tensor_tensor(mT[:, f, :], mT[:, f, :], tmp, ALU.add).then_inc(c.merged.sem, c.merged.one())
    c.next_stage()


def token_mix(c, plan, l, load_norm):
    b = mix_buffers(c)
    mix_projection_stage(c, plan, b, l)
    mix_small_stage(c, plan, b)
    attention_stage(c, mix_units(c, b), b["raw"], b["nm"], b["lsum"])
    outT = mix_combine_stage(c, b)
    mix_merge_stage(c, plan, b, outT, load_norm)


class SsdPlan:
    def __init__(self, c):
        s, a = c.stream, c.a
        w = a["ssd_w_in_2"][0]
        self.z = [s.add(col_piece(w, CHUNK * i)) for i in range(8)]
        self.xbc = [s.add(col_piece(w, 2048 + CHUNK * i)) for i in range(12)]
        self.dt = s.add(col_piece(w, 5120, 32))
        self.proj_end = len(s.loads)
        self.out = [s.add(row_piece(a["ssd_w_out_2"][0], r * 2 * P)) for r in range(8)]
        self.end = len(s.loads)


def ssd_mixer(c, plan, load_norm):
    nc, s, ps, a = c.nc, c.stream, c.ps, c.a
    c.taken = 0
    c.etaken = 0
    NH, PG = 32, 4
    zT = c.take(16 * S).rearrange("p (i n) -> p i n", i=16)
    xbc = c.take(24 * S).rearrange("p (i n) -> p i n", i=24)
    conv = [c.take(S) for _ in range(2)]
    dt = c.take(64).rearrange("p (t n) -> p t n", t=2)
    da = c.take(64).rearrange("p (t n) -> p t n", t=2)
    dt1 = c.take(64).rearrange("p (t n) -> p t n", t=2)
    ncs = c.take(64).rearrange("p (t n) -> p t n", t=2)
    csT = c.take(S)
    dtb = c.take(32)
    alog = c.take(32)
    cols = c.take(6 * 24 + 32)
    diff = [c.take(384) for _ in range(2)]
    dec = [c.take(384) for _ in range(4)]
    rstd = c.take(S)
    xr = c.etake(2 * 2048).rearrange("p (t n) -> p t n", t=2)
    cb = c.etake(4 * 384).rearrange("p (g n) -> p g n", g=4)
    conv_w = cols[:, 0:96].rearrange("p (i k) -> p i k", i=24)
    conv_b = cols[:, 96:120]
    norm_w = cols[:, 120:136]
    dskip = cols[:, 136:152]

    def z_group(i):
        w = cols8(s.slot(plan.z[i]))

        def copy(eng, bank):
            return eng.activation(zT[:, 2 * i:2 * i + 2, :], bank.rearrange("p (j n) -> p j n", j=2), ACT.Silu)
        return Group(lambda bank: [[(bank[:, j * S:(j + 1) * S], w[:, k, j * P:(j + 1) * P], c.xT[:, k, :])
                                    for k in range(KT)] for j in range(2)], copy, "act", (plan.z[i],), 1)

    with nc.Block() as block:
        @block.sync
        def _(sp):
            for dst, src in ((cols[:, 0:152], a["c_ssd"]), (dtb, a["ssd_dt_bias_2"][0].partition_broadcast(P)),
                             (alog, a["ssd_a_log_2"][0].partition_broadcast(P))):
                sp.dma_start(dst, src).then_inc(c.small.sem, 16)
            s.issue(sp, plan.proj_end + AHEAD)

        @block.gpsimd
        def _(pool):
            finish_rows(c, pool)

        @block.tensor
        def _(pe):
            owed = 0
            for g in range(8 + 24):
                is_z = g < 8
                bank = 4 + g % 4
                if g >= 4:
                    if g - 4 < 8:
                        pe.wait_ge(c.by_act.sem, c.by_act.at(g - 3))
                    else:
                        pe.wait_ge(c.by_dve.sem, c.by_dve.at(g - 4 - 8 + 1))
                if is_z:
                    s.ready(pe, plan.z[g])
                    w = cols8(s.slot(plan.z[g]))
                    tiles = [(ps[:, bank, j * S:(j + 1) * S], j) for j in range(2)]
                    free = 1
                else:
                    i = g - 8
                    if i % 2 == 0:
                        s.ready(pe, plan.xbc[i // 2])
                    w = cols8(s.slot(plan.xbc[i // 2]))
                    tiles = [(ps[:, bank, 0:S], i % 2)]
                    free = i % 2
                for o, j in tiles:
                    for k in range(KT):
                        m = pe.matmul(o, w[:, k, j * P:(j + 1) * P], c.xT[:, k, :], start=(k == 0), stop=(k == KT - 1))
                        if owed and k == 0:
                            m.then_inc(s.used, owed)
                            owed = 0
                m.then_inc(c.proj_full.sem, c.proj_full.one())
                owed = free
            pe.wait_ge(c.by_dve.sem, c.by_dve.at(21))
            s.ready(pe, plan.dt)
            w = cols8(s.slot(plan.dt))
            for t in range(TT):
                for k in range(KT):
                    m = pe.matmul(ps[:, 4, t * 32:(t + 1) * 32], c.xT[:, k, t * P:(t + 1) * P], w[:, k, 0:32],
                                  start=(k == 0), stop=(k == KT - 1))
                    if owed and k == 0:
                        m.then_inc(s.used, owed)
                        owed = 0
            m.then_inc(c.proj_full.sem, c.proj_full.one())
            settle(c, pe, 1)

        @block.scalar
        def _(act):
            for g in range(8):
                act.wait_ge(c.proj_full.sem, c.proj_full.at(g + 1))
                act.activation(zT[:, 2 * g:2 * g + 2, :], ps[:, 4 + g % 4, :].rearrange("p (j n) -> p j n", j=2),
                               ACT.Silu).then_inc(c.by_act.sem, c.by_act.one())
            for i in range(24):
                act.wait_ge(c.by_dve.sem, c.by_dve.at(i + 1))
                act.activation(xbc[:, i, :], conv[i % 2], ACT.Silu).then_inc(c.aux_act.sem, c.aux_act.one())

        @block.vector
        def _(dve):
            ch = c.dve_chain
            dve.wait_ge(c.small.sem, c.small.at(48))
            for i in range(24):
                dve.wait_ge(c.proj_full.sem, c.proj_full.at(8 + i + 1))
                if i >= 2:
                    dve.wait_ge(c.aux_act.sem, c.aux_act.at(i - 1))
                u, y = ps[:, 4 + i % 4, 0:S], conv[i % 2]
                ch.link(dve, dve.tensor_scalar(y, u, conv_w[:, i, 3:4], conv_b[:, i:i + 1], ALU.mult, ALU.add))
                for k in (2, 1, 0):
                    d = 3 - k
                    ins = dve.scalar_tensor_tensor(y[:, d:S], u[:, 0:S - d], conv_w[:, i, k:k + 1], y[:, d:S], ALU.mult, ALU.add)
                    if k:
                        ch.link(dve, ins)
                ins.then_inc(c.by_dve.sem, c.by_dve.one())
            dve.wait_ge(c.proj_full.sem, c.proj_full.at(33))
            v = ps[:, 4, 0:64].rearrange("p (t n) -> p t n", t=2)
            dve.tensor_tensor(dt, v, bass.AP(dtb.tensor, dtb.offset, [dtb.ap[0], [0, 2], [1, 32]]), ALU.add)
    c.small.issued += 48
    c.next_stage()

    with nc.Block() as block:
        @block.scalar
        def _(act):
            ch = c.act_chain
            act.wait_ge(c.aux_dve.sem, c.aux_dve.at(1))
            ch.link(act, act.activation(dt1, dt1, ACT.Exp, scale=-1.0))
            act.activation(alog, alog, ACT.Exp).then_inc(c.aux_act.sem, c.aux_act.one())
            act.activation(dt1, dt1, ACT.Ln, bias=c.ones[:, 0:1]).then_inc(c.aux_act.sem, c.aux_act.one())

        @block.vector
        def _(dve):
            ch = c.dve_chain
            dve.scalar_tensor_tensor(dt1, dt, -1.0, dt, ALU.mult, ALU.max).then_inc(c.aux_dve.sem, c.aux_dve.one())
            dve.wait_ge(c.aux_act.sem, c.aux_act.at(2))
            ch.link(dve, dve.scalar_tensor_tensor(dt, dt, 0.0, dt1, ALU.max, ALU.add))
            dve.scalar_tensor_tensor(da, dt, -1.0, bass.AP(alog.tensor, alog.offset, [alog.ap[0], [0, 2], [1, 32]]),
                                     ALU.mult, ALU.mult).then_inc(c.aux_dve.sem, c.aux_dve.one())
            for q in range(8):
                t, f = q % 2, q // 2
                dve.wait_ge(c.mixT_ps.sem, c.mixT_ps.at(q + 1))
                dve.tensor_tensor(xr[:, t, f * 512:(f + 1) * 512].rearrange("p (h d) -> p h d", h=8),
                                  ps[:, q % 4, :].rearrange("p (h d) -> p h d", h=8),
                                  spread(dt[:, t, 8 * f:8 * f + 8], HD), ALU.mult).then_inc(c.mixT.sem, c.mixT.one())
            for g in range(PG):
                dve.wait_ge(c.aux_pe.sem, c.aux_pe.at(g + 1))
                dve.tensor_tensor(cb[:, g, 0:S], ps[:, 4 + g % 4, 0:S], c.tri[:, 0, :], ALU.mult)
                dve.tensor_tensor(cb[:, g, S:384], ps[:, 4 + g % 4, S:384], c.tri[:, 1, P:S], ALU.mult).then_inc(c.by_dve.sem, c.by_dve.one())
            dve.wait_ge(c.aux_pe.sem, c.aux_pe.at(5))
            for t in range(TT):
                dve.tensor_scalar(ncs[:, t, :], ps[:, 4, 64 * t:64 * t + 32], -1.0, None, ALU.mult)
            dve.tensor_copy(csT[0:32, :], ps[0:32, 5, 0:S])

        @block.tensor
        def _(pe):
            for q in range(8):
                t, f = q % 2, q // 2
                if q >= 4:
                    pe.wait_ge(c.mixT.sem, c.mixT.at(q - 3))
                for i in range(4):
                    m = pe.transpose(ps[:, q % 4, i * P:(i + 1) * P], xbc[:, 4 * f + i, t * P:(t + 1) * P], c.ident[:, :])
                m.then_inc(c.mixT_ps.sem, c.mixT_ps.one())
            for g in range(PG):
                pe.matmul(ps[:, 4 + g, 0:S], xbc[:, 16 + g, 0:P], xbc[:, 20 + g, :], start=True, stop=True)
                pe.matmul(ps[:, 4 + g, S:384], xbc[:, 16 + g, P:S], xbc[:, 20 + g, P:S], start=True, stop=True
                          ).then_inc(c.aux_pe.sem, c.aux_pe.one())
            pe.wait_ge(c.aux_dve.sem, c.aux_dve.at(2))
            pe.wait_ge(c.by_dve.sem, c.by_dve.at(2))
            for t in range(TT):
                for u in range(TT):
                    pe.matmul(ps[:, 4, 64 * t:64 * t + 32], c.tri[:, u, t * P:(t + 1) * P], da[:, u, :], start=(u == 0), stop=(u == 1))
            for u in range(TT):
                m = pe.matmul(ps[0:32, 5, 0:S], da[:, u, :], c.tri[:, u, :], start=(u == 0), stop=(u == 1))
            m.then_inc(c.aux_pe.sem, c.aux_pe.one())
    c.next_stage()

    with nc.Block() as block:
        @block.tensor
        def _(pe):
            for step in range(NH + 3):
                h = step
                if h < NH:
                    if h >= 2:
                        pe.wait_ge(c.s_ready.sem, c.s_ready.at(h - 1))
                    pe.matmul(ps[:, h % 2, 0:S], c.ident[0:32, h:h + 1].to_broadcast([32, P]), csT[0:32, :],
                              start=True, stop=True).then_inc(c.sc_full.sem, c.sc_full.one())
                h = step - 3
                if h >= 0:
                    i, lo = h // 2, 64 * (h % 2)
                    if h % 2 == 0 and i >= 2:
                        pe.wait_ge(c.o_raw.sem, c.o_raw.at(i - 1))
                    pe.wait_ge(c.p_ready.sem, c.p_ready.at(h + 1))
                    pe.matmul(ps[lo:lo + 64, 2 + i % 2, 0:S], xr[:, 0, h * HD:(h + 1) * HD], dec[h % 4][:, 0:S], start=True, stop=False)
                    pe.matmul(ps[lo:lo + 64, 2 + i % 2, P:S], xr[:, 1, h * HD:(h + 1) * HD], dec[h % 4][:, S:384],
                              start=False, stop=True).then_inc(c.o_ps.sem, c.o_ps.one())

        @block.vector
        def _(dve):
            ch = c.dve_chain
            for step in range(NH + 4):
                h = step
                if h < NH:
                    dve.wait_ge(c.sc_full.sem, c.sc_full.at(h + 1))
                    if h >= 2:
                        dve.wait_ge(c.pt_ready.sem, c.pt_ready.at(h - 1))
                    dve.tensor_scalar(diff[h % 2][:, 0:S], ps[:, h % 2, 0:S], ncs[:, 0, h:h + 1], 0.0, ALU.add, ALU.min)
                    dve.tensor_scalar(diff[h % 2][:, S:384], ps[:, h % 2, P:S], ncs[:, 1, h:h + 1], 0.0, ALU.add, ALU.min
                                      ).then_inc(c.s_ready.sem, c.s_ready.one())
                h = step - 2
                if 0 <= h < NH:
                    dve.wait_ge(c.pt_ready.sem, c.pt_ready.at(h + 1))
                    dve.tensor_tensor(dec[h % 4], dec[h % 4], cb[:, h // 8, :], ALU.mult).then_inc(c.p_ready.sem, c.p_ready.one())
                h = step - 4
                if h >= 0 and h % 2 == 1:
                    i = h // 2
                    dve.wait_ge(c.o_ps.sem, c.o_ps.at(h + 1))
                    ins = dve.scalar_tensor_tensor(xbc[:, i, :], xbc[:, i, :], dskip[:, i:i + 1], ps[:, 2 + i % 2, 0:S], ALU.mult, ALU.add)
                    ins.then_inc(c.o_raw.sem, c.o_raw.one())
                    dve.wait_ge(c.o_raw.sem, c.o_raw.at(i + 1))
                    dve.tensor_tensor(zT[:, i, :], zT[:, i, :], xbc[:, i, :], ALU.mult)

        @block.scalar
        def _(act):
            for h in range(NH):
                act.wait_ge(c.s_ready.sem, c.s_ready.at(h + 1))
                if h >= 4:
                    act.wait_ge(c.o_ps.sem, c.o_ps.at(h - 3))
                act.activation(dec[h % 4], diff[h % 2], ACT.Exp).then_inc(c.pt_ready.sem, c.pt_ready.one())
    c.next_stage()

    with nc.Block() as block:
        @block.sync
        def _(sp):
            s.issue(sp, plan.end + AHEAD)

        @block.scalar
        def _(act):
            load_norm(act)
            for i in range(16):
                act.activation(xbc[:, i, :], zT[:, i, :], ACT.Square).then_inc(c.aux_act.sem, c.aux_act.one())
            for g in range(PG):
                act.wait_ge(c.stat.sem, c.stat.at(g + 1))
                act.activation(diff[0][:, 0:S], diff[1][:, 0:S], ACT.Sqrt).then_inc(c.std.sem, c.std.one())

        @block.tensor
        def _(pe):
            for g in range(PG):
                for i in range(4):
                    pe.wait_ge(c.aux_act.sem, c.aux_act.at(4 * g + i + 1))
                    m = pe.matmul(ps[:, 4 + g, 0:S], c.ones[:, :], xbc[:, 4 * g + i, :], start=(i == 0), stop=(i == 3))
                m.then_inc(c.aux_pe.sem, c.aux_pe.one())
            for r in range(8):
                pe.wait_ge(c.mix.sem, c.mix.at(r // 2 + 1))
                s.ready(pe, plan.out[r])
                w = rows2(s.slot(plan.out[r]))
                for kk in range(2):
                    k = 2 * r + kk
                    for t in range(TT):
                        for half in range(2):
                            m = pe.matmul(ps[:, 2 * t + half, :], zT[:, k, t * P:(t + 1) * P],
                                          w[:, kk, half * 512:(half + 1) * 512], start=(k == 0), stop=(k == 15))
                m.then_inc(s.used, 1)

        @block.vector
        def _(dve):
            ch = c.dve_chain
            for g in range(PG):
                dve.wait_ge(c.aux_pe.sem, c.aux_pe.at(g + 1))
                if g:
                    dve.wait_ge(c.std.sem, c.std.at(g))
                dve.tensor_scalar(diff[1][:, 0:S], ps[:, 4 + g, 0:S], 1.0 / 512, 1e-5, ALU.mult, ALU.add).then_inc(c.stat.sem, c.stat.one())
                dve.wait_ge(c.std.sem, c.std.at(g + 1))
                ch.link(dve, dve.reciprocal(rstd, diff[0][:, 0:S]))
                for i in range(4):
                    k = 4 * g + i
                    ins = dve.scalar_tensor_tensor(zT[:, k, :], zT[:, k, :], norm_w[:, k:k + 1], rstd, ALU.mult, ALU.mult)
                ins.then_inc(c.mix.sem, c.mix.one())
    c.next_stage()


class MoePlan:
    def __init__(self, c, l):
        s, a = c.stream, c.a
        self.router = s.add(((lambda v: cols8(v)[:, :, 0:4]), a["moe_w_router_group_2"][l].rearrange("(k p) n -> p k n", p=P)),
                            ((lambda v: cols8(v)[:, :, 4:36]), a["moe_w_router_expert_2"][l].rearrange("(k p) n -> p k n", p=P)))
        self.router_end = len(s.loads)
        wg, wu, wd = a["moe_w_gate_2"][l], a["moe_w_up_2"][l], a["moe_w_down_2"][l]

        def source(q, i):
            e, half = i * 2 + q % 2, (q // 4 if q < 8 else (q - 8) // 2)
            if q < 8:
                return rows4, (wu, wg)[q % 4 // 2][bass.ds(e, 1), half * 4 * P:(half + 1) * 4 * P, :].rearrange("o (k p) n -> p (o k) n", p=P)
            return rows2, wd[bass.ds(e, 1), half * CHUNK:(half + 1) * CHUNK, :].rearrange("o (k p) n -> p (o k) n", p=P)
        self.mlp = Mlp(c, 2 * EXPERTS, source)
        self.end = len(s.loads)


def router_stage(c, plan, l):
    nc, s, ps, a = c.nc, c.stream, c.ps, c.a
    c.taken = EXPERTS * S
    slots = c.take(2 * (EXPERTS + 2)).rearrange("p (t n) -> p t n", t=2)
    iota = c.take(SLOTS + 1)
    kept = c.taken
    mask = c.take(64).rearrange("p (t n) -> p t n", t=2)
    most = c.take(4)
    sT = c.take(S)
    lg = c.take(2 * 36).rearrange("p (t n) -> p t n", t=2)
    bias = c.take(36)
    first = c.take(36)
    eg = c.take(8).rearrange("p (t n) -> p t n", t=2)
    e32 = c.take(64).rearrange("p (t n) -> p t n", t=2)
    o1 = c.take(64).rearrange("p (t n) -> p t n", t=2)
    o2 = c.take(64).rearrange("p (t n) -> p t n", t=2)
    w32 = c.take(64).rearrange("p (t n) -> p t n", t=2)
    sc = c.take(32).rearrange("p (k t) -> p k t", t=2)
    gT = c.take(S)

    def over(v, t_step, n):
        return bass.AP(v.tensor, v.offset, [v.ap[0], [t_step, 2], [0, n]])

    with nc.Block() as block:
        @block.sync
        def _(sp):
            sp.dma_start(bias[:, 0:4], a["moe_b_router_group_2"][l].partition_broadcast(P)).then_inc(c.small.sem, 16)
            sp.dma_start(bias[:, 4:36], a["moe_b_router_expert_2"][l].partition_broadcast(P)).then_inc(c.small.sem, 16)
            sp.dma_start(first, a["c_first"]).then_inc(c.small.sem, 16)
            sp.dma_start(iota, a["c_iota"]).then_inc(c.small.sem, 16)
            s.issue(sp, plan.router_end + AHEAD)
            sp.wait_ge(c.aux_dve.sem, c.aux_dve.at(7))
            sp.dma_start(c.gates_dram[l], gT[0:32, :]).then_inc(c.stored.sem, 16)
            sp.dma_start(c.slots_dram[l], sT[0:32, :]).then_inc(c.stored.sem, 16)
            sp.wait_ge(c.stored.sem, c.stored.at(32))

        @block.gpsimd
        def _(pool):
            finish_rows(c, pool)

        @block.tensor
        def _(pe):
            s.ready(pe, plan.router)
            w = cols8(s.slot(plan.router))
            for t in range(TT):
                for k in range(KT):
                    m = pe.matmul(ps[:, 4, t * 64:t * 64 + 36], c.xT[:, k, t * P:(t + 1) * P], w[:, k, 0:36],
                                  start=(k == 0), stop=(k == KT - 1))
            m.then_inc(c.aux_pe.sem, c.aux_pe.one())
            settle(c, pe, 1)
            pe.wait_ge(c.aux_dve.sem, c.aux_dve.at(2))
            for t in range(TT):
                for u in range(TT):
                    m = pe.matmul(ps[:, 6, t * 64:t * 64 + 32], c.tri[:, u, t * P:(t + 1) * P], mask[:, u, :],
                                  start=(u == 0), stop=(u == 1))
            m.then_inc(c.aux_pe.sem, c.aux_pe.one())
            pe.wait_ge(c.aux_dve.sem, c.aux_dve.at(5))
            for t in range(TT):
                pe.transpose(ps[0:32, 5, t * P:(t + 1) * P], w32[:, t, :], c.ident[:, :])
                pe.transpose(ps[0:32, 5, S + t * P:S + (t + 1) * P], slots[:, t, 0:32], c.ident[:, :])
            pe.transpose(ps[0:1, 7, 0:P], most[:, 0:1], c.ident[:, :]).then_inc(c.aux_pe.sem, c.aux_pe.one())

        @block.scalar
        def _(act):
            act.wait_ge(c.aux_dve.sem, c.aux_dve.at(1))
            act.activation(eg, eg, ACT.Exp).then_inc(c.aux_act.sem, c.aux_act.one())
            act.wait_ge(c.aux_dve.sem, c.aux_dve.at(3))
            act.activation(sc[:, 5, :], sc[:, 5, :], ACT.Exp).then_inc(c.aux_act.sem, c.aux_act.one())

        @block.vector
        def _(dve):
            ch = c.dve_chain

            def do(ins):
                ch.link(dve, ins)

            def first_of_largest(onehot, v, idx, n):
                do(dve.tensor_reduce(sc[:, 0, :], v, AX, ALU.max))
                do(dve.tensor_tensor(onehot, v, over(sc[:, 0, :], 1, n), ALU.is_equal))
                do(dve.tensor_tensor(onehot, onehot, bass.AP(idx.tensor, idx.offset, [idx.ap[0], [0, 2], [1, n]]), ALU.mult))
                do(dve.tensor_reduce(sc[:, 1, :], onehot, AX, ALU.max))
                do(dve.tensor_tensor(onehot, onehot, over(sc[:, 1, :], 1, n), ALU.is_equal))

            dve.wait_ge(c.small.sem, c.small.at(64))
            dve.wait_ge(c.aux_pe.sem, c.aux_pe.at(1))
            do(dve.tensor_tensor(lg, ps[:, 4, 0:128].rearrange("p (t n) -> p t n", t=2)[:, :, 0:36],
                                 bass.AP(bias.tensor, bias.offset, [bias.ap[0], [0, 2], [1, 36]]), ALU.add))
            og = o1[:, :, 0:4]
            first_of_largest(og, lg[:, :, 0:4], first[:, 0:4], 4)
            dve.tensor_tensor(eg, lg[:, :, 0:4], over(sc[:, 0, :], 1, 4), ALU.subtract).then_inc(c.aux_dve.sem, c.aux_dve.one())
            do(dve.tensor_scalar(og, og, 1.0, -NEG, ALU.subtract, ALU.mult))
            for t in range(TT):
                ins = dve.tensor_tensor(e32[:, t, :].rearrange("p (g n) -> p g n", g=4), lg[:, t, 4:36].rearrange("p (g n) -> p g n", g=4),
                                        spread(o1[:, t, 0:4], 8), ALU.add)
            do(ins)
            dve.wait_ge(c.aux_act.sem, c.aux_act.at(1))
            do(dve.tensor_reduce(sc[:, 2, :], eg, AX, ALU.add))
            first_of_largest(o1, e32, first[:, 4:36], 32)
            do(dve.tensor_copy(sc[:, 3, :], sc[:, 0, :]))
            do(dve.scalar_tensor_tensor(e32, o1, 3 * NEG, e32, ALU.mult, ALU.add))
            first_of_largest(o2, e32, first[:, 4:36], 32)
            dve.tensor_tensor(mask, o1, o2, ALU.add).then_inc(c.aux_dve.sem, c.aux_dve.one())
            dve.tensor_tensor(sc[:, 5, :], sc[:, 0, :], sc[:, 3, :], ALU.subtract).then_inc(c.aux_dve.sem, c.aux_dve.one())
            dve.wait_ge(c.aux_act.sem, c.aux_act.at(2))
            do(dve.scalar_tensor_tensor(sc[:, 6, :], sc[:, 5, :], 1.0, sc[:, 2, :], ALU.add, ALU.mult))
            do(dve.reciprocal(sc[:, 6, :], sc[:, 6, :]))
            do(dve.tensor_tensor(o2, o2, over(sc[:, 5, :], 1, 32), ALU.mult))
            do(dve.tensor_tensor(o1, o1, o2, ALU.add))
            dve.tensor_tensor(w32, o1, over(sc[:, 6, :], 1, 32), ALU.mult).then_inc(c.aux_dve.sem, c.aux_dve.one())
            dve.wait_ge(c.aux_pe.sem, c.aux_pe.at(2))
            dve.memset(slots[:, :, 32:34], -1.0)
            cnt = ps[:, 6, 0:P].rearrange("p (t n) -> p t n", t=2)[:, :, 0:32]
            do(dve.tensor_tensor(slots[:, :, 0:32], cnt, mask, ALU.mult))
            do(dve.tensor_scalar(slots[:, :, 0:32], slots[:, :, 0:32], 1.0, None, ALU.subtract))
            dve.tensor_reduce(most[:, 0:1], slots[:, :, 0:32], mybir.AxisListType.XY, ALU.max).then_inc(c.aux_dve.sem, c.aux_dve.one())
            dve.wait_ge(c.aux_pe.sem, c.aux_pe.at(3))
            do(dve.tensor_copy(gT[0:32, :], ps[0:32, 5, 0:S]))
            do(dve.tensor_reduce(most[0:1, 2:3], ps[0:1, 7, 0:P], AX, ALU.max))
            dve.tensor_copy(sT[0:32, :], ps[0:32, 5, S:2 * S]).then_inc(c.aux_dve.sem, c.aux_dve.one())
            dve.tensor_scalar(c.over[0:1, 0:1], most[0:1, 2:3], float(SLOTS), None, ALU.is_ge).then_inc(c.aux_dve.sem, c.aux_dve.one())
    c.small.issued += 64
    c.stored.issued += 32
    c.next_stage()
    c.taken = kept
    return slots, iota


def experts_stage(c, mlp, l, load_norm, slots, iota):
    nc, ps, s = c.nc, c.ps, c.stream
    p0 = mlp.pos
    landed0 = [s.value[p0 + q] for q in range(RING)]
    start = c.taken
    TURNS = EXPERTS // 2
    assert mlp.loops == TURNS and mlp.tail == 0
    over_max = 1

    slots_sp = c.arena[:, 0:TURNS * S]
    gates_sp = c.arena[:, TURNS * S:2 * TURNS * S]
    PAIR = 2 * SLOTS
    xe = c.take(KT * PAIR).rearrange("p (k n) -> p k n", k=KT)
    y = c.take(D)
    chosen = c.take(2 * PAIR).rearrange("p (t n) -> p t n", t=2)
    back = c.take(S)
    h = c.take(HIDDEN)
    sgp = c.take(HIDDEN)
    hT = c.take(4 * PAIR).rearrange("p (j n) -> p j n", j=4)
    c.taken = start
    gates_all = c.arena[:, 0:EXPERTS * S]
    hid = [c.take(2 * S).rearrange("p (k n) -> p k n", k=2) for _ in range(BODY)]
    sg = [c.take(S) for _ in range(2)]
    upg = [c.take(S) for _ in range(2)]
    K, DN = c.packed[l], c.dense[l]

    def branch(eng, packed, dense):
        overrun = eng.value_load(c.over[0:1, 0:1], min_val=0, max_val=over_max)
        with eng.If(overrun == 0):
            packed()
        with eng.Else():
            dense()

    def open_accumulators(pe):
        for b in range(4):
            z = pe.matmul(ps[:, b, :], c.zeros[0:1, 0:P], c.zeros[0:1, :], start=True, stop=False)
            if b == 0 and mlp.pad:
                z.then_inc(s.used, mlp.pad)

    def close_accumulators(pe):
        for b in range(4):
            z = pe.matmul(ps[:, b, 0:1], c.zeros[0:1, 0:P], c.zeros[0:1, 0:1], start=False, stop=True)
        return z

    with nc.Block() as block:
        @block.sync
        def _(sp):
            issue_mlp(s, sp, mlp)

        @block.tensor
        def _(pe):
            def packed():
                def piece(q):
                    return s.ring[:, q, :]

                def landed(q, i):
                    pe.wait_ge(s.landed[q], i * 16 + landed0[q])

                def gather(count):
                    pe.wait_ge(K.chosen, count)
                    for k in range(KT):
                        for t in range(TT):
                            m = pe.matmul(ps[:, 4 + k // 4, k % 4 * PAIR:(k % 4 + 1) * PAIR], c.x[:, t, k * P:(k + 1) * P],
                                          chosen[:, t, :], start=(t == 0), stop=(t == 1))
                    m.then_inc(K.gathered, 1)

                def hidden(i):
                    pe.wait_ge(K.xe_full, i + 1)
                    for half in range(2):
                        for w in range(2):
                            if half == 0:
                                pe.wait_ge(K.y_full[w], i + 1)
                            for k in range(4):
                                for e in range(2):
                                    q = 4 * half + 2 * w + e
                                    if k == 0:
                                        landed(q, i)
                                    m = pe.matmul(ps[e * SLOTS:(e + 1) * SLOTS, 7 - w, :], xe[:, 4 * half + k, e * SLOTS:(e + 1) * SLOTS],
                                                  rows4(piece(q))[:, k, :], start=(half == 0 and k == 0), stop=(half == 1 and k == 3))
                                    if k == 3 and q < 7:
                                        m.then_inc(s.used, 1)
                    m.then_inc(K.hid_full, 1)

                def scatter(count, owed):
                    pe.wait_ge(K.weights, count)
                    for half in range(2):
                        pe.wait_ge(K.y_full[half], count)
                        for t in range(TT):
                            m = pe.matmul(ps[:, 2 * t + half, :], back[:, t * P:(t + 1) * P], y[:, half * 512:(half + 1) * 512],
                                          start=False, stop=False)
                            if owed and t == 0 and half == 0:
                                m.then_inc(s.used, owed)
                    m.then_inc(K.scattered, 1)

                def transpose_hidden(i):
                    pe.wait_ge(K.h_full, i + 2)
                    for j in range(4):
                        m = pe.transpose(ps[:, 6, j * PAIR:(j + 1) * PAIR], h[:, j * P:(j + 1) * P], c.ident[:, :])
                    m.then_inc(K.hT_ps, 1)

                def down(i):
                    pe.wait_ge(K.hT_full, i + 1)
                    for half in range(2):
                        for kk in range(4):
                            for e in range(2):
                                q = 8 + 2 * (kk // 2) + e
                                if half == 0 and kk % 2 == 0:
                                    landed(q, i)
                                m = pe.matmul(ps[e * SLOTS:(e + 1) * SLOTS, 7 - half, :], hT[:, kk, e * SLOTS:(e + 1) * SLOTS],
                                              rows2(piece(q))[:, kk % 2, half * 512:(half + 1) * 512], start=(kk == 0), stop=(kk == 3))
                                if half == 1 and kk % 2 == 1:
                                    m.then_inc(s.used, 1)
                        if half == 0:
                            m.then_inc(K.y0_ps, 1)

                open_accumulators(pe)
                gather(1)
                with pe.Fori(0, TURNS) as i:
                    hidden(i)
                    scatter(i + 1, 1)
                    transpose_hidden(i)
                    gather(i + 2)
                    down(i)
                scatter(TURNS + 1, 0)
                close_accumulators(pe)

            def dense():
                open_accumulators(pe)
                with pe.Fori(0, TURNS) as i:
                    for n in range(BODY):
                        for j in range(2):
                            m_ = 2 * n + j
                            bank = 4 + m_ % 4
                            pe.wait_ge(DN.h_full, i * 2 * BODY + m_ + 1)
                            for q in range(2):
                                for k in range(KT):
                                    slot = 4 * (k // 4) + 2 * (1 - q) + n // 2
                                    if n % 2 == 0 and j == 0 and k % 4 == 0:
                                        pe.wait_ge(s.landed[slot], i * 16 + landed0[slot])
                                    col = (n % 2 * 2 + j) * P
                                    m = pe.matmul(ps[:, bank, q * S:(q + 1) * S], rows4(s.slot(slot))[:, k % 4, col:col + P],
                                                  c.xT[:, k, :], start=(k == 0), stop=(k == KT - 1))
                            m.then_inc(DN.hid_full, 1)
                    for n in range(BODY):
                        slot = 8 + 2 * (n % 2) + n // 2
                        pe.wait_ge(s.landed[slot], i * 16 + landed0[slot])
                        w = rows2(s.slot(slot))
                        for kk in range(2):
                            pe.wait_ge(DN.h_full, i * 2 * BODY + 4 + 2 * n + kk + 1)
                            for t in range(TT):
                                for half in range(2):
                                    m = pe.matmul(ps[:, 2 * t + half, :], hid[n][:, kk, t * P:(t + 1) * P],
                                                  w[:, kk, half * 512:(half + 1) * 512], start=False, stop=False)
                                    if n == 0 and kk == 0 and t == 0 and half == 0:
                                        m.then_inc(s.used, 8)
                        if n != 1:
                            m.then_inc(s.used, 2 if n == 2 else 1)
                close_accumulators(pe)
            branch(pe, packed, dense)

        @block.scalar
        def _(act):
            load_norm(act)

            def spread_loads(parts, sem):
                for dst, src in parts:
                    act.dma_start(dst, src).then_inc(sem, 16)

            def packed():
                def halves(dst, dram):
                    for e in range(2):
                        v = dram[l].rearrange("(i e) n -> e i n", e=2)[e]
                        yield (dst[64 * e:64 * e + 64, :].rearrange("p (i n) -> p i n", i=TURNS), v.partition_broadcast(64))
                spread_loads(list(halves(slots_sp, c.slots_dram)) + list(halves(gates_sp, c.gates_dram)), c.spread_landed.sem)

                def tokens_out(count):
                    act.wait_ge(K.gathered, count)
                    act.activation(xe, ps[:, 4:6, :].rearrange("p b (k n) -> p (b k) n", k=4), ACT.Copy).then_inc(K.xe_full, 1)

                tokens_out(1)
                with act.Fori(0, TURNS) as i:
                    act.wait_ge(K.hid_full, i + 1)
                    act.wait_ge(K.h_full, i + 1)
                    act.activation(sgp, ps[:, 6, :], ACT.Silu).then_inc(K.sg_full, 1)
                    act.wait_ge(K.hT_ps, i + 1)
                    act.activation(hT, ps[:, 6, :].rearrange("p (j n) -> p j n", j=4), ACT.Copy).then_inc(K.hT_full, 1)
                    tokens_out(i + 2)
                    act.wait_ge(s.used, i * RING + (p0 + RING))
                    act.activation(y[:, 512:D], ps[:, 6, :], ACT.Copy).then_inc(K.y_full[1], 1)

            def dense():
                spread_loads([(gates_all[:, q * 8 * S:(q + 1) * 8 * S],
                               c.gates_dram[l, 8 * q:8 * q + 8, :].rearrange("e n -> (e n)").partition_broadcast(P)) for q in range(4)],
                             c.spread_landed.sem)
                with act.Fori(0, TURNS) as i:
                    for m in range(2 * BODY):
                        act.wait_ge(DN.hid_full, i * 2 * BODY + m + 1)
                        act.wait_ge(DN.h_full, i * 2 * BODY + m + 3)
                        act.activation(sg[m % 2], ps[:, 4 + m % 4, 0:S], ACT.Silu).then_inc(DN.sg_full, 1)
            branch(act, packed, dense)

        @block.vector
        def _(dve):
            def packed():
                def choose(expert):
                    sl = slots[:, :, bass.ds(expert, 2)]
                    dve.tensor_tensor(chosen.rearrange("p t (e n) -> p t e n", e=2),
                                      bass.AP(iota.tensor, iota.offset, [iota.ap[0], [0, 2], [0, 2], [1, SLOTS]]),
                                      bass.AP(sl.tensor, sl.offset, [sl.ap[0], sl.ap[1], sl.ap[2], [0, SLOTS]]),
                                      ALU.is_equal).then_inc(K.chosen, 1)
                choose(0)
                dve.memset(back, 0.0).then_inc(K.weights, 1)
                for half in range(2):
                    dve.memset(y[:, half * 512:(half + 1) * 512], 0.0).then_inc(K.y_full[half], 1)
                dve.memset(h, 0.0).then_inc(K.h_full, 1)
                dve.wait_ge(c.spread_landed.sem, 64 * (l + 1))
                with dve.Fori(0, TURNS) as i:
                    dve.wait_ge(K.gathered, i + 1)
                    choose(i * 2 + 2)
                    dve.wait_ge(K.sg_full, i + 1)
                    dve.tensor_tensor(h, ps[:, 7, :], sgp, ALU.mult).then_inc(K.h_full, 1)
                    dve.wait_ge(K.scattered, i + 1)
                    dve.scalar_tensor_tensor(back, slots_sp[:, bass.ds(i * S, S)], iota[:, SLOTS:SLOTS + 1],
                                             gates_sp[:, bass.ds(i * S, S)], ALU.is_equal, ALU.mult).then_inc(K.weights, 1)
                    dve.wait_ge(K.y0_ps, i + 1)
                    dve.tensor_copy(y[:, 0:512], ps[:, 7, :]).then_inc(K.y_full[0], 1)

            def dense():
                dve.memset(sg[0], 0.0).then_inc(DN.h_full, 4)
                dve.wait_ge(c.spread_landed.sem, 64 * (l + 1))
                with dve.Fori(0, TURNS) as i:
                    for n in range(BODY):
                        for j in range(2):
                            m = 2 * n + j
                            dve.wait_ge(s.used, i * RING + p0)
                            dve.wait_ge(DN.sg_full, i * 2 * BODY + m + 1)
                            dve.tensor_tensor(upg[m % 2], ps[:, 4 + m % 4, S:2 * S], gates_all[:, bass.ds((i * 2 + n // 2) * S, S)],
                                              ALU.mult).then_inc(DN.up_gated, 1)
                            dve.wait_ge(DN.up_gated, i * 2 * BODY + m + 1)
                            dve.tensor_tensor(hid[n][:, j, :], upg[m % 2], sg[m % 2], ALU.mult).then_inc(DN.h_full, 1)
            branch(dve, packed, dense)
    c.next_stage()


class DilatedPlan:
    def __init__(self, c):
        s, a = c.stream, c.a
        w = a["attn_w_qkv_2"][0]
        self.qkv = [s.add(col_piece(w, CHUNK * i)) for i in range(18)]
        self.proj_end = len(s.loads)
        self.out = [s.add(row_piece(a["attn_w_o_2"][0], r * 2 * P)) for r in range(2)]
        self.end = len(s.loads)


def dilated_mixer(c, plan, load_norm):
    nc, s, ps, a = c.nc, c.stream, c.ps, c.a
    c.taken = 0
    c.etaken = 0
    qk = c.take(24 * S).rearrange("p (i n) -> p i n", i=24)
    raw = c.take(24 * 2 * HD).rearrange("p (u s d) -> p u s d", u=24, s=2)
    nm = c.take(48).rearrange("p (u s) -> p u s", s=2)
    lsum = c.take(48).rearrange("p (u s) -> p u s", s=2)
    cosT = c.take(S)
    sinT = c.take(S)
    rot = [c.take(512) for _ in range(1)][0]
    base_taken = c.taken
    v = c.etake(3 * 2 * 512).rearrange("p (g t n) -> p g t n", g=3, t=2)
    masks = c.etake(3 * 384).rearrange("p (g n) -> p g n", g=3)
    rotm = c.etake(P)
    pos_i = c.etake(S).bitcast(I32)
    ang = c.etake(S)
    red = c.etake(S)
    turns = c.etake(S)
    perm = c.etake(P)
    TWO_PI = 2 * np.pi
    C1 = 6.28125
    C2 = float(np.float32(TWO_PI - C1))
    C3 = float(TWO_PI - C1 - C2)
    MAGIC = 12582912.0

    def qk_group(g, part, i):
        pos = plan.qkv[g * 6 + part * 2 + i]
        t0 = g * 8 + part * 4 + 2 * i
        return feature_tiles(c, pos, lambda k, j: cols8(s.slot(pos))[:, k, j * P:(j + 1) * P], qk[:, t0:t0 + 2, :], "act", 1)

    def v_group(g, i):
        pos = plan.qkv[g * 6 + 4 + i]
        w = cols8(s.slot(pos))
        return Group(lambda bank: [[(bank[:, t * S:(t + 1) * S], c.xT[:, k, t * P:(t + 1) * P], w[:, k, :])
                                    for k in range(KT)] for t in range(TT)],
                     copier(v[:, g, :, i * CHUNK:(i + 1) * CHUNK], lambda bank: bank.rearrange("p (t n) -> p t n", t=2)),
                     "act", (pos,), 1)
    groups = []
    for g in range(3):
        groups += [qk_group(g, part, i) for part in range(2) for i in range(2)] + [v_group(g, i) for i in range(2)]

    with nc.Block() as block:
        @block.sync
        def _(sp):
            for dst, src in ((masks, a["c_dilated"]), (rotm, a["c_rot"]), (pos_i, a["positions_2"][0].partition_broadcast(P))):
                sp.dma_start(dst, src).then_inc(c.small.sem, 16)
            s.issue(sp, plan.proj_end + AHEAD)

        @block.gpsimd
        def _(pool):
            finish_rows(c, pool)

        @block.tensor
        def _(pe):
            _, owed = run_projections(c, groups, pe=pe)
            settle(c, pe, owed)

        @block.scalar
        def _(act):
            run_projections(c, groups, act=act)
            act.wait_ge(c.aux_dve.sem, c.aux_dve.at(2))
            act.activation(sinT, sinT, ACT.Sin)
            act.activation(cosT, cosT, ACT.Sin)

        @block.vector
        def _(dve):
            ch = c.dve_chain
            dve.wait_ge(c.small.sem, c.small.at(48))
            ch.link(dve, dve.tensor_copy(ang, pos_i))
            ch.link(dve, dve.tensor_scalar(ang, ang, c.tiny[:, 1:2], None, ALU.mult))
            for out, shift in ((sinT, 0.0), (cosT, 0.25)):
                ch.link(dve, dve.tensor_scalar(turns, ang, 1.0 / TWO_PI, shift, ALU.mult, ALU.add))
                ch.link(dve, dve.tensor_scalar(turns, turns, MAGIC, None, ALU.add))
                ch.link(dve, dve.tensor_scalar(turns, turns, MAGIC, None, ALU.subtract))
                ch.link(dve, dve.scalar_tensor_tensor(red, turns, -C1, ang, ALU.mult, ALU.add))
                ch.link(dve, dve.scalar_tensor_tensor(red, turns, -C2, red, ALU.mult, ALU.add))
                ch.link(dve, dve.scalar_tensor_tensor(red, turns, -C3, red, ALU.mult, ALU.add))
                ch.link(dve, dve.tensor_scalar(red, red, shift * TWO_PI, 3.1415925, ALU.add, ALU.min))
                dve.tensor_scalar(out, red, -3.1415925, None, ALU.max).then_inc(c.aux_dve.sem, c.aux_dve.one())
    c.small.issued += 48
    c.next_stage()

    with nc.Block() as block:
        @block.tensor
        def _(pe):
            for i in range(24):
                if i >= 4:
                    pe.wait_ge(c.by_dve.sem, c.by_dve.at(i - 3))
                pe.matmul(ps[:, 4 + i % 4, 0:S], rotm, qk[:, i, :], start=True, stop=True).then_inc(c.aux_pe.sem, c.aux_pe.one())

        @block.vector
        def _(dve):
            ch = c.dve_chain
            for i in range(24):
                dve.wait_ge(c.aux_pe.sem, c.aux_pe.at(i + 1))
                ins = dve.tensor_tensor(rot[:, (i % 2) * S:(i % 2 + 1) * S], ps[:, 4 + i % 4, 0:S], sinT, ALU.mult)
                ins.then_inc(c.by_dve.sem, c.by_dve.one())
                ch.link(dve, dve.tensor_tensor(qk[:, i, :], qk[:, i, :], cosT, ALU.mult))
                dve.tensor_tensor(qk[:, i, :], qk[:, i, :], rot[:, (i % 2) * S:(i % 2 + 1) * S], ALU.add)
    c.next_stage()

    units = []
    for g in range(3):
        for h in range(8):
            i, lo = h // 2, 64 * (h % 2)
            q = (lambda t, g=g, i=i, lo=lo: qk[lo:lo + 64, g * 8 + i, t * P:(t + 1) * P])
            units.append(Unit(q, qk[lo:lo + 64, g * 8 + 4 + i, :], S, window(c.E[:, :], 3072 + g * 384, [[P, 2], [1, S]]),
                              [v[:, g, t, h * HD:(h + 1) * HD] for t in range(TT)]))
    c.taken = base_taken
    attention_stage(c, units, raw, nm, lsum)
    c.taken = base_taken

    w = c.take(48).rearrange("p (g n) -> p g n", g=3)
    top = c.take(16)
    den = c.take(16)
    rows = c.take(1024).rearrange("p (s n) -> p s n", s=2)
    outT = c.take(4 * S).rearrange("p (f n) -> p f n", f=4)
    nmv = nm.rearrange("p (g u) s -> p g (u s)", g=3)
    lv = lsum.rearrange("p (g u) s -> p g (u s)", g=3)
    tensor, scalar = transpose_mix(c, rows, outT, 4)
    with nc.Block() as block:
        @block.sync
        def _(sp):
            s.issue(sp, plan.end + AHEAD)

        @block.vector
        def _(dve):
            ch = c.dve_chain

            def do(ins):
                ch.link(dve, ins)
            do(dve.tensor_tensor(top, nmv[:, 0, :], nmv[:, 1, :], ALU.min))
            do(dve.tensor_tensor(top, top, nmv[:, 2, :], ALU.min))
            for g in range(3):
                ins = dve.tensor_tensor(w[:, g, :], top, nmv[:, g, :], ALU.subtract)
            ins.then_inc(c.aux_dve.sem, c.aux_dve.one())
            dve.wait_ge(c.aux_act.sem, c.aux_act.at(1))
            do(dve.tensor_tensor(lv, lv, w, ALU.mult))
            do(dve.tensor_tensor(den, lv[:, 0, :], lv[:, 1, :], ALU.add))
            do(dve.tensor_tensor(den, den, lv[:, 2, :], ALU.add))
            do(dve.reciprocal(den, den))
            for g in range(3):
                ins = dve.tensor_tensor(w[:, g, :], w[:, g, :], den, ALU.mult)
            do(ins)
            hr = rows.rearrange("p s (h d) -> p h s d", h=8)
            for g in range(3):
                rg = raw[:, 8 * g:8 * g + 8, :, :]
                ins = dve.tensor_tensor(hr if g == 0 else rg, rg, spread(w[:, g, :].rearrange("p (u s) -> p u s", s=2), HD), ALU.mult)
            do(ins)
            do(dve.tensor_tensor(raw[:, 8:16, :, :], raw[:, 8:16, :, :], raw[:, 16:24, :, :], ALU.add))
            dve.tensor_tensor(hr, hr, raw[:, 8:16, :, :], ALU.add).then_inc(c.mix.sem, c.mix.one())

        @block.scalar
        def _(act):
            load_norm(act)
            act.wait_ge(c.aux_dve.sem, c.aux_dve.at(1))
            act.activation(w, w, ACT.Exp).then_inc(c.aux_act.sem, c.aux_act.one())
            scalar(act)

        @block.tensor
        def _(pe):
            pe.wait_ge(c.mix.sem, c.mix.at(1))
            tensor(pe)
            pe.wait_ge(c.mixT.sem, c.mixT.at(2))
            for r in range(2):
                s.ready(pe, plan.out[r])
                wo = rows2(s.slot(plan.out[r]))
                for kk in range(2):
                    k = 2 * r + kk
                    for t in range(TT):
                        for half in range(2):
                            m = pe.matmul(ps[:, 2 * t + half, :], outT[:, k, t * P:(t + 1) * P],
                                          wo[:, kk, half * 512:(half + 1) * 512], start=(k == 0), stop=(k == 3))
                m.then_inc(s.used, 1)
    c.next_stage()


def ffn_plan(c, w1, w2):
    def source(q, i):
        c0 = (i * BODY + q // 3) * CHUNK
        if q % 3 == 2:
            return rows2, w2[bass.ds(c0, CHUNK), :].rearrange("(k p) n -> p k n", p=P)
        return cols8, w1[:, bass.ds(c0 + D_FF * (q % 3), CHUNK)].rearrange("(k p) n -> p k n", p=P)
    return Mlp(c, D_FF // CHUNK, source)


def build(nc, a, out, until=None):
    with ExitStack() as ctx:
        c = Core(nc, ctx, a, out)
        plans = []
        for l in range(DEPTH):
            plans.append((ffn_plan(c, a["ffn1_w1"][l], a["ffn1_w2"][l]), MixPlan(c, l),
                          ffn_plan(c, a["ffn2_w1"][l], a["ffn2_w2"][l])))
        ssd, moe0 = SsdPlan(c), MoePlan(c, 0)
        dil, moe1 = DilatedPlan(c), MoePlan(c, 1)

        setup_stage(c)
        for l, (ffn1, mix, ffn2) in enumerate(plans):
            c.taken = 0
            mlp_stage(c, ffn1, norm_loader(c, a["ln1_g"][l], a["ln1_b"][l]), load_bias_tiles if l == 0 else None)
            norm_stage(c, 0.5)
            if until == ("ffn1", l):
                return c
            if l == 0:
                flip_bias_stage(c)
            token_mix(c, mix, l, norm_loader(c, a["ln2_g"][l], a["ln2_b"][l]))
            norm_stage(c, 1.0)
            if until == ("mix", l):
                return c
            c.taken = 0
            mlp_stage(c, ffn2, norm_loader(c, a["ln3_g"][l], a["ln3_b"][l]))
            norm_stage(c, 0.5)
        if until == "first":
            return c
        ssd_mixer(c, ssd, norm_loader(c, a["ln_g_2"][0, 0], a["ln_b_2"][0, 0]))
        norm_stage(c, 1.0)
        if until == "ssd":
            return c
        slots, iota = router_stage(c, moe0, 0)
        experts_stage(c, moe0.mlp, 0, norm_loader(c, a["ln_g_2"][0, 1], a["ln_b_2"][0, 1]), slots, iota)
        norm_stage(c, 1.0)
        if until == "moe0":
            return c
        dilated_mixer(c, dil, norm_loader(c, a["ln_g_2"][1, 0], a["ln_b_2"][1, 0]))
        norm_stage(c, 1.0)
        if until == "dil":
            return c
        slots, iota = router_stage(c, moe1, 1)
        experts_stage(c, moe1.mlp, 1, norm_loader(c, a["ln_g_2"][1, 1], a["ln_b_2"][1, 1]), slots, iota)
        norm_stage(c, 1.0, last=True)
        return c


def t5_bucket(dist):
    n = np.maximum(dist, 0)
    ratio = np.log(np.maximum(n, 1).astype(np.float32) / np.float32(16)) / np.float32(np.log(128 / 16))
    large = 16 + (ratio * 16).astype(np.int32)
    return np.where(n < 16, n, np.minimum(large, 31))


def constants():
    f = np.float32
    k = {}
    k["c_ident"] = np.eye(P, dtype=f)
    k["c_flip"] = np.eye(P, dtype=f)[::-1].copy()
    dist = 255 - np.arange(512)
    onehot = np.zeros((32, 512), f)
    onehot[t5_bucket(dist), np.arange(512)] = 1
    k["c_onehot"] = onehot * (dist >= 0)
    bmask = np.zeros((16, 512), f)
    bmask[:, dist < 0] = NEG
    bmask[8:, dist >= 128] = NEG
    k["c_bmask"] = bmask
    tok = np.arange(S)
    k["c_tri"] = (tok[:, None] <= tok[None]).astype(f).reshape(TT, P, S).transpose(1, 0, 2).copy()
    d = 128 + np.arange(P)[:, None] - np.arange(384)[None]
    k["c_causal"] = np.where(d >= 0, 0, NEG).astype(f)
    k["c_dilated"] = np.stack([np.where((d >= 0) & (d % r == 0) & (d <= 128 * r), 0, NEG) for r in (1, 4, 16)], 1).astype(f)
    rot = np.zeros((P, P), f)
    for b in (0, 64):
        for j in range(8):
            rot[b + j + 8, b + j] = -1
            rot[b + j, b + j + 8] = 1
    k["c_rot"] = rot
    inv = (f(500000.0) ** (-np.arange(0, 16, 2, dtype=f) / f(16))).astype(f)
    p = np.arange(P) % 64
    k["c_cols"] = np.stack([(np.arange(P) >= 31).astype(f), np.where(p < 16, inv[p % 8], 0).astype(f)], 1)
    k["c_iota"] = np.concatenate([np.tile(np.arange(SLOTS, dtype=f), (P, 1)), (np.arange(P) % SLOTS)[:, None].astype(f)], 1)
    first = np.concatenate([8 - np.arange(4), 64 - np.arange(32)]).astype(f)
    k["c_first"] = np.tile(first, (P, 1))
    return k


_DIRECT = ["x", "rel_bias", "ln1_g", "ln1_b", "ffn1_w1", "ffn1_w2", "w_in", "cmp_k_w1", "cmp_k_w2", "cmp_v_w1",
           "cmp_v_w2", "swa_sinks", "fox_b_f", "w_br_a", "w_br_b", "w_br_c", "w_gate", "w_out", "ln2_g", "ln2_b",
           "ffn2_w1", "ffn2_w2", "ln3_g", "ln3_b", "positions_2", "ssd_w_in_2", "ssd_dt_bias_2", "ssd_a_log_2",
           "ssd_w_out_2", "attn_w_qkv_2", "attn_w_o_2", "ln_g_2", "ln_b_2", "moe_w_router_group_2",
           "moe_b_router_group_2", "moe_w_router_expert_2", "moe_b_router_expert_2", "moe_w_gate_2",
           "moe_w_up_2", "moe_w_down_2"]


def lay_out(inputs):
    arrays = {n: np.ascontiguousarray(inputs[n]) for n in _DIRECT}
    pe = [np.asarray(inputs[n]).reshape(DEPTH, 16, P).transpose(0, 2, 1) for n in ("cmp_pe_k", "cmp_pe_v")]
    arrays["c_pe"] = np.ascontiguousarray(np.concatenate(pe, 2))
    rows = [inputs[n + p][l] for l in range(DEPTH) for n in ("ln1", "ln2", "ln3") for p in ("_g", "_b")]
    rows += [inputs["ln_" + p + "_2"][i, j] for i in range(DEPTH) for j in range(2) for p in ("g", "b")]
    arrays["c_norms"] = np.ascontiguousarray(np.stack([np.asarray(r) for r in rows]).reshape(2 * NORMS * KT, P).T)
    arrays["c_bgate"] = np.ascontiguousarray(np.asarray(inputs["b_gate"]).reshape(DEPTH, 24, P).transpose(0, 2, 1))
    cw = np.asarray(inputs["ssd_conv_w_2"])[0].reshape(4, 24, P).transpose(2, 1, 0).reshape(P, 96)
    cbias = np.asarray(inputs["ssd_conv_b_2"])[0].reshape(24, P).T
    nw = np.asarray(inputs["ssd_norm_w_2"])[0].reshape(16, P).T
    dsk = np.repeat(np.asarray(inputs["ssd_d_2"])[0], HD).reshape(16, P).T
    arrays["c_ssd"] = np.ascontiguousarray(np.concatenate([cw, cbias, nw, dsk], 1))
    arrays.update(constants())
    return arrays


def kernel(**inputs):
    import concourse.bacc as bacc
    from concourse.bass_utils import run_bass_kernel_spmd

    nc = bacc.Bacc("TRN2", target_bir_lowering=False, num_devices=1)
    arrays = lay_out(inputs)
    a = {n: nc.dram_tensor(f"in_{n}", v.shape, mybir.dt.from_np(v.dtype), kind="ExternalInput").ap() for n, v in arrays.items()}
    out = nc.dram_tensor("out_x", (1, S, D), F32, kind="ExternalOutput").ap()
    build(nc, a, out)
    r = run_bass_kernel_spmd(nc, [{f"in_{n}": v for n, v in arrays.items()}], core_ids=[0])
    return r.results[0]["out_x"]
```
